# Optimizing a Trainium2 kernel written in Bass

```python
import math
import jax
import jax.numpy as jnp
from jax import lax
import numpy as np

D_MODEL = 1024
BATCH = 1
SEQ = 1024
DEPTH = 1
DEC_BATCH = 8
DEC_SEQ = 4
PAST_LEN = 1024
PAGE_SIZE = 128

HEAD_DIM = 64
NSA_HEADS = 8
FOX_HEADS = 8
MIX_WIDTH = (NSA_HEADS + FOX_HEADS) * HEAD_DIM
NSA_KV_HEADS = 2
NSA_GROUP = NSA_HEADS // NSA_KV_HEADS
CMP_BLOCK = 32
CMP_STRIDE = 16
CMP_HIDDEN = 2 * HEAD_DIM
SLC_BLOCK = 64
N_SELECT = 16
WINDOW = 512
T5_BUCKETS = 32
T5_EXACT = T5_BUCKETS // 2
T5_MAX_DIST = 128
D_FF = -(-8 * D_MODEL // (3 * 256)) * 256
Q_BLOCK = 128
NORM_EPS = 1e-6
NEG_INF = -1e30
FORCE_SCORE = 1e4
FORGET_BIAS_INIT = 3.0
IN_SIZES = (NSA_HEADS * HEAD_DIM,) + (NSA_KV_HEADS * HEAD_DIM,) * 6 + (3 * NSA_HEADS,) + (FOX_HEADS * HEAD_DIM,) * 3 + (FOX_HEADS,)
IN_COLS = sum(IN_SIZES)

kernel_name = 'nsa_fox_hybrid_step'

def rms_norm(x, g):
    xf = x.astype(jnp.float32)
    y = xf * lax.rsqrt(jnp.mean(xf * xf, axis=-1, keepdims=True) + NORM_EPS)
    return (y * g.astype(jnp.float32)).astype(x.dtype)

def masked_softmax(logits, mask):
    p = jax.nn.softmax(jnp.where(mask, logits, NEG_INF), axis=-1)
    return jnp.where(mask, p, 0.0)

def t5_bucket(dist):
    n = jnp.maximum(dist, 0)
    nf = jnp.maximum(n, 1).astype(jnp.float32)
    large = T5_EXACT + (jnp.log(nf / T5_EXACT) / math.log(T5_MAX_DIST / T5_EXACT) * (T5_BUCKETS - T5_EXACT)).astype(jnp.int32)
    large = jnp.minimum(large, T5_BUCKETS - 1)
    return jnp.where(n < T5_EXACT, n, large)

def t5_bias_2d(dist, rel_bias):
    b = rel_bias[t5_bucket(dist)].astype(jnp.float32)
    b = b.reshape(dist.shape + (NSA_KV_HEADS, NSA_GROUP))
    return jnp.transpose(b, (2, 3, 0, 1))

def project(h, w_in, b_gate, b_forget):
    B, T, _ = h.shape
    z = jnp.einsum('btd,dc->btc', h, w_in)
    splits = np.cumsum(IN_SIZES)[:-1].tolist()
    q_n, k_c, v_c, k_s, v_s, k_w, v_w, g, q_f, k_f, v_f, f = jnp.split(z, splits, axis=-1)
    nsa_kv = lambda a: a.reshape(B, T, NSA_KV_HEADS, HEAD_DIM)
    fox = lambda a: a.reshape(B, T, FOX_HEADS, HEAD_DIM)
    gates = jax.nn.sigmoid(g.reshape(B, T, 3, NSA_HEADS) + b_gate)
    logf = jax.nn.log_sigmoid((f + b_forget).astype(jnp.float32))
    return (q_n.reshape(B, T, NSA_HEADS, HEAD_DIM), nsa_kv(k_c), nsa_kv(v_c), nsa_kv(k_s), nsa_kv(v_s),
            nsa_kv(k_w), nsa_kv(v_w), gates, fox(q_f), fox(k_f), fox(v_f), logf)

def compress(k, pe, w1, w2):
    B, L, G, Dh = k.shape
    n_chunks = L // CMP_STRIDE
    r = CMP_BLOCK // CMP_STRIDE
    n_cmp = n_chunks - r + 1
    c = k[:, : n_chunks * CMP_STRIDE].reshape(B, n_chunks, CMP_STRIDE, G, Dh)
    blk = jnp.concatenate([c[:, i:i + n_cmp] for i in range(r)], axis=2)
    blk = blk + pe[None, None, :, None, :]
    flat = jnp.transpose(blk, (0, 1, 3, 2, 4)).reshape(B, n_cmp, G, CMP_BLOCK * Dh)
    return jax.nn.gelu(flat @ w1) @ w2

def to_blocks(k):
    B, L, G, Dh = k.shape
    n_slc = -(-L // SLC_BLOCK)
    k = jnp.pad(k, ((0, 0), (0, n_slc * SLC_BLOCK - L), (0, 0), (0, 0)))
    return jnp.transpose(k.reshape(B, n_slc, SLC_BLOCK, G, Dh), (0, 3, 1, 2, 4))

def cmp_to_slc(n_cmp, n_slc):
    start = jnp.arange(n_cmp, dtype=jnp.int32) * CMP_STRIDE
    j0 = jnp.arange(n_slc, dtype=jnp.int32) * SLC_BLOCK
    return ((start[:, None] < j0[None, :] + SLC_BLOCK) & (start[:, None] + CMP_BLOCK > j0[None, :])).astype(jnp.float32)

def nsa_full_keys(k_c, v_c, k_s, v_s, cmp_pe, cmp_w1, cmp_w2):
    kc = compress(k_c, cmp_pe[0], cmp_w1[0], cmp_w2[0])
    vc = compress(v_c, cmp_pe[1], cmp_w1[1], cmp_w2[1])
    n_cmp = kc.shape[1]
    c_end = jnp.arange(n_cmp, dtype=jnp.int32) * CMP_STRIDE + (CMP_BLOCK - 1)
    ksb, vsb = to_blocks(k_s), to_blocks(v_s)
    ovl = cmp_to_slc(n_cmp, ksb.shape[2])
    return kc, vc, c_end, ovl, ksb, vsb

def attend_block(t_pos, q_n, gates, q_f, cq, kw, vw, w_pos, kc, vc, c_end, ovl, ksb, vsb, kf, vf, ck, rel_bias):
    B, Q = q_n.shape[:2]
    G, R = NSA_KV_HEADS, NSA_GROUP
    scale = HEAD_DIM ** -0.5
    qg = q_n.reshape(B, Q, G, R, HEAD_DIM)

    dist_c = t_pos[:, None] - c_end[None, :]
    lc = jnp.einsum('bqgrd,bcgd->bgrqc', qg, kc).astype(jnp.float32) * scale + t5_bias_2d(dist_c, rel_bias)
    pc = masked_softmax(lc, dist_c >= 0)
    o_c = jnp.einsum('bgrqc,bcgd->bqgrd', pc.astype(vc.dtype), vc)

    n_slc = ksb.shape[2]
    n_top = min(N_SELECT, n_slc)
    imp = jnp.einsum('bgrqc,cs->bgqs', pc, ovl)
    j = jnp.arange(n_slc, dtype=jnp.int32)[None, :]
    cur = (t_pos // SLC_BLOCK)[:, None]
    forced = (j == 0) | (j == cur) | (j == cur - 1)
    score = jnp.where(forced, FORCE_SCORE, imp)
    score = jnp.where(j * SLC_BLOCK > t_pos[:, None], -FORCE_SCORE, score)
    _, idx = lax.top_k(score, n_top)

    bi = jnp.arange(B)[:, None, None, None]
    gi = jnp.arange(G)[None, :, None, None]
    M = n_top * SLC_BLOCK
    ks_sel = ksb[bi, gi, idx].reshape(B, G, Q, M, HEAD_DIM)
    vs_sel = vsb[bi, gi, idx].reshape(B, G, Q, M, HEAD_DIM)
    s_pos = (idx[..., None] * SLC_BLOCK + jnp.arange(SLC_BLOCK, dtype=jnp.int32)).reshape(B, G, Q, M)
    dist_s = t_pos[None, None, :, None] - s_pos
    bias_s = jnp.moveaxis(rel_bias.reshape(T5_BUCKETS, G, R)[t5_bucket(dist_s), gi], -1, 2)
    ls = jnp.einsum('bqgrd,bgqmd->bgrqm', qg, ks_sel).astype(jnp.float32) * scale + bias_s.astype(jnp.float32)
    ps = masked_softmax(ls, (dist_s >= 0)[:, :, None])
    o_s = jnp.einsum('bgrqm,bgqmd->bqgrd', ps.astype(vs_sel.dtype), vs_sel)

    dist_w = t_pos[:, None] - w_pos[None, :]
    valid_w = (dist_w >= 0) & (dist_w < WINDOW) & (w_pos[None, :] >= 0)
    lw = jnp.einsum('bqgrd,bkgd->bgrqk', qg, kw).astype(jnp.float32) * scale + t5_bias_2d(dist_w, rel_bias)
    pw = masked_softmax(lw, valid_w)
    o_w = jnp.einsum('bgrqk,bkgd->bqgrd', pw.astype(vw.dtype), vw)

    g = gates.reshape(B, Q, 3, G, R)[..., None]
    o_n = (g[:, :, 0] * o_c + g[:, :, 1] * o_s + g[:, :, 2] * o_w).reshape(B, Q, NSA_HEADS * HEAD_DIM)

    k_pos = jnp.arange(kf.shape[1], dtype=jnp.int32)
    decay = jnp.transpose(cq, (0, 2, 1))[..., None] - jnp.transpose(ck, (0, 2, 1))[:, :, None, :]
    lf = jnp.einsum('bqhd,bkhd->bhqk', q_f, kf).astype(jnp.float32) * scale + decay
    pf = masked_softmax(lf, k_pos[None, :] <= t_pos[:, None])
    o_f = jnp.einsum('bhqk,bkhd->bqhd', pf.astype(vf.dtype), vf).reshape(B, Q, FOX_HEADS * HEAD_DIM)
    return o_n, o_f

def mixer_prompt(h, w_in, b_gate, b_forget, cmp_pe, cmp_w1, cmp_w2, rel_bias):
    B, T, _ = h.shape
    q_n, k_c, v_c, k_s, v_s, k_w, v_w, gates, q_f, k_f, v_f, logf = project(h, w_in, b_gate, b_forget)
    kc, vc, c_end, ovl, ksb, vsb = nsa_full_keys(k_c, v_c, k_s, v_s, cmp_pe, cmp_w1, cmp_w2)
    pad = ((0, 0), (WINDOW, 0), (0, 0), (0, 0))
    kw_pad, vw_pad = jnp.pad(k_w, pad), jnp.pad(v_w, pad)
    ck = jnp.cumsum(logf, axis=1)
    q_blk = min(Q_BLOCK, T)

    def one_block(i):
        q0 = i * q_blk
        t_pos = q0 + jnp.arange(q_blk, dtype=jnp.int32)
        rows = lambda a: lax.dynamic_slice_in_dim(a, q0, q_blk, axis=1)
        band = lambda a: lax.dynamic_slice_in_dim(a, q0, WINDOW + q_blk, axis=1)
        w_pos = q0 - WINDOW + jnp.arange(WINDOW + q_blk, dtype=jnp.int32)
        return attend_block(t_pos, rows(q_n), rows(gates), rows(q_f), rows(ck), band(kw_pad), band(vw_pad), w_pos,
                            kc, vc, c_end, ovl, ksb, vsb, k_f, v_f, ck, rel_bias)

    o_n, o_f = lax.map(one_block, jnp.arange(T // q_blk, dtype=jnp.int32))
    o_n = jnp.swapaxes(o_n, 0, 1).reshape(B, T, NSA_HEADS * HEAD_DIM)
    o_f = jnp.swapaxes(o_f, 0, 1).reshape(B, T, FOX_HEADS * HEAD_DIM)
    n_win = min(WINDOW, T)
    state = (jnp.stack([k_c, v_c, k_s, v_s], axis=2), jnp.stack([k_f, v_f], axis=2), logf,
             jnp.stack([k_w, v_w], axis=2)[:, T - n_win:])
    return o_n, o_f, state

def mixer_sample(h, past_nsa, past_fox, past_logf, win_buf, w_in, b_gate, b_forget, cmp_pe, cmp_w1, cmp_w2, rel_bias):
    B, T, _ = h.shape
    P = past_nsa.shape[1]
    n_win = win_buf.shape[1]
    q_n, k_c, v_c, k_s, v_s, k_w, v_w, gates, q_f, k_f, v_f, logf = project(h, w_in, b_gate, b_forget)
    cat = lambda past, new: jnp.concatenate([past.astype(new.dtype), new], axis=1)
    kc, vc, c_end, ovl, ksb, vsb = nsa_full_keys(cat(past_nsa[:, :, 0], k_c), cat(past_nsa[:, :, 1], v_c),
                                                 cat(past_nsa[:, :, 2], k_s), cat(past_nsa[:, :, 3], v_s),
                                                 cmp_pe, cmp_w1, cmp_w2)
    kw = cat(win_buf[:, :, 0], k_w)
    vw = cat(win_buf[:, :, 1], v_w)
    w_pos = P - n_win + jnp.arange(n_win + T, dtype=jnp.int32)
    t_pos = P + jnp.arange(T, dtype=jnp.int32)
    ck = jnp.cumsum(cat(past_logf, logf), axis=1)
    o_n, o_f = attend_block(t_pos, q_n, gates, q_f, ck[:, P:], kw, vw, w_pos, kc, vc, c_end, ovl, ksb, vsb,
                            cat(past_fox[:, :, 0], k_f), cat(past_fox[:, :, 1], v_f), ck, rel_bias)
    state = (jnp.stack([k_c, v_c, k_s, v_s], axis=2), jnp.stack([k_f, v_f], axis=2), logf,
             jnp.stack([kw, vw], axis=2)[:, T:])
    return o_n, o_f, state

def finish_layer(x, o_n, o_f, g_n, g_f, w_o, g_post_mix, g_pre_ffn, g_post_ffn, w_gate, w_up, w_down):
    mixed = jnp.concatenate([rms_norm(o_n, g_n), rms_norm(o_f, g_f)], axis=-1) @ w_o
    x = x + rms_norm(mixed, g_post_mix)
    hf = rms_norm(x, g_pre_ffn)
    ffn = (jax.nn.silu(hf @ w_gate) * (hf @ w_up)) @ w_down
    return x + rms_norm(ffn, g_post_ffn)

def setup_inputs(seed: int = 0) -> dict:
    key = jax.random.key(seed)
    ks = jax.random.split(key, 32)

    def nrm(k, shape, scale=1.0):
        return scale * jax.random.normal(k, shape, jnp.float32)

    def gain(k, shape):
        return 1.0 + nrm(k, shape, 0.05)

    n_pages = PAST_LEN // PAGE_SIZE
    n_pool = (5 * DEC_BATCH * n_pages) // 4
    n_win = min(WINDOW, PAST_LEN)
    page_table = jax.random.permutation(ks[6], n_pool)[: DEC_BATCH * n_pages].reshape(DEC_BATCH, n_pages).astype(jnp.int32)
    return {
        'x_prompt': nrm(ks[0], (BATCH, SEQ, D_MODEL)),
        'x_sample': nrm(ks[1], (DEC_BATCH, DEC_SEQ, D_MODEL)),
        'cache_nsa_kv': nrm(ks[2], (DEPTH, n_pool, PAGE_SIZE, 4, NSA_KV_HEADS, HEAD_DIM)),
        'cache_fox_kv': nrm(ks[3], (DEPTH, n_pool, PAGE_SIZE, 2, FOX_HEADS, HEAD_DIM)),
        'cache_fox_logf': jax.nn.log_sigmoid(FORGET_BIAS_INIT + nrm(ks[4], (DEPTH, n_pool, PAGE_SIZE, FOX_HEADS))),
        'state_win_kv': nrm(ks[5], (DEPTH, DEC_BATCH, n_win, 2, NSA_KV_HEADS, HEAD_DIM)),
        'page_table': page_table,
        'rel_bias': nrm(ks[7], (T5_BUCKETS, NSA_HEADS), 0.5),
        'norm_mix_pre': gain(ks[8], (DEPTH, D_MODEL)),
        'norm_mix_post': gain(ks[9], (DEPTH, D_MODEL)),
        'norm_ffn_pre': gain(ks[10], (DEPTH, D_MODEL)),
        'norm_ffn_post': gain(ks[11], (DEPTH, D_MODEL)),
        'w_in': nrm(ks[12], (DEPTH, D_MODEL, IN_COLS), D_MODEL ** -0.5),
        'b_gate': nrm(ks[13], (DEPTH, 3, NSA_HEADS), 0.1),
        'b_forget': FORGET_BIAS_INIT + nrm(ks[14], (DEPTH, FOX_HEADS), 0.5),
        'cmp_pe': nrm(ks[15], (DEPTH, 2, CMP_BLOCK, HEAD_DIM), 0.1),
        'cmp_w1': nrm(ks[16], (DEPTH, 2, CMP_BLOCK * HEAD_DIM, CMP_HIDDEN), (CMP_BLOCK * HEAD_DIM) ** -0.5),
        'cmp_w2': nrm(ks[17], (DEPTH, 2, CMP_HIDDEN, HEAD_DIM), CMP_HIDDEN ** -0.5),
        'grp_norm_nsa': gain(ks[18], (DEPTH, NSA_HEADS * HEAD_DIM)),
        'grp_norm_fox': gain(ks[19], (DEPTH, FOX_HEADS * HEAD_DIM)),
        'w_o': nrm(ks[20], (DEPTH, MIX_WIDTH, D_MODEL), MIX_WIDTH ** -0.5),
        'w_ffn_gate': nrm(ks[21], (DEPTH, D_MODEL, D_FF), D_MODEL ** -0.5),
        'w_ffn_up': nrm(ks[22], (DEPTH, D_MODEL, D_FF), D_MODEL ** -0.5),
        'w_ffn_down': nrm(ks[23], (DEPTH, D_FF, D_MODEL), D_FF ** -0.5),
    }

def reference(x_prompt, x_sample, cache_nsa_kv, cache_fox_kv, cache_fox_logf, state_win_kv, page_table,
              rel_bias, norm_mix_pre, norm_mix_post, norm_ffn_pre, norm_ffn_post, w_in, b_gate, b_forget,
              cmp_pe, cmp_w1, cmp_w2, grp_norm_nsa, grp_norm_fox, w_o, w_ffn_gate, w_ffn_up, w_ffn_down):
    n_seq, n_pages = page_table.shape

    def gather_pages(cache):
        return cache[page_table].reshape((n_seq, n_pages * PAGE_SIZE) + cache.shape[2:])

    xp, xs = x_prompt, x_sample
    st_p, st_s = [], []
    for l in range(DEPTH):
        o_n, o_f, s_p = mixer_prompt(rms_norm(xp, norm_mix_pre[l]), w_in[l], b_gate[l], b_forget[l],
                                     cmp_pe[l], cmp_w1[l], cmp_w2[l], rel_bias)
        xp = finish_layer(xp, o_n, o_f, grp_norm_nsa[l], grp_norm_fox[l], w_o[l], norm_mix_post[l],
                          norm_ffn_pre[l], norm_ffn_post[l], w_ffn_gate[l], w_ffn_up[l], w_ffn_down[l])
        o_n, o_f, s_s = mixer_sample(rms_norm(xs, norm_mix_pre[l]), gather_pages(cache_nsa_kv[l]),
                                     gather_pages(cache_fox_kv[l]), gather_pages(cache_fox_logf[l]),
                                     state_win_kv[l], w_in[l], b_gate[l], b_forget[l],
                                     cmp_pe[l], cmp_w1[l], cmp_w2[l], rel_bias)
        xs = finish_layer(xs, o_n, o_f, grp_norm_nsa[l], grp_norm_fox[l], w_o[l], norm_mix_post[l],
                          norm_ffn_pre[l], norm_ffn_post[l], w_ffn_gate[l], w_ffn_up[l], w_ffn_down[l])
        st_p.append(s_p)
        st_s.append(s_s)

    stack = lambda states, i: jnp.stack([s[i] for s in states], axis=0)
    return (xp, xs, stack(st_p, 0), stack(st_p, 1), stack(st_p, 2), stack(st_p, 3),
            stack(st_s, 0), stack(st_s, 1), stack(st_s, 2), stack(st_s, 3))


_drawn_inputs = setup_inputs


def setup_inputs(seed=0):
    import zlib

    import numpy as np

    out = dict(_drawn_inputs(seed))
    spreads = {}
    factors = {}
    for name, (base, spread) in spreads.items():
        noise = np.random.default_rng([zlib.crc32(name.encode()), seed]).standard_normal(out[name].shape)
        drawn = base * np.exp(spread * noise) if base else spread * noise
        out[name] = jnp.asarray(drawn.astype(out[name].dtype))
    for name, factor in factors.items():
        out[name] = (out[name] * factor).astype(out[name].dtype)
    return out
```

```python
import numpy as np
import concourse.bass as bass
from concourse import mybir
from contextlib import ExitStack

F32 = mybir.dt.float32
F32R = mybir.dt.float32r
I32 = mybir.dt.int32
ACT = mybir.ActivationFunctionType
ALU = mybir.AluOpType
AX = mybir.AxisListType

P = 128
D = 1024
KD = D // P
T = 1024
QT = T // P
NS, TS = 8, 4
S = NS * TS
N = T + S
NB = N // 3
DH = 64
H = 8
G, R = 2, 4
PAST = 1024
PAGE = 128
PAGES = PAST // PAGE
WIN = 512
DFF = 2816
FT = DFF // P
CB, CS = 32, 16
NC = PAST // CS - 1
EPS = 1e-6
POOL_PAGES = 80
NEG = -1e30
SCALE = DH ** -0.5
GF = 64
GATE0 = 32


class Steps:

    def __init__(self, sem, names, rounds=1):
        self.sem, self.names, self.per = sem, list(names), len(names)
        self.index = {n: i for i, n in enumerate(self.names)}
        assert len(self.index) == self.per, "two steps of one name"
        self.slack = self.per if rounds > 1 else 0
        self.cursor = 0

    def start(self, eng):
        if self.slack:
            eng.sem_inc(self.sem, self.slack)

    def at(self, name, i=0, back=0):
        return i * self.per + (self.index[name] + 1 + self.slack - back * self.per)

    def wait(self, eng, name, i=0, back=0):
        if back and not self.slack:
            return
        eng.wait_ge(self.sem, self.at(name, i, back))

    def done(self, instruction, name):
        assert self.names[self.cursor] == name, (self.names[self.cursor], name)
        self.cursor = (self.cursor + 1) % self.per
        instruction.then_inc(self.sem, 1)


def apart(eng):
    eng.nop(nofuse=True)


def projection_plan():
    loops = [dict(name="q_n", col=0, pairs=2, turn=False), dict(name="nsa_kv", col=512, pairs=2, turn=True),
             dict(name="win_kv", col=1024, pairs=1, turn=True), dict(name="q_f", col=1304, pairs=2, turn=False),
             dict(name="fox_kv", col=1816, pairs=4, turn=True)]
    n = t = 0
    stored = [16, 16]
    for l in loops:
        l.update(n0=n, t0=t, stored0=list(stored))
        n += 2 * l["pairs"]
        if l["turn"]:
            t += 2 * l["pairs"]
            per = [32, 48] if l["name"] == "win_kv" else [32, 32]
            l["per"] = per
            stored = [a + b * l["pairs"] for a, b in zip(stored, per)]
    return loops, n, t, stored


PLAN, NZ, NTURN, NAT_STORED = projection_plan()
TILE = {l["name"]: l["n0"] for l in PLAN}


def program(nc, a, o, c):
    (y_prompt, y_sample, nsa_kv_prompt, fox_kv_prompt, logf_prompt, win_kv_prompt,
     nsa_kv_sample, fox_kv_sample, logf_sample, win_kv_sample) = o
    root = ExitStack()
    with root:
        def sb(ctx, name, shape, dt=F32):
            return ctx.enter_context(nc.sbuf_tensor(name, shape, dt))

        def sem(name):
            return root.enter_context(nc.semaphore(name))

        psum = root.enter_context(nc.psum_tensor("psum", [P, 8, 512], F32))
        bank = [psum[:, i, :] for i in range(8)]

        zT = nc.dram_tensor("zT", (NZ, P, N), F32).ap()
        vw_nat = nc.dram_tensor("vw_nat", (T, P), F32).ap()
        negck = nc.dram_tensor("negck", (H, T), F32).ap()
        gfT = nc.dram_tensor("gfT", (GF, N), F32).ap()
        bias_tab = nc.dram_tensor("bias_tab", (H, P, 384), F32).ap()
        gates_dram = nc.dram_tensor("gates_dram", (3, NS, H * TS), F32).ap()
        kc_dram = nc.dram_tensor("kc_dram", (G * DH, NC), F32).ap()
        vc_dram = nc.dram_tensor("vc_dram", (NC, G * DH), F32).ap()
        oT_dram = nc.dram_tensor("oT_dram", (2 * H * DH, N), F32).ap()

        xT = sb(root, "xT", [P, KD, N])
        ident = sb(root, "ident", [P, P])
        ones = sb(root, "ones", [P, P])
        gains = sb(root, "gains", [P, 6, KD])
        eps = sb(root, "eps", [P, 1])
        gf_nat = sb(root, "gf_nat", [P, QT + 1, GF])

        env = dict(locals())
        build_a(nc, a, o, c, env)
        build_b(nc, a, o, c, env)
        build_c(nc, a, o, c, env)
        hfT = sb(root, "hfT", [P, KD, N])
        build_d(nc, a, env, hfT)
        build_e(nc, a, env, hfT)
        build_f(nc, a, o, env, hfT)


def product(nc, dst, w_hi, w_lo, x_hi, x_lo, start, stop):
    nc.tensor.matmul(dst, w_hi, x_hi, start=start, stop=False)
    nc.tensor.matmul(dst, w_hi, x_lo, start=False, stop=False)
    return nc.tensor.matmul(dst, w_lo, x_hi, start=False, stop=stop)


def norm_act(nc, act, src, n, sq, sq_free, sq_ready):
    for k in range(n):
        if k >= 2:
            act.wait_ge(sq_free, k - 1)
        nc.scalar.activation(sq[:, k % 2, :], src(k), ACT.Square).then_inc(sq_ready, 1)


def build_a(nc, a, o, c, env):
    (y_prompt, y_sample, nsa_kv_prompt, fox_kv_prompt, logf_prompt, win_kv_prompt,
     nsa_kv_sample, fox_kv_sample, logf_sample, win_kv_sample) = o
    xT, ident, ones, gains, gf_nat, bank = (env[k] for k in ("xT", "ident", "ones", "gains", "gf_nat", "bank"))
    eps = env["eps"]
    zT, vw_nat, negck, gfT = (env[k] for k in ("zT", "vw_nat", "negck", "gfT"))
    sem = env["sem"]
    ctx = ExitStack()
    with ctx:
        def sb(name, shape, dt=F32):
            return ctx.enter_context(nc.sbuf_tensor(name, shape, dt))

        x_hi = sb("x_hi", [P, KD, N], F32R)
        with ExitStack() as early:
            x_nat = early.enter_context(nc.sbuf_tensor("x_nat", [P, QT, D], F32))
            xs_nat = early.enter_context(nc.sbuf_tensor("xs_nat", [S, D], F32))
        x_lo = sb("x_lo", [P, KD, N], F32R)
        sq = sb("sq", [P, 2, N])
        ssum = sb("ssum", [P, N])
        rstd = sb("rstd", [P, N])
        w_ring = sb("w_ring", [P, 2, KD, P])
        w_hi = sb("w_hi", [P, 2, KD, P], F32R)
        w_lo = sb("w_lo", [P, 2, KD, P], F32R)
        w_gf = sb("w_gf", [P, KD, GF])
        w_gf_hi = sb("w_gf_hi", [P, KD, GF], F32R)
        w_gf_lo = sb("w_gf_lo", [P, KD, GF], F32R)
        z_stage = sb("z_stage", [P, 2, N])
        nat = sb("nat", [P, 2, QT + 1, P])
        gf_bias = sb("gf_bias", [GF, 1])
        gfz = sb("gfz", [GF, N])
        lf_min = sb("lf_min", [H, N])
        lf_abs = sb("lf_abs", [H, N])
        neg_cum = sb("neg_cum", [H, T])

        x_loaded = [sem(f"x_loaded{t}") for t in range(QT + 1)]
        const_loaded = sem("const_loaded")
        gf_loaded = sem("gf_loaded")
        ones_set = sem("ones_set")
        xt_turned = sem("xt_turned")
        xt_copied = sem("xt_copied")
        sq_ready = sem("sq_ready")
        ssum_ready = sem("ssum_ready")
        ms_ready = sem("ms_ready")
        rms_ready = sem("rms_ready")
        rstd_ready = sem("rstd_ready")
        xn_ready = sem("xn_ready")
        w_loaded = [sem(f"w_loaded{s}") for s in range(2)]
        w_high = sem("w_high")
        w_split = sem("w_split")
        gf_split = sem("gf_split")
        xn_high = sem("xn_high")
        xn_split = sem("xn_split")
        z_done = sem("z_done")
        z_copied = sem("z_copied")
        zt_stored = [sem(f"zt_stored{s}") for s in range(2)]
        turned = sem("turned")
        turn_copied = sem("turn_copied")
        nat_stored = [sem(f"nat_stored{s}") for s in range(2)]
        gf_done = sem("gf_done")
        gf_act = sem("gf_act")
        gf_dve = sem("gf_dve")
        gf_turned = sem("gf_turned")
        gf_copied = sem("gf_copied")
        gf_stored = sem("gf_stored")
        win_moved = sem("win_moved")

        W = a["w_in"][0].rearrange("(k p) n -> p k n", p=P)
        block = ctx.enter_context(nc.Block())

        @block.sync
        def _(sp):
            for t in range(QT):
                sp.dma_start(x_nat[:, t, :], a["x_prompt"][0, t * P:(t + 1) * P, :]).then_inc(x_loaded[t], 16)
            sp.dma_start(xs_nat[:, :], a["x_sample"].rearrange("s t d -> (s t) d")).then_inc(x_loaded[QT], 16)
            for s in range(2):
                sp.sem_inc(zt_stored[s], 16)
                sp.sem_inc(nat_stored[s], 16)
            sp.wait_ge(gf_act, 4)
            sp.wait_ge(gf_dve, 5)
            sp.dma_start(gfT[:, :], gfz[:, :]).then_inc(gf_stored, 16)
            sp.dma_start(negck[:, :], neg_cum[:, :]).then_inc(gf_stored, 16)
            sp.wait_ge(gf_copied, 2)
            with nc.allow_non_contiguous_dma(reason="eight numbers per token"):
                sp.dma_start(logf_prompt[0, 0].rearrange("(t p) h -> p t h", p=P), gf_nat[:, 0:QT, 0:H]).then_inc(gf_stored, 16)
                sp.dma_start(logf_sample[0].rearrange("s t h -> (s t) h"), gf_nat[0:S, QT, 0:H]).then_inc(gf_stored, 16)

            for l in PLAN:
                def pair(i):
                    for s in range(2):
                        n = i * 2 + (l["n0"] + s)
                        sp.wait_ge(z_copied, n + 3)
                        sp.dma_start(zT[bass.ds(n, 1)].rearrange("o p n -> p (o n)"), z_stage[:, s, :]).then_inc(zt_stored[s], 16)
                    if not l["turn"]:
                        return
                    for s in range(2):
                        m = i * 2 + (l["t0"] + s)
                        sp.wait_ge(turn_copied, m * 3 + 5)
                        done = nat_stored[s]
                        if l["name"] == "win_kv":
                            kv = s
                            sp.dma_start(win_kv_prompt[0, 0].rearrange("(t p) a g d -> p t a (g d)", p=P)[:, :, kv],
                                           nat[:, s, QT // 2:QT, :]).then_inc(done, 16)
                            sp.dma_start(win_kv_sample[0, :, WIN - TS:WIN, kv].rearrange("s t g d -> s t (g d)"),
                                           nat[0:S, s, QT, :]).then_inc(done, 16)
                            if s == 1:
                                sp.dma_start(vw_nat.rearrange("(t p) d -> p t d", p=P), nat[:, s, 0:QT, :]).then_inc(done, 16)
                        else:
                            op, os = (nsa_kv_prompt, nsa_kv_sample) if l["name"] == "nsa_kv" else (fox_kv_prompt, fox_kv_sample)
                            cols = bass.ds(i * 256 + s * P, P)
                            sp.dma_start(op[0, 0].rearrange("(t p) a g d -> p t (a g d)", p=P)[:, :, cols],
                                           nat[:, s, 0:QT, :]).then_inc(done, 16)
                            sp.dma_start(os[0].rearrange("s t a g d -> (s t) (a g d)")[:, cols],
                                           nat[0:S, s, QT, :]).then_inc(done, 16)
                loop(sp, l["pairs"], pair)
            for s in range(2):
                sp.wait_ge(zt_stored[s], 16 + 16 * (NZ // 2))
                sp.wait_ge(nat_stored[s], NAT_STORED[s])
            sp.wait_ge(gf_stored, 64)

        @block.gpsimd
        def _(pool):
            pool.memset(ones[:, :], 1.0).then_inc(ones_set, 1)
            pool.memset(w_gf[:, :, :], 0.0).then_inc(ones_set, 1)
            pool.memset(gf_bias[:, :], 0.0).then_inc(ones_set, 1)
            pool.memset(eps[:, :], EPS).then_inc(ones_set, 1)
            pool.dma_start(ident[:, :], c["ident"]).then_inc(const_loaded, 16)
            with nc.allow_non_contiguous_dma(reason="gains are one number per row"):
                for i, g in enumerate(("norm_mix_pre", "norm_mix_post", "norm_ffn_pre", "norm_ffn_post")):
                    pool.dma_start(gains[:, i, :], a[g][0].rearrange("(k p) -> p k", p=P)).then_inc(const_loaded, 16)
                pool.dma_start(gains[:, 4, 0:4], a["grp_norm_nsa"][0].rearrange("(k p) -> p k", p=P)).then_inc(const_loaded, 16)
                pool.dma_start(gains[:, 4, 4:8], a["grp_norm_fox"][0].rearrange("(k p) -> p k", p=P)).then_inc(const_loaded, 16)
                pool.wait_ge(ones_set, 4)
                pool.dma_start(w_gf[:, :, 0:H], W[:, :, 2840:2848]).then_inc(gf_loaded, 16)
                pool.dma_start(w_gf[:, :, GATE0:GATE0 + 24], W[:, :, 1280:1304]).then_inc(gf_loaded, 16)
                pool.dma_start(gf_bias[0:H, :], a["b_forget"][0].rearrange("(h o) -> h o", o=1)).then_inc(gf_loaded, 16)
                pool.dma_start(gf_bias[GATE0:GATE0 + 24, :], a["b_gate"][0].rearrange("b (h o) -> (b h) o", o=1)).then_inc(gf_loaded, 16)
            pool.dma_start(win_kv_sample[0, :, 0:WIN - TS].rearrange("s w a g d -> s w (a g d)"),
                           a["state_win_kv"][0, :, TS:WIN].rearrange("s w a g d -> s w (a g d)")).then_inc(win_moved, 16)
            for l in PLAN:
                def pair(i):
                    for s in range(2):
                        n = i * 2 + (l["n0"] + s)
                        pool.wait_ge(w_split, n + 1)
                        pool.dma_start(w_ring[:, s], W[:, :, bass.ds(i * 256 + (l["col"] + s * P), P)]).then_inc(w_loaded[s], 16)
                loop(pool, l["pairs"], pair)

            pool.wait_ge(win_moved, 16)

        @block.tensor
        def _(pe):
            pe.sem_inc(z_done, 2)
            pe.wait_ge(const_loaded, 16 * 7)
            for t in range(QT + 1):
                rows = P if t < QT else S
                pe.wait_ge(x_loaded[t], 16)
                for b in range(2):
                    j = 2 * t + b
                    if j >= 6:
                        pe.wait_ge(xt_copied, j - 5)
                    for q in range(4):
                        k = 4 * b + q
                        src = x_nat[:, t, k * P:(k + 1) * P] if t < QT else xs_nat[:, k * P:(k + 1) * P]
                        last = nc.tensor.transpose(bank[j % 6][:, q * P:q * P + rows], src, ident[0:rows, 0:rows])
                    last.then_inc(xt_turned, 1)
            pe.wait_ge(xt_copied, 18)
            pe.wait_ge(ones_set, 4)
            pe.wait_ge(ssum_ready, KD)
            for b in range(3):
                last = nc.tensor.matmul(bank[b][:, 0:NB], ones[:, :], ssum[:, b * NB:(b + 1) * NB], start=True, stop=True)
            last.then_inc(ms_ready, 1)
            pe.wait_ge(gf_split, 2)
            pe.wait_ge(xn_split, KD)
            for b in range(3):
                for k in range(KD):
                    tok = slice(b * NB, (b + 1) * NB)
                    last = product(nc, bank[3 + b][:, 0:NB][0:GF], w_gf_hi[:, k, :], w_gf_lo[:, k, :], x_hi[:, k, tok], x_lo[:, k, tok],
                                   k == 0, k == KD - 1)
            last.then_inc(gf_done, 1)
            pe.wait_ge(gf_act, 4)
            pe.wait_ge(gf_dve, 5)
            for t in range(QT + 1):
                n = P if t < QT else S
                dst = bank[6][0:n, t * GF:(t + 1) * GF] if t < QT else bank[7][0:n, 0:GF]
                last = nc.tensor.transpose(dst, gfz[:, t * P:t * P + n], ident[0:GF, 0:GF])
            last.then_inc(gf_turned, 1)
            pe.wait_ge(gf_copied, 2)
            for l in PLAN:
                def pair(i):
                    for s in range(2):
                        n = i * 2 + (l["n0"] + s)
                        pe.wait_ge(w_split, n + 3)
                        pe.wait_ge(z_copied, n + 1)
                        for b in range(3):
                            for k in range(KD):
                                tok = slice(b * NB, (b + 1) * NB)
                                last = product(nc, bank[3 * s + b][:, 0:NB], w_hi[:, s, k, :], w_lo[:, s, k, :],
                                               x_hi[:, k, tok], x_lo[:, k, tok], k == 0, k == KD - 1)
                        last.then_inc(z_done, 1)
                    if not l["turn"]:
                        return
                    for s in range(2):
                        n = i * 2 + (l["n0"] + s)
                        m = i * 2 + (l["t0"] + s)
                        pe.wait_ge(z_copied, n + 3)
                        for part in range(3):
                            pe.wait_ge(turn_copied, m * 3 + (part + 1))
                            for q in range(4 if part < 2 else 1):
                                t = 4 * part + q
                                cols = P if part < 2 else S
                                dst = bank[6 + (part if s == 0 else 1 - part) % 2]
                                last = nc.tensor.transpose(dst[0:cols, q * P:(q + 1) * P],
                                                           z_stage[:, s, t * P:t * P + cols], ident[:, :])
                            last.then_inc(turned, 1)
                loop(pe, l["pairs"], pair)

        @block.scalar
        def _(act):
            act.wait_ge(xt_copied, 18)
            norm_act(nc, act, lambda k: xT[:, k, :], KD, sq, ssum_ready, sq_ready)
            act.wait_ge(ms_ready, 1)
            act.wait_ge(ones_set, 4)
            for b in range(3):
                last = nc.scalar.activation(rstd[:, b * NB:(b + 1) * NB], bank[b][:, 0:NB], ACT.Sqrt, bias=eps[:, 0:1], scale=1.0 / D)
            last.then_inc(rms_ready, 1)
            for k in range(KD):
                act.wait_ge(xn_ready, k + 1)
                nc.scalar.copy(x_hi[:, k, :], sq[:, k % 2, :]).then_inc(xn_high, 1)
            act.wait_ge(gf_done, 1)
            for b in range(3):
                nc.scalar.activation(gfz[:, b * NB:(b + 1) * NB], bank[3 + b][0:GF, 0:NB], ACT.Identity,
                                     bias=gf_bias[:, :]).then_inc(gf_act, 1) if b == 2 else \
                    nc.scalar.activation(gfz[:, b * NB:(b + 1) * NB], bank[3 + b][0:GF, 0:NB], ACT.Identity, bias=gf_bias[:, :])
            act.wait_ge(gf_act, 1)
            nc.scalar.activation(gfz[GATE0:GF, :], gfz[GATE0:GF, :], ACT.Sigmoid).then_inc(gf_act, 1)
            act.wait_ge(gf_dve, 2)
            nc.scalar.activation(lf_abs[:, :], lf_abs[:, :], ACT.Exp, scale=-1.0).then_inc(gf_act, 1)
            act.wait_ge(gf_act, 3)
            nc.scalar.activation(lf_abs[:, :], lf_abs[:, :], ACT.Ln, bias=1.0).then_inc(gf_act, 1)
            act.sem_inc(z_copied, 2)
            for l in PLAN:
                scale = SCALE if l["name"] in ("q_n", "q_f") else 1.0

                def pair(i):
                    for s in range(2):
                        n = i * 2 + (l["n0"] + s)
                        act.wait_ge(z_done, n + 3)
                        act.wait_ge(zt_stored[s], i * 16 + 16 * (l["n0"] // 2 + 1))
                        for b in range(3):
                            last = nc.scalar.activation(z_stage[:, s, b * NB:(b + 1) * NB], bank[3 * s + b][:, 0:NB],
                                                        ACT.Copy, scale=scale)
                        last.then_inc(z_copied, 1)
                loop(act, l["pairs"], pair)

        @block.vector
        def _(dve):
            for t in range(QT + 1):
                rows = P if t < QT else S
                for b in range(2):
                    j = 2 * t + b
                    dve.wait_ge(xt_turned, j + 1)
                    nc.vector.tensor_copy(xT[:, 4 * b:4 * b + 4, t * P:t * P + rows],
                                          bank[j % 6][:, :].rearrange("p (q n) -> p q n", q=4)[:, :, 0:rows]).then_inc(xt_copied, 1)
            for k in range(KD):
                dve.wait_ge(sq_ready, k + 1)
                if k == 0:
                    nc.vector.tensor_copy(ssum[:, :], sq[:, 0, :]).then_inc(ssum_ready, 1)
                else:
                    dve.wait_ge(ssum_ready, k)
                    nc.vector.tensor_tensor(ssum[:, :], ssum[:, :], sq[:, k % 2, :], ALU.add).then_inc(ssum_ready, 1)
            dve.wait_ge(rms_ready, 1)
            nc.vector.reciprocal(rstd[:, :], rstd[:, :]).then_inc(rstd_ready, 1)
            dve.wait_ge(rstd_ready, 1)
            dve.wait_ge(const_loaded, 16 * 7)
            def low(k):
                dve.wait_ge(xn_high, k + 1)
                nc.vector.tensor_tensor(x_lo[:, k, :], sq[:, k % 2, :], x_hi[:, k, :].bitcast(F32), ALU.subtract).then_inc(xn_split, 1)

            for k in range(KD):
                if k >= 2:
                    dve.wait_ge(xn_split, k - 1)
                nc.vector.scalar_tensor_tensor(out=sq[:, k % 2, :], in0=xT[:, k, :], scalar=gains[:, 0, k:k + 1], in1=rstd[:, :],
                                               op0=ALU.mult, op1=ALU.mult).then_inc(xn_ready, 1)
                if k >= 1:
                    low(k - 1)
            low(KD - 1)
            dve.wait_ge(gf_loaded, 64)
            nc.vector.tensor_copy(w_gf_hi[:, :, :], w_gf[:, :, :]).then_inc(gf_split, 1)
            dve.wait_ge(gf_split, 1)
            nc.vector.tensor_tensor(w_gf_lo[:, :, :], w_gf[:, :, :], w_gf_hi[:, :, :].bitcast(F32), ALU.subtract).then_inc(gf_split, 1)
            dve.sem_inc(w_split, 2)

            def split(n, s, load):
                dve.wait_ge(w_loaded[s], load)
                dve.wait_ge(z_done, n + 1)
                nc.vector.tensor_copy(w_hi[:, s], w_ring[:, s]).then_inc(w_high, 1)
                dve.wait_ge(w_high, n + 1)
                nc.vector.tensor_tensor(w_lo[:, s], w_ring[:, s], w_hi[:, s].bitcast(F32), ALU.subtract).then_inc(w_split, 1)

            split(0, 0, 16)
            split(1, 1, 16)
            dve.wait_ge(gf_act, 1)
            nc.vector.tensor_scalar(lf_min[:, :], gfz[0:H, :], 0.0, None, ALU.min).then_inc(gf_dve, 1)
            dve.wait_ge(gf_dve, 1)
            nc.vector.scalar_tensor_tensor(out=lf_abs[:, :], in0=lf_min[:, :], scalar=-2.0, in1=gfz[0:H, :],
                                           op0=ALU.mult, op1=ALU.add).then_inc(gf_dve, 1)
            dve.wait_ge(gf_act, 4)
            nc.vector.tensor_tensor(gfz[0:H, :], lf_min[:, :], lf_abs[:, :], ALU.subtract).then_inc(gf_dve, 1)
            dve.wait_ge(gf_dve, 3)
            dve.wait_ge(ones_set, 4)
            nc.vector.tensor_tensor_scan(neg_cum[:, :], ones[0:H, 0:1].to_broadcast([H, T]), gfz[0:H, 0:T], 0.0, ALU.mult, ALU.subtract).then_inc(gf_dve, 2)
            dve.wait_ge(gf_turned, 1)
            nc.vector.tensor_copy(gf_nat[:, 0:QT, :], bank[6][:, :].rearrange("p (t g) -> p t g", t=QT)).then_inc(gf_copied, 1)
            nc.vector.tensor_copy(gf_nat[0:S, QT, :], bank[7][0:S, 0:GF]).then_inc(gf_copied, 1)
            dve.sem_inc(turn_copied, 2)
            for l in PLAN:
                def pair(i, ahead=True):
                    for s in range(2):
                        if ahead:
                            n = i * 2 + (l["n0"] + s + 2)
                            split(n, s, i * 16 + 16 * (l["n0"] // 2 + 2))
                    if not l["turn"]:
                        return
                    for s in range(2):
                        m = i * 2 + (l["t0"] + s)
                        dve.wait_ge(nat_stored[s], i * l["per"][s] + l["stored0"][s])
                        for part in range(3):
                            dve.wait_ge(turned, m * 3 + (part + 1))
                            src = bank[6 + (part if s == 0 else 1 - part) % 2]
                            if part < 2:
                                nc.vector.tensor_copy(nat[:, s, 4 * part:4 * part + 4, :],
                                                      src[:, :].rearrange("p (q n) -> p q n", q=4)).then_inc(turn_copied, 1)
                            else:
                                nc.vector.tensor_copy(nat[0:S, s, QT, :], src[0:S, 0:P]).then_inc(turn_copied, 1)
                if l is PLAN[-1]:
                    loop(dve, l["pairs"] - 1, pair)
                    pair(l["pairs"] - 1, ahead=False)
                else:
                    loop(dve, l["pairs"], pair)


def loop(eng, count, body):
    if count == 1:
        body(0)
        return
    with eng.Fori(0, count) as i:
        body(i)



def compress_jobs(seqs):
    jobs = [(("ct", kv, g, half), "AV"[(2 * kv + g + half) % 2]) for kv in range(2) for g in range(G) for half in range(2)]
    jobs += [(("hid", 0), "A"), (("hid", 1), "A"), (("kc",), "V")]
    jobs += [(("vc", b), "V") for b in range(seqs)]
    return jobs


def sample_jobs(b):
    jobs = [("s_cmp", "V"), ("lf0", "V"), ("lf1", "V"), ("ks0", "A"), ("ks1", "A"), ("kw", "A"), ("s_win", "V"), ("s_win_new", "V"),
            ("s_slc0", "V"), ("s_slc1", "V"), ("s_slc_new", "V"), ("pt_imp", "A")]
    jobs += [(f"kf{n}", "AV"[n % 2]) for n in range(4)]
    jobs += [("imp", "A")]
    jobs += [(f"kf{n}", "AV"[n % 2]) for n in range(4, 8)]
    jobs += [("imp_sum", "V"), ("s_fox0", "V"), ("s_fox1", "V"), ("s_fox_new", "V"), ("pt_cw", "A"), ("pt_slc", "A"), ("o_nsa", "V"),
             ("pt_fox", "A"), ("o_fox", "V")]
    return [((name, b), engine) for name, engine in jobs]


class Banks:

    def __init__(self, jobs):
        self.order = [name for name, _ in jobs]
        self.engine = dict(jobs)
        self.bank, self.before = {}, {}
        for engine, first in (("A", 0), ("V", 4)):
            mine = [name for name, e in jobs if e == engine]
            for n, name in enumerate(mine):
                self.bank[name] = first + n % 4
            for n, name in enumerate(mine):
                same = [m for m in range(len(mine)) if m % 4 == n % 4]
                p = same.index(n)
                self.before[name] = (mine[same[p - 1]], int(p == 0))


def compress_dve(seqs):
    return [("ord", 0)] + [("ev", j) for j, e in compress_jobs(seqs) if e == "V"]


def compress_act(seqs):
    return [("ord", 1)] + [("ev", j) for j, e in compress_jobs(seqs) if e == "A"]


def sample_act(b):
    return [(n, b) if isinstance(n, str) else ("ev", (n[1], b)) for n in (
        ("ev", "ks0"), ("ev", "ks1"), ("ev", "kw"), "exp_cmp", ("ev", "pt_imp"), "exp_win", ("ev", "kf0"), ("ev", "kf2"), ("ev", "imp"),
        ("ev", "kf4"), ("ev", "kf6"), "exp_slc", "exp_fox", ("ev", "pt_cw"), ("ev", "pt_slc"), ("ev", "pt_fox"))]


def sample_dve(b):
    return [(n, b) if isinstance(n, str) else ("ev", (n[1], b)) for n in (
        ("ev", "s_cmp"), "max_cmp", ("ev", "lf0"), ("ev", "lf1"), "scan", ("ev", "s_win"), ("ev", "s_win_new"), "max_win",
        ("ev", "s_slc0"), ("ev", "s_slc1"), ("ev", "s_slc_new"),
        "rec_cmp", "norm_cmp", "gate_cmp", "rec_win", "fac_win", "gate_win", ("ev", "kf1"), ("ev", "kf3"), ("ev", "kf5"), ("ev", "kf7"),
        ("ev", "imp_sum"), "least", "which", "last", "drop", "mask", "max_slc",
        ("ev", "s_fox0"), ("ev", "s_fox1"), ("ev", "s_fox_new"), "max_fox",
        "rec_slc", "fac_slc", "gate_slc", "rec_fox", "gate_fox", ("ev", "o_nsa"), ("ev", "o_fox"))]


def order_chunks(nc, eng, copy, i, kv, seqs, PE, MINE, buf, loaded):
    rows = seqs * DH
    eng.wait_ge(*loaded)
    PE.wait(eng, ("ct", kv, 1, 1), i, back=1)
    for g in range(G):
        col = (2 * kv + g) * DH
        last = copy(buf["chunks_by_head"][0:rows, kv, g], buf["chunks"][0:rows, :, col:col + DH])
    MINE.done(last, ("ord", kv))


def pe_compress(nc, pe, i, seqs, B, PE, ENG, buf):
    rows = seqs * DH
    psum, ident = buf["psum"], buf["ident"]
    n_blk = seqs * NC

    def start(job):
        before, back = B.before[job]
        e = ENG[B.engine[job]]
        e.wait(pe, ("ev", before), i, back=back) if (back == 0 or e.slack) else None
        return psum[:, B.bank[job], :]

    for kv in range(2):
        ENG["VA"[kv]].wait(pe, ("ord", kv), i)
        for g in range(G):
            for half in range(2):
                job = ("ct", kv, g, half)
                dst = start(job)
                for q in range(4):
                    jj = 4 * half + q
                    src = buf["chunks_by_head"][0:rows, kv, g, 2 * jj:2 * jj + 2].rearrange("p j d -> p (j d)")
                    last = nc.tensor.transpose(dst[:, q * P:q * P + rows], src, ident[0:rows, 0:rows])
                PE.done(last, job)
    for kv in range(2):
        job = ("hid", kv)
        dst = start(job)
        for g in range(G):
            for half in range(2):
                j = ("ct", kv, g, half)
                ENG[B.engine[j]].wait(pe, ("ev", j), i)
        ct = buf["chunksT"][:, kv].rearrange("p j g (b c) -> p j g b c", c=DH)
        for jj in range(16):
            first = jj // 8
            for g in range(G):
                last = nc.tensor.matmul(dst[:, g * n_blk:(g + 1) * n_blk], buf["w1"][:, kv, jj, :],
                                        ct[:, jj % 8, g, 0:seqs, first:first + NC], start=(jj == 0 and g == 0), stop=(jj == 15),
                                        skip_group_check=True)
        PE.done(last, job)
    job = ("kc",)
    dst = start(job)
    ENG["A"].wait(pe, ("ev", ("hid", 0)), i)
    w2k = buf["w2k"]
    nc.tensor.matmul(dst[:, 0:n_blk], w2k[:, DH:3 * DH], buf["hidden"][:, 0, 0:n_blk], start=True, stop=False)
    PE.done(nc.tensor.matmul(dst[:, 0:n_blk], w2k[:, 0:2 * DH], buf["hidden"][:, 0, n_blk:2 * n_blk], start=False, stop=True), job)
    for b in range(seqs):
        job = ("vc", b)
        dst = start(job)
        ENG["A"].wait(pe, ("ev", ("hid", 1)), i)
        apart(pe)
        for g in range(G):
            at = g * n_blk + b * NC
            last = nc.tensor.matmul(dst[0:NC, g * DH:(g + 1) * DH], buf["hidden"][:, 1, at:at + NC], buf["w2v"][:, :], start=True, stop=True)
        PE.done(last, job)


def evict_ct(nc, eng, copy, i, seqs, B, PE, MINE, buf, job):
    _, kv, g, half = job
    rows = seqs * DH
    PE.wait(eng, job, i)
    if PE.slack:
        PE.wait(eng, ("s_fox1", 1), i, back=1)
    MINE.done(copy(buf["chunksT"][:, kv, 4 * half:4 * half + 4, g, 0:rows],
                   buf["psum"][:, B.bank[job], :].rearrange("p (q n) -> p q n", q=4)[:, :, 0:rows]), ("ev", job))


def act_compress(nc, act, i, seqs, B, PE, MINE, buf, loaded):
    order_chunks(nc, act, nc.scalar.copy, i, 1, seqs, PE, MINE, buf, loaded)
    for job, e in compress_jobs(seqs):
        if e != "A":
            continue
        if job[0] == "ct":
            evict_ct(nc, act, nc.scalar.copy, i, seqs, B, PE, MINE, buf, job)
        else:
            kv = job[1]
            PE.wait(act, job, i)
            PE.wait(act, ("kc",) if kv == 0 else ("vc", seqs - 1), i, back=1)
            n = G * seqs * NC
            MINE.done(nc.scalar.activation(buf["hidden"][:, kv, 0:n], buf["psum"][:, B.bank[job], 0:n], ACT.Gelu_apprx_tanh,
                                           bias=buf["pe_bias"][:, kv:kv + 1]), ("ev", job))


def dve_compress(nc, dve, i, seqs, B, PE, MINE, buf, loaded, kc_free, vc_free):
    order_chunks(nc, dve, nc.vector.tensor_copy, i, 0, seqs, PE, MINE, buf, loaded)
    for job, e in compress_jobs(seqs):
        if e != "V":
            continue
        if job[0] == "ct":
            evict_ct(nc, dve, nc.vector.tensor_copy, i, seqs, B, PE, MINE, buf, job)
        elif job[0] == "kc":
            PE.wait(dve, job, i)
            kc_free(dve)
            MINE.done(nc.vector.tensor_copy(buf["kc"][:, 0:seqs * NC], buf["psum"][:, B.bank[job], 0:seqs * NC]), ("ev", job))
        else:
            b = job[1]
            PE.wait(dve, job, i)
            vc_free(dve, b)
            MINE.done(nc.vector.tensor_copy(buf["vc"][0:NC, b, :], buf["psum"][0:NC, B.bank[job], 0:P]), ("ev", job))


def build_b(nc, a, o, c, env):
    (y_prompt, y_sample, nsa_kv_prompt, fox_kv_prompt, logf_prompt, win_kv_prompt,
     nsa_kv_sample, fox_kv_sample, logf_sample, win_kv_sample) = o
    ident, psum, sem = env["ident"], env["psum"], env["sem"]
    zT, gfT, oT_dram, bias_tab, kc_dram, vc_dram, gates_dram = (env[k] for k in ("zT", "gfT", "oT_dram", "bias_tab", "kc_dram", "vc_dram", "gates_dram"))
    ctx = ExitStack()
    with ctx:
        def sb(name, shape, dt=F32, where=None):
            return (where or ctx).enter_context(nc.sbuf_tensor(name, shape, dt))

        w1 = sb("w1", [P, 2, 16, P])
        w2k = sb("w2k", [P, 3 * DH])
        w2v = sb("w2v", [P, DH])
        pe_cols = sb("pe_cols", [P, 2, 16])
        pe_bias = sb("pe_bias", [P, 2])
        chunks = sb("chunks", [P, CS, 2 * P])
        chunks_by_head = sb("chunks_by_head", [P, 2, G, CS, DH])
        turned = sb("turned", [P, 4 * PAST])
        chunksT = turned[:, :].rearrange("p (v j g n) -> p v j g n", v=2, j=8, g=G)
        kT_fox = turned[:, :].rearrange("p (n k) -> p n k", n=4)
        hidden = sb("hidden", [P, 2, G * 2 * NC])
        kc = sb("kc", [P, 2 * NC])
        vc = sb("vc", [NC, 2, P])
        buf = dict(psum=psum, ident=ident, w1=w1, w2k=w2k, w2v=w2v, pe_bias=pe_bias, chunks=chunks, chunks_by_head=chunks_by_head, chunksT=chunksT,
                   hidden=hidden, kc=kc, vc=vc)

        with ExitStack() as first:
            rel = sb("rel", [33, H], where=first)
            onehot = sb("onehot", [33, 384], where=first)
            bias_vec = sb("bias_vec", [H, 384], where=first)
            w_loaded, rel_loaded, rel_set, chunk_loaded = sem("b0_w_loaded"), sem("b0_rel_loaded"), sem("b0_rel_set"), sem("b0_chunk_loaded")
            tab_done, tab_copied, tab_stored = sem("b0_tab_done"), sem("b0_tab_copied"), sem("b0_tab_stored")
            peb_done, peb_copied, w2_zero = sem("b0_peb_done"), sem("b0_peb_copied"), sem("b0_w2_zero")
            B0 = Banks(compress_jobs(1))
            PE0 = Steps(sem("b0_pe"), B0.order)
            ACT0 = Steps(sem("b0_act"), compress_act(1))
            DVE0 = Steps(sem("b0_dve"), compress_dve(1))
            ENG0 = {"A": ACT0, "V": DVE0}
            with nc.Block() as block:
                @block.sync
                def _(sp):
                    sp.dma_start(chunks[0:DH, :, :], nsa_kv_prompt[0, 0].rearrange("(c j) a g d -> c j (a g d)", j=CS)[:, :, 0:2 * P]).then_inc(chunk_loaded, 16)
                    for kv in range(2):
                        sp.dma_start(w1[:, kv], a["cmp_w1"][0, kv].rearrange("(j p) n -> p j n", p=P)).then_inc(w_loaded, 16)
                    sp.wait_ge(w2_zero, 1)
                    sp.dma_start(w2k[:, DH:2 * DH], a["cmp_w2"][0, 0]).then_inc(w_loaded, 16)
                    sp.dma_start(w2v[:, :], a["cmp_w2"][0, 1]).then_inc(w_loaded, 16)
                    with nc.allow_non_contiguous_dma(reason="position embeddings as columns"):
                        for kv in range(2):
                            sp.dma_start(pe_cols[:, kv, :], a["cmp_pe"][0, kv].rearrange("(j b) d -> (b d) j", b=2)).then_inc(w_loaded, 16)
                        for br in range(3):
                            sp.dma_start(gates_dram[br].rearrange("s (h t) -> h s t", t=TS),
                                         gfT[GATE0 + br * H:GATE0 + (br + 1) * H, T:N].rearrange("h (s t) -> h s t", t=TS)).then_inc(tab_stored, 16)
                    sp.dma_start(rel[0:32, :], a["rel_bias"]).then_inc(rel_loaded, 16)
                    sp.dma_start(onehot[:, :], c["onehot"]).then_inc(rel_loaded, 16)
                    sp.wait_ge(tab_copied, 1)
                    sp.dma_start(bias_tab, bias_vec[:, :].unsqueeze(1).to_broadcast([H, P, 384])).then_inc(tab_stored, 16)
                    DVE0.wait(sp, ("ev", ("kc",)))
                    sp.dma_start(kc_dram, kc[:, 0:NC]).then_inc(tab_stored, 16)
                    DVE0.wait(sp, ("ev", ("vc", 0)))
                    sp.dma_start(vc_dram, vc[:, 0, :]).then_inc(tab_stored, 16)
                    sp.wait_ge(tab_stored, 96)

                @block.gpsimd
                def _(pool):
                    pool.memset(w2k[:, :], 0.0).then_inc(w2_zero, 1)
                    pool.wait_ge(w2_zero, 1)
                    pool.memset(rel[32:33, :], NEG).then_inc(rel_set, 1)

                @block.tensor
                def _(pe):
                    pe.wait_ge(rel_loaded, 32)
                    pe.wait_ge(rel_set, 1)
                    nc.tensor.matmul(psum[0:H, 7, 0:384], rel[:, :], onehot[:, :], start=True, stop=True).then_inc(tab_done, 1)
                    pe.wait_ge(tab_copied, 1)
                    pe.wait_ge(w_loaded, 96)
                    for kv in range(2):
                        for jj in range(16):
                            last = nc.tensor.matmul(psum[:, 7, kv:kv + 1], w1[:, kv, jj, :], pe_cols[:, kv, jj:jj + 1], start=(jj == 0), stop=(jj == 15))
                    last.then_inc(peb_done, 1)
                    pe.wait_ge(peb_copied, 1)
                    pe_compress(nc, pe, 0, 1, B0, PE0, ENG0, buf)

                @block.scalar
                def _(act):
                    act.wait_ge(peb_copied, 1)
                    act_compress(nc, act, 0, 1, B0, PE0, ACT0, buf, (chunk_loaded, 16))

                @block.vector
                def _(dve):
                    dve.wait_ge(tab_done, 1)
                    nc.vector.tensor_copy(bias_vec[:, :], psum[0:H, 7, 0:384]).then_inc(tab_copied, 1)
                    dve.wait_ge(peb_done, 1)
                    nc.vector.tensor_copy(pe_bias[:, :], psum[:, 7, 0:2]).then_inc(peb_copied, 1)
                    dve_compress(nc, dve, 0, 1, B0, PE0, DVE0, buf, (chunk_loaded, 16), lambda e: None, lambda e, b: None)

        L = PAST + TS
        pages = sb("pages", [1, NS * PAGES], I32)
        nsa_page = sb("nsa_page", [P, 2, PAGES, 2 * P])
        fox_k = sb("fox_k", [P, PAGES, 512])
        fox_v = sb("fox_v", [P, PAGES, 512])
        win_rows = sb("win_rows", [P, 2, WIN // P, 2 * P])
        lf_rows = sb("lf_rows", [P, 2, PAGES, H])
        kT_slc = sb("kT_slc", [P, PAST])
        kT_win = sb("kT_win", [P, WIN])
        lfT = sb("lfT", [H, 2, L])
        ck = sb("ck", [H, L])
        q_nsa = sb("sq_nsa", [P, 2, 32])
        q_fox = sb("sq_fox", [P, 2, 160])
        k_new = sb("k_new", [P, 2, 6, TS])
        v_new = sb("v_new", [TS, 2, 2 * P + 512])
        gates = sb("gates", [32, 2, 3])
        s_cmp, s_win, s_slc, s_fox = sb("s_cmp", [32, NC]), sb("s_win", [32, WIN + TS]), sb("s_slc", [32, L]), sb("s_fox", [32, L])
        p_imp = sb("p_imp", [32, NC])
        stat = sb("stat", [32, 16])
        choice = sb("choice", [32, 4, 16])
        iota = sb("iota", [32, 16])
        bias_s = sb("bias_s", [32, P + TS])
        bias_c = sb("bias_c", [32, NC])
        mask_new = sb("mask_new", [32, 2 * TS])
        overlap = sb("overlap", [NC, 16])
        group_sum = sb("group_sum", [32, 32])
        neg_pick = sb("neg_pick", [H, 32])
        ptT = sb("ptT", [P, 4, 320])
        imp_rows = sb("imp_rows", [32, 16])
        o_nsa = sb("so_nsa", [P, 2, 32])
        o_fox = sb("so_fox", [P, 2, 160])

        jobs = compress_jobs(2) + sample_jobs(0) + sample_jobs(1)
        B = Banks(jobs)
        RN = NS // 2
        PE = Steps(sem("b_pe"), B.order, RN)
        ACTS = Steps(sem("b_act"), compress_act(2) + sample_act(0) + sample_act(1), RN)
        DVE = Steps(sem("b_dve"), compress_dve(2) + sample_dve(0) + sample_dve(1), RN)
        ENG = {"A": ACTS, "V": DVE}
        setup_loaded, setup_set, bias_c_set = sem("b_setup_loaded"), sem("b_setup_set"), sem("b_bias_c_set")
        pages_loaded = sem("b_pages_loaded")
        ch_loaded = sem("b_ch_loaded")
        fk_loaded = sem("b_fk_loaded")
        fv_loaded = sem("b_fv_loaded")
        ns_loaded = [sem(f"b_ns_loaded{b}") for b in range(2)]
        small_loaded = [sem(f"b_small_loaded{b}") for b in range(2)]
        so_stored = [sem(f"b_so_stored{b}") for b in range(2)]
        so_free = [sem(f"b_so_free{b}") for b in range(2)]
        zrow = zT.rearrange("n p t -> (n p) t")

        with nc.Block() as block:
            @block.sync
            def _(sp):
                sp.dma_start(pages[:, :], a["page_table"].rearrange("s (p o) -> o (s p)", o=1)).then_inc(pages_loaded, 16)
                flat = bias_tab.rearrange("h q x -> h (q x)")[:, 127:127 + P * 383].rearrange("h (q x) -> h q x", x=383)
                for h in range(H):
                    sp.dma_start(bias_s[h * TS:(h + 1) * TS, :], flat[h, 0:TS, 0:P + TS]).then_inc(setup_loaded, 16)
                for dst, name in ((mask_new, "mask_new"), (overlap, "overlap"), (group_sum, "group_sum"), (neg_pick, "neg_pick"), (iota, "iota")):
                    sp.dma_start(dst[:, :], c[name]).then_inc(setup_loaded, 16)
                sp.wait_ge(pages_loaded, 16)
                sp.wait_ge(setup_set, 2)

                def load_chunks(i):
                    for b in range(2):
                        for p in range(PAGES):
                            page = sp.value_load(pages[0:1, bass.ds(i * (2 * PAGES) + (b * PAGES + p), 1)], min_val=0, max_val=POOL_PAGES - 1)
                            src = a["cache_nsa_kv"][0, bass.ds(page, 1)].rearrange("o (c j) a g d -> (o c) j (a g d)", j=CS)[:, :, 0:2 * P]
                            sp.dma_start(chunks[b * DH + p * 8:b * DH + (p + 1) * 8, :, :], src).then_inc(ch_loaded, 16)

                def one_round(i):
                    DVE.wait(sp, ("ord", 0), i, back=1)
                    ACTS.wait(sp, ("ord", 1), i, back=1)
                    load_chunks(i)
                    for b in range(2):
                        s = i * 2 + b
                        other = 1 - b
                        col = s * TS + T
                        back = int(b == 0)
                        PE.wait(sp, ("o_fox", b), i, back=1)
                        with nc.allow_non_contiguous_dma(reason="four new tokens"):
                            small = small_loaded[b]
                            for e in range(2):
                                sp.dma_start(q_fox[e * DH:(e + 1) * DH, b].rearrange("p (n x) -> p n x", x=40)[:, :, 4 * e:4 * e + 4],
                                             zT[TILE["q_f"]:TILE["q_f"] + 4, e * DH:(e + 1) * DH, bass.ds(col, TS)].rearrange("n p t -> p n t")).then_inc(small, 16)
                                sp.dma_start(q_nsa[e * DH:(e + 1) * DH, b, 16 * e:16 * e + 16].rearrange("p (r t) -> p r t", t=TS),
                                             zrow[TILE["q_n"] * P + e * 4 * DH:TILE["q_n"] * P + (e + 1) * 4 * DH, bass.ds(col, TS)].rearrange("(r d) t -> d r t", d=DH)).then_inc(small, 16)
                            sp.dma_start(k_new[:, b, 0, :], zT[TILE["nsa_kv"] + 2, :, bass.ds(col, TS)]).then_inc(small, 16)
                            sp.dma_start(k_new[:, b, 1, :], zT[TILE["win_kv"], :, bass.ds(col, TS)]).then_inc(small, 16)
                            sp.dma_start(k_new[:, b, 2:6, :], zT[TILE["fox_kv"]:TILE["fox_kv"] + 4, :, bass.ds(col, TS)].rearrange("n p t -> p n t")).then_inc(small, 16)
                            sp.dma_start(lfT[:, b, PAST:L], gfT[0:H, bass.ds(col, TS)]).then_inc(small, 16)
                            sp.dma_start(gates[:, b, :], gates_dram[:, bass.ds(s, 1), :].rearrange("b o r -> (o r) b")).then_inc(small, 16)
                        sp.dma_start(v_new[:, b, 0:P], nsa_kv_sample[0, bass.ds(s, 1), :, 3].rearrange("o t g d -> (o t) (g d)")).then_inc(small, 16)
                        sp.dma_start(v_new[:, b, P:2 * P], win_kv_sample[0, bass.ds(s, 1), WIN - TS:WIN, 1].rearrange("o t g d -> (o t) (g d)")).then_inc(small, 16)
                        sp.dma_start(v_new[:, b, 2 * P:2 * P + 512], fox_kv_sample[0, bass.ds(s, 1), :, 1].rearrange("o t h d -> (o t) (h d)")).then_inc(small, 16)
                        sp.dma_start(win_rows[:, b], a["state_win_kv"][0, bass.ds(s, 1)].rearrange("o (t p) a g d -> p (o t) (a g d)", p=P)).then_inc(small, 16)
                        for p in range(PAGES):
                            page = sp.value_load(pages[0:1, bass.ds(i * (2 * PAGES) + (b * PAGES + p), 1)], min_val=0, max_val=POOL_PAGES - 1)
                            sp.dma_start(nsa_page[:, b, p, :], a["cache_nsa_kv"][0, bass.ds(page, 1)].rearrange("o p a g d -> (o p) (a g d)")[:, 2 * P:4 * P]).then_inc(ns_loaded[b], 16)
                            sp.dma_start(lf_rows[:, b, p, :], a["cache_fox_logf"][0, bass.ds(page, 1)].rearrange("o p h -> (o p) h")).then_inc(ns_loaded[b], 16)
                            if p == 0:
                                PE.wait(sp, ("kf7", other), i, back=back)
                            src = a["cache_fox_kv"][0, bass.ds(page, 1)].rearrange("o p a h d -> (o p) (a h d)")
                            sp.dma_start(fox_k[:, p, :], src[:, 0:512]).then_inc(fk_loaded, 16)
                        for p in range(PAGES):
                            page = sp.value_load(pages[0:1, bass.ds(i * (2 * PAGES) + (b * PAGES + p), 1)], min_val=0, max_val=POOL_PAGES - 1)
                            if p == 0:
                                PE.wait(sp, ("o_fox", other), i, back=back)
                            src = a["cache_fox_kv"][0, bass.ds(page, 1)].rearrange("o p a h d -> (o p) (a h d)")
                            sp.dma_start(fox_v[:, p, :], src[:, 512:1024]).then_inc(fv_loaded, 16)
                with sp.Fori(0, RN) as i:
                    one_round(i)

            @block.gpsimd
            def _(pool):
                pool.memset(q_nsa[:, :, :], 0.0).then_inc(setup_set, 1)
                pool.memset(q_fox[:, :, :], 0.0).then_inc(setup_set, 1)
                for s in so_free:
                    pool.sem_inc(s, 1)

                def one_round(i):
                    for b in range(2):
                        cols = bass.ds(i * (2 * TS) + (b * TS + T), TS)
                        with nc.allow_non_contiguous_dma(reason="four tokens of each feature"):
                            DVE.wait(pool, ("ev", ("o_nsa", b)), i)
                            for g in range(G):
                                pool.dma_start(oT_dram[g * 4 * DH:(g + 1) * 4 * DH, cols].rearrange("(r d) t -> d r t", d=DH),
                                               o_nsa[g * DH:(g + 1) * DH, b, 16 * g:16 * g + 16].rearrange("p (r t) -> p r t", t=TS)).then_inc(so_stored[b], 16)
                            DVE.wait(pool, ("ev", ("o_fox", b)), i)
                            for e in range(2):
                                pool.dma_start(oT_dram[H * DH:2 * H * DH, cols].rearrange("(n e d) t -> e d n t", e=2, d=DH)[e],
                                               o_fox[e * DH:(e + 1) * DH, b, 0:160].rearrange("p (n x) -> p n x", x=40)[:, :, 4 * e:4 * e + 4]).then_inc(so_stored[b], 16)
                        pool.wait_ge(so_stored[b], i * 64 + 64)
                        pool.sem_inc(so_free[b], 1)
                with pool.Fori(0, RN) as i:
                    one_round(i)

            @block.tensor
            def _(pe):
                PE.start(pe)
                pe.wait_ge(setup_loaded, 16 * 13)

                def start(job, i):
                    before, back = B.before[job]
                    ENG[B.engine[job]].wait(pe, ("ev", before), i, back=back)
                    return psum[:, B.bank[job], :]

                def one_round(i):
                    pe_compress(nc, pe, i, 2, B, PE, ENG, buf)
                    for b in range(2):
                        def wait_ev(name):
                            ENG[B.engine[name, b]].wait(pe, ("ev", (name, b)), i)

                        def turn_pages(name, src, n):
                            dst = start((name, b), i)
                            for q in range(n):
                                last = nc.tensor.transpose(dst[:, q * P:(q + 1) * P], src(q), ident[:, :])
                            PE.done(last, (name, b))

                        def turn_fox(n):
                            half, p = n // 4, n % 4
                            if n == 0:
                                pe.wait_ge(fk_loaded, i * 256 + 128 * (b + 1))
                            turn_pages(f"kf{n}", lambda q: fox_k[:, 4 * half + q, p * P:(p + 1) * P], 4)

                        pe.wait_ge(small_loaded[b], i * 208 + 208)
                        dst = start(("s_cmp", b), i)
                        if b == 0:
                            DVE.wait(pe, ("ev", ("kc",)), i)
                        PE.done(nc.tensor.matmul(dst[0:32, 0:NC], q_nsa[:, b, :], kc[:, b * NC:(b + 1) * NC], start=True, stop=True), ("s_cmp", b))
                        pe.wait_ge(ns_loaded[b], i * 256 + 256)
                        for half in range(2):
                            dst = start((f"lf{half}", b), i)
                            for q in range(4):
                                last = nc.tensor.transpose(dst[0:H, q * P:(q + 1) * P], lf_rows[:, b, 4 * half + q, :], ident[:, :])
                            PE.done(last, (f"lf{half}", b))
                        for half in range(2):
                            turn_pages(f"ks{half}", lambda q: nsa_page[:, b, 4 * half + q, 0:P], 4)
                        turn_pages("kw", lambda q: win_rows[:, b, q, 0:P], 4)

                        def score(name, terms):
                            dst = start((name, b), i)
                            for n, (lhs, rhs) in enumerate(terms):
                                last = nc.tensor.matmul(dst[0:32, 0:rhs.shape[-1]], lhs, rhs, start=(n == 0), stop=(n == len(terms) - 1))
                            PE.done(last, (name, b))

                        wait_ev("kw")
                        score("s_win", [(q_nsa[:, b, :], kT_win[:, :])])
                        score("s_win_new", [(q_nsa[:, b, :], k_new[:, b, 1, :])])
                        score("s_slc0", [(q_nsa[:, b, :], kT_slc[:, 0:512])])
                        score("s_slc1", [(q_nsa[:, b, :], kT_slc[:, 512:1024])])
                        score("s_slc_new", [(q_nsa[:, b, :], k_new[:, b, 0, :])])
                        dst = start(("pt_imp", b), i)
                        DVE.wait(pe, ("norm_cmp", b), i)
                        apart(pe)
                        PE.done(nc.tensor.transpose(dst[0:NC, 0:32], p_imp[:, :], ident[0:32, 0:32]), ("pt_imp", b))
                        for n in range(4):
                            turn_fox(n)
                        dst = start(("imp", b), i)
                        wait_ev("pt_imp")
                        apart(pe)
                        PE.done(nc.tensor.matmul(dst[0:32, 0:16], ptT[0:NC, 0, 0:32], overlap[:, :], start=True, stop=True), ("imp", b))
                        for n in range(4, 8):
                            turn_fox(n)
                        dst = start(("imp_sum", b), i)
                        wait_ev("imp")
                        apart(pe)
                        PE.done(nc.tensor.matmul(dst[0:32, 0:16], group_sum[:, :], imp_rows[:, :], start=True, stop=True), ("imp_sum", b))
                        DVE.wait(pe, ("scan", b), i)
                        for half in range(2):
                            wait_ev(f"kf{4 * half + 2}")
                            wait_ev(f"kf{4 * half + 3}")
                            cols = slice(half * 512, half * 512 + 512)
                            score(f"s_fox{half}", [(q_fox[:, b, 32 * p:32 * p + 32], kT_fox[:, p, cols]) for p in range(4)] + [(neg_pick[:, :], ck[:, cols])])
                        score("s_fox_new", [(q_fox[:, b, 32 * p:32 * p + 32], k_new[:, b, 2 + p, :]) for p in range(4)] + [(neg_pick[:, :], ck[:, PAST:L])])

                        def turn_probs(name, pieces):
                            dst = start((name, b), i)
                            apart(pe)
                            for n, (src, w) in enumerate(pieces):
                                last = nc.tensor.transpose(dst[0:w, n * 32:n * 32 + 32], src, ident[0:32, 0:32])
                            PE.done(last, (name, b))

                        DVE.wait(pe, ("gate_win", b), i)
                        turn_probs("pt_cw", [(s_cmp[:, :], NC)] + [(s_win[:, n * P:(n + 1) * P], P) for n in range(4)] + [(s_win[:, WIN:WIN + TS], TS)])
                        DVE.wait(pe, ("gate_slc", b), i)
                        turn_probs("pt_slc", [(s_slc[:, n * P:(n + 1) * P], P) for n in range(8)] + [(s_slc[:, PAST:L], TS)])
                        dst = start(("o_nsa", b), i)
                        wait_ev("pt_slc")
                        if b == 0:
                            DVE.wait(pe, ("ev", ("vc", 1)), i)
                        apart(pe)
                        terms = [(vc[:, b, :], ptT[0:NC, 1, 0:32])]
                        terms += [(win_rows[:, b, n, P:2 * P], ptT[:, 1, 32 * (n + 1):32 * (n + 2)]) for n in range(4)]
                        terms += [(v_new[:, b, P:2 * P], ptT[0:TS, 1, 160:192])]
                        terms += [(nsa_page[:, b, n, P:2 * P], ptT[:, 2, 32 * n:32 * (n + 1)]) for n in range(8)]
                        terms += [(v_new[:, b, 0:P], ptT[0:TS, 2, 256:288])]
                        for n, (lhs, rhs) in enumerate(terms):
                            last = nc.tensor.matmul(dst[:, 0:32], lhs, rhs, start=(n == 0), stop=(n == len(terms) - 1))
                        PE.done(last, ("o_nsa", b))
                        DVE.wait(pe, ("gate_fox", b), i)
                        turn_probs("pt_fox", [(s_fox[:, n * P:(n + 1) * P], P) for n in range(8)] + [(s_fox[:, PAST:L], TS)])
                        dst = start(("o_fox", b), i)
                        wait_ev("pt_fox")
                        pe.wait_ge(fv_loaded, i * 256 + 128 * (b + 1))
                        for p in range(4):
                            for n in range(9):
                                lhs = fox_v[:, n, p * P:(p + 1) * P] if n < 8 else v_new[:, b, 2 * P + p * P:2 * P + (p + 1) * P]
                                rhs = ptT[:, 3, 32 * n:32 * n + 32] if n < 8 else ptT[0:TS, 3, 256:288]
                                last = nc.tensor.matmul(dst[:, 32 * p:32 * p + 32], lhs, rhs, start=(n == 0), stop=(n == 8))
                        PE.done(last, ("o_fox", b))
                with pe.Fori(0, RN) as i:
                    one_round(i)

            @block.scalar
            def _(act):
                ACTS.start(act)

                def one_round(i):
                    act_compress(nc, act, i, 2, B, PE, ACTS, buf, (ch_loaded, i * 256 + 256))
                    for b in range(2):
                        back = int(b == 0)
                        other = 1 - b

                        def copy(name, dst, n=512, rows=P, free=None):
                            PE.wait(act, (name, b), i)
                            if free:
                                PE.wait(act, (free, other), i, back=back)
                            ACTS.done(nc.scalar.copy(dst, psum[0:rows, B.bank[name, b], 0:n]), ("ev", (name, b)))

                        def exponent(kind, s, at, out=None):
                            DVE.wait(act, (f"max_{kind}", b), i)
                            ACTS.done(nc.scalar.activation(s[:, :] if out is None else out, s[:, :], ACT.Exp, bias=stat[:, at:at + 1], scale=1.0,
                                                           accum_out=stat[:, at + 4:at + 5]), (f"exp_{kind}", b))

                        copy("ks0", kT_slc[:, 0:512], free="s_slc1")
                        copy("ks1", kT_slc[:, 512:1024], free="s_slc1")
                        copy("kw", kT_win[:, :], free="s_win")
                        exponent("cmp", s_cmp, 0)
                        copy("pt_imp", ptT[0:NC, 0, 0:32], n=32, rows=NC, free="imp")
                        exponent("win", s_win, 1)
                        for n in (0, 2):
                            copy(f"kf{n}", kT_fox[:, n % 4, 0:512], free="s_fox1")
                        copy("imp", imp_rows[:, :], n=16, rows=32, free="imp_sum")
                        for n in (4, 6):
                            copy(f"kf{n}", kT_fox[:, n % 4, 512:1024], free="s_fox1")
                        exponent("slc", s_slc, 2)
                        exponent("fox", s_fox, 3)
                        PE.wait(act, ("pt_cw", b), i)
                        PE.wait(act, ("o_nsa", other), i, back=back)
                        nc.scalar.copy(ptT[0:NC, 1, 0:32], psum[0:NC, B.bank["pt_cw", b], 0:32])
                        nc.scalar.copy(ptT[:, 1, 32:160], psum[:, B.bank["pt_cw", b], 32:160])
                        ACTS.done(nc.scalar.copy(ptT[0:TS, 1, 160:192], psum[0:TS, B.bank["pt_cw", b], 160:192]), ("ev", ("pt_cw", b)))
                        for name, k, user in (("pt_slc", 2, "o_nsa"), ("pt_fox", 3, "o_fox")):
                            PE.wait(act, (name, b), i)
                            PE.wait(act, (user, other), i, back=back)
                            nc.scalar.copy(ptT[:, k, 0:256], psum[:, B.bank[name, b], 0:256])
                            ACTS.done(nc.scalar.copy(ptT[0:TS, k, 256:288], psum[0:TS, B.bank[name, b], 256:288]), ("ev", (name, b)))
                with act.Fori(0, RN) as i:
                    one_round(i)

            @block.vector
            def _(dve):
                DVE.start(dve)
                dve.wait_ge(setup_loaded, 16 * 13)
                dve.wait_ge(setup_set, 2)
                nc.vector.memset(bias_c[:, 0:55], 0.0).then_inc(bias_c_set, 1)
                nc.vector.tensor_copy(bias_c[:, 55:63], bias_s[:, 15:P:16]).then_inc(bias_c_set, 1)
                dve.wait_ge(bias_c_set, 2)

                def one_round(i):
                    dve_compress(nc, dve, i, 2, B, PE, DVE, buf, (ch_loaded, i * 256 + 256),
                                 lambda e: PE.wait(e, ("s_cmp", 1), i, back=1), lambda e, b: PE.wait(e, ("o_nsa", 1), i, back=1))
                    for b in range(2):
                        back = int(b == 0)
                        other = 1 - b

                        def bk(name):
                            return psum[:, B.bank[name, b], :]

                        def step(ins, name):
                            DVE.done(ins, (name, b))

                        def after(name):
                            DVE.wait(dve, (name, b), i)

                        def ev(name):
                            return ("ev", (name, b))

                        def top(kind, s, at, last):
                            DVE.wait(dve, last, i)
                            step(nc.vector.tensor_reduce(stat[:, at:at + 1], s[:, :], AX.X, ALU.max, negate=True), f"max_{kind}")

                        PE.wait(dve, ("s_cmp", b), i)
                        PE.wait(dve, ("pt_cw", other), i, back=back)
                        DVE.done(nc.vector.tensor_tensor(s_cmp[:, :], bk("s_cmp")[0:32, 0:NC], bias_c[:, :], ALU.add), ev("s_cmp"))
                        top("cmp", s_cmp, 0, ev("s_cmp"))
                        dve.wait_ge(small_loaded[b], i * 208 + 208)
                        for half in range(2):
                            PE.wait(dve, (f"lf{half}", b), i)
                            DVE.done(nc.vector.tensor_copy(lfT[:, b, half * 512:half * 512 + 512], bk(f"lf{half}")[0:H, :]), ev(f"lf{half}"))
                        DVE.wait(dve, ev("lf1"), i)
                        PE.wait(dve, ("s_fox_new", other), i, back=back)
                        step(nc.vector.tensor_tensor_scan(ck[:, :], env["ones"][0:H, 0:1].to_broadcast([H, L]), lfT[:, b, :], 0.0, ALU.mult, ALU.add), "scan")
                        PE.wait(dve, ("s_win", b), i)
                        w = bk("s_win")
                        nc.vector.tensor_tensor(s_win[:, 0:TS], w[0:32, 0:TS], mask_new[:, TS:2 * TS], ALU.add)
                        nc.vector.tensor_copy(s_win[:, TS:WIN - P], w[0:32, TS:WIN - P])
                        DVE.done(nc.vector.tensor_tensor(s_win[:, WIN - P:WIN], w[0:32, WIN - P:WIN], bias_s[:, 0:P], ALU.add), ev("s_win"))
                        PE.wait(dve, ("s_win_new", b), i)
                        DVE.done(nc.vector.tensor_tensor(s_win[:, WIN:WIN + TS], bk("s_win_new")[0:32, 0:TS], bias_s[:, P:P + TS], ALU.add), ev("s_win_new"))
                        top("win", s_win, 1, ev("s_win_new"))
                        PE.wait(dve, ("s_slc0", b), i)
                        PE.wait(dve, ("pt_slc", other), i, back=back)
                        DVE.done(nc.vector.tensor_copy(s_slc[:, 0:512], bk("s_slc0")[0:32, :]), ev("s_slc0"))
                        PE.wait(dve, ("s_slc1", b), i)
                        w = bk("s_slc1")
                        nc.vector.tensor_copy(s_slc[:, 512:PAST - P], w[0:32, 0:512 - P])
                        DVE.done(nc.vector.tensor_tensor(s_slc[:, PAST - P:PAST], w[0:32, 512 - P:512], bias_s[:, 0:P], ALU.add), ev("s_slc1"))
                        PE.wait(dve, ("s_slc_new", b), i)
                        DVE.done(nc.vector.tensor_tensor(s_slc[:, PAST:L], bk("s_slc_new")[0:32, 0:TS], bias_s[:, P:P + TS], ALU.add), ev("s_slc_new"))
                        ACTS.wait(dve, ("exp_cmp", b), i)
                        step(nc.vector.reciprocal(stat[:, 8:9], stat[:, 4:5]), "rec_cmp")
                        after("rec_cmp")
                        step(nc.vector.tensor_scalar(p_imp[:, :], s_cmp[:, :], stat[:, 8:9], None, ALU.mult), "norm_cmp")
                        after("norm_cmp")
                        step(nc.vector.tensor_scalar(s_cmp[:, :], p_imp[:, :], gates[:, b, 0:1], None, ALU.mult), "gate_cmp")

                        def weigh(kind, s, at, br, fac, gate):
                            ACTS.wait(dve, (f"exp_{kind}", b), i)
                            step(nc.vector.reciprocal(stat[:, at + 8:at + 9], stat[:, at + 4:at + 5]), f"rec_{kind}")
                            after(f"rec_{kind}")
                            if fac:
                                step(nc.vector.tensor_tensor(stat[:, at + 8:at + 9], stat[:, at + 8:at + 9], gates[:, b, br:br + 1], ALU.mult), fac)
                                after(fac)
                            step(nc.vector.tensor_scalar(s[:, :], s[:, :], stat[:, at + 8:at + 9], None, ALU.mult), gate)

                        weigh("win", s_win, 1, 2, "fac_win", "gate_win")

                        def keys(n):
                            half, p = n // 4, n % 4
                            PE.wait(dve, (f"kf{n}", b), i)
                            PE.wait(dve, ("s_fox1", other), i, back=back)
                            DVE.done(nc.vector.tensor_copy(kT_fox[:, p, half * 512:half * 512 + 512], bk(f"kf{n}")), ev(f"kf{n}"))
                        for n in (1, 3, 5, 7):
                            keys(n)
                        PE.wait(dve, ("imp_sum", b), i)
                        cand = choice[:, 0, 0:14]
                        DVE.done(nc.vector.tensor_copy(cand, bk("imp_sum")[0:32, 1:15]), ev("imp_sum"))
                        DVE.wait(dve, ev("imp_sum"), i)
                        step(nc.vector.tensor_reduce(stat[:, 12:13], cand, AX.X, ALU.min), "least")
                        after("least")
                        step(nc.vector.scalar_tensor_tensor(out=choice[:, 1, 0:14], in0=cand, scalar=stat[:, 12:13], in1=iota[:, 1:15],
                                                            op0=ALU.is_equal, op1=ALU.mult), "which")
                        after("which")
                        step(nc.vector.tensor_reduce(stat[:, 13:14], choice[:, 1, 0:14], AX.X, ALU.max), "last")
                        after("last")
                        step(nc.vector.tensor_scalar(choice[:, 2, 0:14], iota[:, 1:15], stat[:, 13:14], NEG, ALU.is_equal, ALU.mult), "drop")
                        after("drop")
                        part = s_slc[:, 64:960].rearrange("p (j n) -> p j n", n=64)
                        step(nc.vector.tensor_tensor(part, part, choice[:, 2, 0:14].unsqueeze(2).to_broadcast([32, 14, 64]), ALU.add), "mask")
                        top("slc", s_slc, 2, ("mask", b))
                        PE.wait(dve, ("s_fox0", b), i)
                        PE.wait(dve, ("pt_fox", other), i, back=back)
                        DVE.done(nc.vector.tensor_copy(s_fox[:, 0:512], bk("s_fox0")[0:32, :]), ev("s_fox0"))
                        PE.wait(dve, ("s_fox1", b), i)
                        DVE.done(nc.vector.tensor_copy(s_fox[:, 512:1024], bk("s_fox1")[0:32, :]), ev("s_fox1"))
                        PE.wait(dve, ("s_fox_new", b), i)
                        DVE.done(nc.vector.tensor_tensor(s_fox[:, PAST:L], bk("s_fox_new")[0:32, 0:TS], mask_new[:, 0:TS], ALU.add), ev("s_fox_new"))
                        top("fox", s_fox, 3, ev("s_fox_new"))
                        weigh("slc", s_slc, 2, 1, "fac_slc", "gate_slc")
                        weigh("fox", s_fox, 3, None, None, "gate_fox")
                        dve.wait_ge(so_free[b], i + 1)
                        PE.wait(dve, ("o_nsa", b), i)
                        DVE.done(nc.vector.tensor_copy(o_nsa[:, b, :], bk("o_nsa")[:, 0:32]), ev("o_nsa"))
                        PE.wait(dve, ("o_fox", b), i)
                        DVE.done(nc.vector.tensor_copy(o_fox[:, b, 0:P], bk("o_fox")[:, 0:P]), ev("o_fox"))
                with dve.Fori(0, RN) as i:
                    one_round(i)


def attention_units():
    units = []
    for i in range(QT):
        units += [("cmp", i, 0, 0), ("slc", i, 0, i), ("win", i, max(0, i - WIN // P), i)]
    units += [("fox", i, 0, i) for i in range(QT)]
    return units


UNITS = attention_units()
NU = len(UNITS)
LAG = 1


def unit_groups(u):
    kind, i, lo, hi = UNITS[u]
    tiles = list(range(lo, hi + 1))
    return [tiles[n:n + 4] for n in range(0, len(tiles), 4)]


GROUPS = [(u, n) for u in range(NU) for n in range(len(unit_groups(u)))]
GROUP_NO = {g: n for n, g in enumerate(GROUPS)}
NG = len(GROUPS)
assert NG % 4 == 0 and NU % 4 == 0


def last_of_output(u):
    return UNITS[u][0] in ("win", "fox")


def output_no(u):
    return UNITS[u][1] + (QT if UNITS[u][0] == "fox" else 0)


def pe_order():
    names = []
    for step in range(-2, NU + LAG + 1):
        if 0 <= step + 2 < NU:
            names.append(("S", step + 2))
        if 0 <= step - LAG < NU:
            names += [("T", step - LAG, n) for n in range(len(unit_groups(step - LAG)))]
        if 0 <= step - LAG - 1 < NU:
            names += [("PV", step - LAG - 1, n) for n in range(len(unit_groups(step - LAG - 1)))]
    return names


def act_order():
    names = []
    for step in range(NU + 2 + LAG):
        if step < NU:
            names.append(("exp", step))
        if 0 <= step - 2 - LAG:
            names += [("pt", step - 2 - LAG, n) for n in range(len(unit_groups(step - 2 - LAG)))]
    return names


def dve_order():
    names = []
    for step in range(NU + 3 + LAG):
        if step < NU:
            kind, i, lo, hi = UNITS[step]
            names.append(("bias", step))
            if kind == "win" and i - lo == WIN // P:
                names.append(("band", step))
            names.append(("max", step))
            if kind == "cmp":
                names.append(("guard", step))
        if 0 <= step - 1 < NU:
            if UNITS[step - 1][0] == "cmp":
                names.append(("dguard", step - 1))
            names.append(("recip", step - 1))
            if UNITS[step - 1][0] != "fox":
                names.append(("gate", step - 1))
        if 0 <= step - 3 - LAG and last_of_output(step - 3 - LAG):
            names.append(("out", output_no(step - 3 - LAG)))
    return names


def gate_step(u):
    return ("gate", u) if UNITS[u][0] != "fox" else ("recip", u)


def max_step(u):
    return ("guard", u) if UNITS[u][0] == "cmp" else ("max", u)


def build_c(nc, a, o, c, env):
    (y_prompt, y_sample, nsa_kv_prompt, fox_kv_prompt, logf_prompt, win_kv_prompt,
     nsa_kv_sample, fox_kv_sample, logf_sample, win_kv_sample) = o
    ident, gf_nat, psum = (env[k] for k in ("ident", "gf_nat", "psum"))
    zT, vw_nat, negck, oT_dram, bias_tab, kc_dram, vc_dram = (env[k] for k in ("zT", "vw_nat", "negck", "oT_dram", "bias_tab", "kc_dram", "vc_dram"))
    sem = env["sem"]
    rows = zT.rearrange("n p t -> (n p) t")
    ctx = ExitStack()
    with ctx:
        def sb(name, shape, dt=F32):
            return ctx.enter_context(nc.sbuf_tensor(name, shape, dt))

        bias = sb("bias", [P, H, 2 * P])
        bias_cmp = sb("bias_cmp", [P, H, 119])
        causal = sb("causal", [P, P])
        band = sb("band", [P, P])
        q_nsa = sb("q_nsa", [DH, T])
        k_slc = sb("k_slc", [DH, T])
        k_win = sb("k_win", [DH, T])
        v_slc = sb("v_slc", [P, QT, DH])
        v_win = sb("v_win", [P, QT, DH])
        k_cmp = sb("k_cmp", [DH, NC])
        v_cmp = sb("v_cmp", [NC, DH])
        q_fox = sb("q_fox", [DH + 1, T])
        k_fox = sb("k_fox", [DH + 1, T])
        v_fox = sb("v_fox", [P, QT, DH])
        probs = sb("probs", [P, 4, T])
        probsT = sb("probsT", [P, 4, 512])
        neg_max = sb("neg_max", [P, 4])
        denom = sb("denom", [P, 4])
        factor = sb("factor", [P, 4])
        o_nsa = sb("o_nsa", [DH, T])
        o_fox = sb("o_fox", [DH, T])
        scores = [psum[:, 2 * b:2 * b + 2, :].rearrange("p b n -> p (b n)") for b in range(2)]
        turns = [psum[:, 4 + b, :] for b in range(2)]
        outs = [psum[:, 6 + b, :] for b in range(2)]

        PE = Steps(sem("c_pe"), pe_order(), H)
        ACTS = Steps(sem("c_act"), act_order(), H)
        DVE = Steps(sem("c_dve"), dve_order(), H)
        POOL = Steps(sem("c_pool"), [("scale", u) for u in range(NU)], H)
        tables_loaded = sem("c_tables_loaded")
        bias_cmp_set = sem("bias_cmp_set")
        ones_row_set = sem("ones_row_set")
        nsa_loaded = sem("nsa_loaded")
        fox_loaded = sem("fox_loaded")
        o_stored = [sem("o_nsa_stored"), sem("o_fox_stored")]
        block = ctx.enter_context(nc.Block())

        LAST_NSA = NU - QT - 1

        @block.sync
        def _(sp):
            for s in o_stored:
                sp.sem_inc(s, 16)
            flat = bias_tab.rearrange("h q x -> h (q x)")[:, 127:127 + P * 383].rearrange("h (q x) -> q h x", x=383)
            sp.dma_start(bias[:, :, :], flat[:, :, 0:2 * P]).then_inc(tables_loaded, 16)
            sp.dma_start(causal[:, :], c["causal"]).then_inc(tables_loaded, 16)
            sp.dma_start(band[:, :], c["band"]).then_inc(tables_loaded, 16)

            def load_nsa(h):
                g = h // R
                for dst, src in (
                        (q_nsa, rows[bass.ds(h * DH + TILE["q_n"] * P, DH), 0:T]),
                        (k_slc, rows[bass.ds(g * DH + (TILE["nsa_kv"] + 2) * P, DH), 0:T]),
                        (k_win, rows[bass.ds(g * DH + TILE["win_kv"] * P, DH), 0:T]),
                        (k_cmp, kc_dram[bass.ds(g * DH, DH), :])):
                    sp.dma_start(dst[:, :], src).then_inc(nsa_loaded, 16)
                sp.dma_start(v_slc[:, :, :], nsa_kv_prompt[0, 0].rearrange("(t p) a g d -> p t (a g d)", p=P)[:, :, bass.ds(g * DH + 6 * DH, DH)]).then_inc(nsa_loaded, 16)
                sp.dma_start(v_win[:, :, :], vw_nat.rearrange("(t p) d -> p t d", p=P)[:, :, bass.ds(g * DH, DH)]).then_inc(nsa_loaded, 16)
                sp.dma_start(v_cmp[:, :], vc_dram[:, bass.ds(g * DH, DH)]).then_inc(nsa_loaded, 16)

            def load_fox(h):
                sp.dma_start(q_fox[0:DH, :], rows[bass.ds(h * DH + TILE["q_f"] * P, DH), 0:T]).then_inc(fox_loaded, 16)
                sp.dma_start(k_fox[0:DH, :], rows[bass.ds(h * DH + TILE["fox_kv"] * P, DH), 0:T]).then_inc(fox_loaded, 16)
                sp.dma_start(k_fox[DH:DH + 1, :], negck[bass.ds(h, 1), :]).then_inc(fox_loaded, 16)
                sp.dma_start(v_fox[:, :, :], fox_kv_prompt[0, 0].rearrange("(t p) a h d -> p t (a h d)", p=P)[:, :, bass.ds(h * DH + H * DH, DH)]).then_inc(fox_loaded, 16)

            load_nsa(0)

            def one_round(h, last):
                PE.wait(sp, ("PV", NU - 1, 1), h, back=1)
                load_fox(h)
                DVE.wait(sp, ("out", QT - 1), h)
                sp.dma_start(oT_dram[bass.ds(h * DH, DH), 0:T], o_nsa[:, :]).then_inc(o_stored[0], 16)
                if not last:
                    PE.wait(sp, ("PV", LAST_NSA, 1), h)
                    load_nsa(h + 1)
                DVE.wait(sp, ("out", 2 * QT - 1), h)
                sp.dma_start(oT_dram[bass.ds(h * DH + H * DH, DH), 0:T], o_fox[:, :]).then_inc(o_stored[1], 16)

            with sp.Fori(0, H - 1) as h:
                one_round(h, False)
            one_round(H - 1, True)
            for s in o_stored:
                sp.wait_ge(s, 16 + 16 * H)

        @block.tensor
        def _(pe):
            PE.start(pe)
            pe.wait_ge(ones_row_set, 1)

            def one_round(h):
                def scores_of(u):
                    kind, i, lo, hi = UNITS[u]
                    if u == 0:
                        pe.wait_ge(nsa_loaded, h * 112 + 112)
                    if kind == "fox" and i == 0:
                        pe.wait_ge(fox_loaded, h * 64 + 64)
                    ACTS.wait(pe, ("exp", (u - 2) % NU), h, back=int(u < 2))
                    q = (q_fox if kind == "fox" else q_nsa)[:, i * P:(i + 1) * P]
                    k = {"cmp": k_cmp, "slc": k_slc, "win": k_win, "fox": k_fox}[kind]
                    first, n = lo * P, (hi - lo + 1) * P if kind != "cmp" else NC
                    for at in range(0, n, 512):
                        w = min(512, n - at)
                        last = nc.tensor.matmul(scores[u % 2][:, at:at + w], q, k[:, first + at:first + at + w], start=True, stop=True)
                    PE.done(last, ("S", u))

                def turn(u):
                    POOL.wait(pe, ("scale", u), h)
                    for n, tiles in enumerate(unit_groups(u)):
                        g = GROUP_NO[u, n]
                        before = GROUPS[(g - 2) % NG]
                        ACTS.wait(pe, ("pt", *before), h, back=int(g < 2))
                        if UNITS[u][0] == "cmp":
                            apart(pe)
                        for j, t in enumerate(tiles):
                            w = NC if UNITS[u][0] == "cmp" else P
                            at = (t - UNITS[u][2]) * P
                            last = nc.tensor.transpose(turns[g % 2][0:w, j * P:(j + 1) * P], probs[:, u % 4, at:at + w], ident[:, :])
                        PE.done(last, ("T", u, n))

                def values(u):
                    kind, i, lo, hi = UNITS[u]
                    out = output_no(u)
                    if kind in ("cmp", "fox"):
                        DVE.wait(pe, ("out", (out - 2) % (2 * QT)), h, back=int(out < 2))
                    v = {"cmp": v_cmp, "slc": v_slc, "win": v_win, "fox": v_fox}[kind]
                    for n, tiles in enumerate(unit_groups(u)):
                        g = GROUP_NO[u, n]
                        ACTS.wait(pe, ("pt", u, n), h)
                        if kind == "cmp":
                            apart(pe)
                        for j, t in enumerate(tiles):
                            if kind == "cmp":
                                lhs, rhs = v[:, :], probsT[0:NC, g % 4, 0:P]
                            else:
                                lhs, rhs = v[:, t, :], probsT[:, g % 4, j * P:(j + 1) * P]
                            last = nc.tensor.matmul(outs[out % 2][0:DH, 0:P], lhs, rhs, start=(kind in ("cmp", "fox") and t == lo),
                                                    stop=(last_of_output(u) and t == hi))
                        PE.done(last, ("PV", u, n))

                for step in range(-2, NU + LAG + 1):
                    if 0 <= step + 2 < NU:
                        scores_of(step + 2)
                    if 0 <= step - LAG < NU:
                        turn(step - LAG)
                    if 0 <= step - LAG - 1 < NU:
                        values(step - LAG - 1)
            with pe.Fori(0, H) as h:
                one_round(h)

        @block.scalar
        def _(act):
            ACTS.start(act)

            def one_round(h):
                for step in range(NU + 2 + LAG):
                    if step < NU:
                        u = step
                        kind, i, lo, hi = UNITS[u]
                        n = (hi - lo + 1) * P if kind != "cmp" else NC
                        DVE.wait(act, max_step(u), h)
                        old = (u - 4) % NU
                        PE.wait(act, ("T", old, len(unit_groups(old)) - 1), h, back=int(u < 4))
                        ACTS.done(nc.scalar.activation(probs[:, u % 4, 0:n], scores[u % 2][:, 0:n], ACT.Exp, bias=neg_max[:, u % 4:u % 4 + 1],
                                                       scale=1.0, accum_out=denom[:, u % 4:u % 4 + 1]), ("exp", u))
                    if step >= 2 + LAG:
                        u = step - 2 - LAG
                        for n, tiles in enumerate(unit_groups(u)):
                            g = GROUP_NO[u, n]
                            PE.wait(act, ("T", u, n), h)
                            PE.wait(act, ("PV", *GROUPS[(g - 4) % NG]), h, back=int(g < 4))
                            w = NC if UNITS[u][0] == "cmp" else P
                            ACTS.done(nc.scalar.copy(probsT[0:w, g % 4, 0:len(tiles) * P], turns[g % 2][0:w, 0:len(tiles) * P]), ("pt", u, n))
            with act.Fori(0, H) as h:
                one_round(h)

        @block.gpsimd
        def _(pool):
            pool.memset(q_fox[DH:DH + 1, :], 1.0).then_inc(ones_row_set, 1)
            POOL.start(pool)

            def one_round(h):
                for u in range(NU):
                    kind, i, lo, hi = UNITS[u]
                    n = (hi - lo + 1) * P if kind != "cmp" else NC
                    DVE.wait(pool, gate_step(u), h)
                    apart(pool)
                    POOL.done(nc.gpsimd.tensor_scalar(probs[:, u % 4, 0:n], probs[:, u % 4, 0:n], factor[:, u % 4:u % 4 + 1], None, ALU.mult),
                              ("scale", u))
            with pool.Fori(0, H) as h:
                one_round(h)

        @block.vector
        def _(dve):
            DVE.start(dve)
            dve.wait_ge(tables_loaded, 48)
            nc.vector.memset(bias_cmp[:, :, 0:47], 0.0).then_inc(bias_cmp_set, 1)
            nc.vector.memset(bias_cmp[:, :, 63:119], NEG).then_inc(bias_cmp_set, 1)
            nc.vector.tensor_copy(bias_cmp[:, :, 47:63], bias[:, :, 15::16]).then_inc(bias_cmp_set, 1)
            dve.wait_ge(bias_cmp_set, 3)

            def one_round(h):
                def shift(u):
                    kind, i, lo, hi = UNITS[u]
                    s = scores[u % 2]
                    PE.wait(dve, ("S", u), h)
                    if kind == "cmp":
                        at, n, add = 0, NC, bias_cmp[:, bass.ds(h, 1), 56 - 8 * i:56 - 8 * i + NC]
                    elif kind == "fox":
                        at, n, add = i * P, P, causal[:, :]
                    elif i == 0:
                        at, n, add = 0, P, bias[:, bass.ds(h, 1), P:2 * P]
                    else:
                        at, n, add = (i - 1 - lo) * P, 2 * P, bias[:, bass.ds(h, 1), :]
                    if kind != "fox":
                        add = add.rearrange("p o n -> p (o n)")
                    DVE.done(nc.vector.tensor_tensor(s[:, at:at + n], s[:, at:at + n], add, ALU.add), ("bias", u))
                    if kind == "win" and i - lo == WIN // P:
                        DVE.done(nc.vector.tensor_tensor(s[:, 0:P], s[:, 0:P], band[:, :], ALU.add), ("band", u))
                        DVE.wait(dve, ("band", u), h)
                    DVE.wait(dve, ("bias", u), h)
                    n = (hi - lo + 1) * P if kind != "cmp" else NC
                    m = neg_max[:, u % 4:u % 4 + 1]
                    DVE.done(nc.vector.tensor_reduce(m, s[:, 0:n], AX.X, ALU.max, negate=True), ("max", u))
                    if kind == "cmp":
                        DVE.wait(dve, ("max", u), h)
                        DVE.done(nc.vector.tensor_scalar(m, m, -0.1 * NEG, None, ALU.min), ("guard", u))

                def weigh(u):
                    kind, i, lo, hi = UNITS[u]
                    ACTS.wait(dve, ("exp", u), h)
                    POOL.wait(dve, ("scale", (u - 4) % NU), h, back=int(u < 4))
                    d, f = denom[:, u % 4:u % 4 + 1], factor[:, u % 4:u % 4 + 1]
                    if kind == "cmp":
                        DVE.done(nc.vector.tensor_scalar(d, d, 1e-30, None, ALU.max), ("dguard", u))
                        DVE.wait(dve, ("dguard", u), h)
                    DVE.done(nc.vector.reciprocal(f, d), ("recip", u))
                    if kind != "fox":
                        br = ("cmp", "slc", "win").index(kind)
                        DVE.wait(dve, ("recip", u), h)
                        DVE.done(nc.vector.tensor_tensor(f, f, gf_nat[:, i, bass.ds(h + (GATE0 + br * H), 1)], ALU.mult), ("gate", u))

                for step in range(NU + 3 + LAG):
                    if step < NU:
                        shift(step)
                    if 0 <= step - 1 < NU:
                        weigh(step - 1)
                    if 0 <= step - 3 - LAG and last_of_output(step - 3 - LAG):
                        u = step - 3 - LAG
                        out = output_no(u)
                        i = UNITS[u][1]
                        PE.wait(dve, ("PV", u, len(unit_groups(u)) - 1), h)
                        if i == 0:
                            dve.wait_ge(o_stored[out // QT], h * 16 + 16)
                        dst = (o_nsa if out < QT else o_fox)[:, i * P:(i + 1) * P]
                        DVE.done(nc.vector.tensor_copy(dst, outs[out % 2][0:DH, 0:P]), ("out", out))
            with dve.Fori(0, H) as h:
                one_round(h)


class RmsNorm:

    def __init__(self, env, prefix, n, banks):
        s = env["sem"]
        self.nc, self.env, self.n, self.banks = env["nc"], env, n, banks
        self.squared, self.summed, self.total = s(prefix + "_squared"), s(prefix + "_summed"), s(prefix + "_total")
        self.rooted, self.inverted = s(prefix + "_rooted"), s(prefix + "_inverted")

    def act(self, act, src, ready, sq, rstd, free=None):
        nc = self.nc
        for k in range(self.n):
            ready(act, k)
            if k >= 2:
                act.wait_ge(self.summed, k - 1)
            nc.scalar.activation(sq[:, k % 2, :], src(k), ACT.Square).then_inc(self.squared, 1)
        act.wait_ge(self.total, 1)
        if free:
            free(act)
        for b in range(3):
            last = nc.scalar.activation(rstd[:, b * NB:(b + 1) * NB], self.env["psum"][:, self.banks + b, 0:NB], ACT.Sqrt,
                                        bias=self.env["eps"][:, 0:1], scale=1.0 / (self.n * P))
        last.then_inc(self.rooted, 1)

    def dve(self, dve, sq, ssum, rstd):
        nc = self.nc
        for k in range(self.n):
            dve.wait_ge(self.squared, k + 1)
            if k == 0:
                nc.vector.tensor_copy(ssum[:, :], sq[:, 0, :]).then_inc(self.summed, 1)
            else:
                dve.wait_ge(self.summed, k)
                nc.vector.tensor_tensor(ssum[:, :], ssum[:, :], sq[:, k % 2, :], ALU.add).then_inc(self.summed, 1)
        dve.wait_ge(self.rooted, 1)
        nc.vector.reciprocal(rstd[:, :], rstd[:, :]).then_inc(self.inverted, 1)
        dve.wait_ge(self.inverted, 1)

    def pe(self, pe, ssum):
        nc = self.nc
        pe.wait_ge(self.summed, self.n)
        for b in range(3):
            last = nc.tensor.matmul(self.env["psum"][:, self.banks + b, 0:NB], self.env["ones"][:, :], ssum[:, b * NB:(b + 1) * NB],
                                    start=True, stop=True)
        last.then_inc(self.total, 1)


def build_d(nc, a, env, hfT):
    xT, gains, psum, sem, oT_dram = (env[k] for k in ("xT", "gains", "psum", "sem", "oT_dram"))
    ctx = ExitStack()
    with ctx:
        def sb(name, shape, dt=F32):
            return ctx.enter_context(nc.sbuf_tensor(name, shape, dt))

        mixT = sb("mixT", [P, KD, N])
        yT = sb("d_yT", [P, KD, N])
        sq = sb("d_sq", [P, 2, N])
        ssum = sb("d_ssum", [P, N])
        ssum2 = sb("d_ssum2", [P, N])
        rstd = sb("d_rstd", [P, 2, N])
        w_ring = sb("d_w_ring", [P, 2, KD, P])
        mix_loaded = [sem(f"d_mix_loaded{k}") for k in range(KD)]
        w_loaded = [sem(f"d_w_loaded{s}") for s in range(2)]
        mix_normed, y_done, y_copied = sem("d_mix_normed"), sem("d_y_done"), sem("d_y_copied")
        x_scaled, x_added, hf_ready = sem("d_x_scaled"), sem("d_x_added"), sem("d_hf_ready")
        norm_n, norm_f = RmsNorm(env, "d_norm_n", 4, 0), RmsNorm(env, "d_norm_f", 4, 3)
        norm_y, norm_x = RmsNorm(env, "d_norm_y", KD, 0), RmsNorm(env, "d_norm_x", KD, 3)
        W = a["w_o"][0].rearrange("(k p) n -> p k n", p=P)
        with nc.Block() as block:
            @block.sync
            def _(sp):
                for k in range(KD):
                    sp.dma_start(mixT[:, k, :], oT_dram[k * P:(k + 1) * P, :]).then_inc(mix_loaded[k], 16)
                with sp.Fori(0, KD // 2) as i:
                    for s in range(2):
                        sp.wait_ge(y_done, i * 2 + (s + 1))
                        sp.dma_start(w_ring[:, s], W[:, :, bass.ds(i * 256 + s * P, P)]).then_inc(w_loaded[s], 16)

            @block.tensor
            def _(pe):
                pe.sem_inc(y_done, 2)
                norm_n.pe(pe, ssum)
                norm_f.pe(pe, ssum2)
                pe.wait_ge(mix_normed, KD)
                with pe.Fori(0, KD // 2) as i:
                    for s in range(2):
                        pe.wait_ge(w_loaded[s], i * 16 + 16)
                        pe.wait_ge(y_copied, i * 2 + (s + 1))
                        for b in range(3):
                            for k in range(KD):
                                last = nc.tensor.matmul(psum[:, 3 * s + b, 0:NB], w_ring[:, s, k, :], mixT[:, k, b * NB:(b + 1) * NB],
                                                        start=(k == 0), stop=(k == KD - 1))
                        last.then_inc(y_done, 1)
                norm_y.pe(pe, ssum)
                norm_x.pe(pe, ssum2)

            @block.scalar
            def _(act):
                norm_n.act(act, lambda k: mixT[:, k, :], lambda e, k: e.wait_ge(mix_loaded[k], 16), sq, rstd[:, 0, :])
                norm_f.act(act, lambda k: mixT[:, 4 + k, :],
                           lambda e, k: (e.wait_ge(mix_loaded[4 + k], 16), k < 2 and e.wait_ge(norm_n.summed, k + 3)), sq, rstd[:, 1, :])
                act.sem_inc(y_copied, 2)
                with act.Fori(0, KD // 2) as i:
                    for s in range(2):
                        act.wait_ge(y_done, i * 2 + (s + 3))
                        for b in range(3):
                            last = nc.scalar.copy(yT[:, bass.ds(i * 2 + s, 1), b * NB:(b + 1) * NB].rearrange("p o n -> p (o n)"),
                                                  psum[:, 3 * s + b, 0:NB])
                        last.then_inc(y_copied, 1)
                norm_y.act(act, lambda k: yT[:, k, :],
                           lambda e, k: (k == 0 and e.wait_ge(y_copied, KD + 2), k < 2 and e.wait_ge(norm_f.summed, k + 3)), sq, rstd[:, 0, :],
                           free=lambda e: e.wait_ge(mix_normed, KD))
                norm_x.act(act, lambda k: xT[:, k, :],
                           lambda e, k: (e.wait_ge(x_added, k + 1), k < 2 and e.wait_ge(norm_y.summed, KD - 1 + k)), sq, rstd[:, 1, :])

            @block.vector
            def _(dve):
                norm_n.dve(dve, sq, ssum, rstd[:, 0, :])
                norm_f.dve(dve, sq, ssum2, rstd[:, 1, :])
                for k in range(KD):
                    nc.vector.scalar_tensor_tensor(out=mixT[:, k, :], in0=mixT[:, k, :], scalar=gains[:, 4, k:k + 1], in1=rstd[:, k // 4, :],
                                                   op0=ALU.mult, op1=ALU.mult).then_inc(mix_normed, 1)
                norm_y.dve(dve, sq, ssum, rstd[:, 0, :])
                for k in range(KD):
                    nc.vector.scalar_tensor_tensor(out=yT[:, k, :], in0=yT[:, k, :], scalar=gains[:, 1, k:k + 1], in1=rstd[:, 0, :],
                                                   op0=ALU.mult, op1=ALU.mult).then_inc(x_scaled, 1)
                for k in range(KD):
                    dve.wait_ge(x_scaled, k + 1)
                    nc.vector.tensor_tensor(xT[:, k, :], xT[:, k, :], yT[:, k, :], ALU.add).then_inc(x_added, 1)
                norm_x.dve(dve, sq, ssum2, rstd[:, 1, :])
                for k in range(KD):
                    nc.vector.scalar_tensor_tensor(out=hfT[:, k, :], in0=xT[:, k, :], scalar=gains[:, 2, k:k + 1], in1=rstd[:, 1, :],
                                                   op0=ALU.mult, op1=ALU.mult).then_inc(hf_ready, 1)
                dve.wait_ge(hf_ready, KD)


def build_e(nc, a, env, hfT):
    psum, sem = env["psum"], env["sem"]
    ctx = ExitStack()
    with ctx:
        def sb(name, shape, dt=F32):
            return ctx.enter_context(nc.sbuf_tensor(name, shape, dt))

        hT = sb("hT", [P, FT, N])
        silu = sb("silu", [P, N])
        gate_ring = sb("gate_ring", [P, 2, KD, P])
        up_ring = sb("up_ring", [P, 2, KD, P])
        down_ring = sb("down_ring", [P, 2, FT, P])
        gate_loaded = [sem(f"e_gate_loaded{s}") for s in range(2)]
        up_loaded = [sem(f"e_up_loaded{s}") for s in range(2)]
        down_loaded = [sem(f"e_down_loaded{s}") for s in range(2)]
        gate_done, up_done, silu_ready, h_ready = sem("e_gate_done"), sem("e_up_done"), sem("e_silu_ready"), sem("e_h_ready")
        y_done, y_copied = sem("e_y_done"), sem("e_y_copied")
        WG, WU, WD = (a[n][0].rearrange("(k p) n -> p k n", p=P) for n in ("w_ffn_gate", "w_ffn_up", "w_ffn_down"))
        with nc.Block() as block:
            @block.sync
            def _(sp):
                with sp.Fori(0, FT // 2) as i:
                    for s in range(2):
                        cols = bass.ds(i * 256 + s * P, P)
                        sp.wait_ge(gate_done, i * 2 + (s + 1))
                        sp.dma_start(gate_ring[:, s], WG[:, :, cols]).then_inc(gate_loaded[s], 16)
                        sp.wait_ge(up_done, i * 2 + (s + 1))
                        sp.dma_start(up_ring[:, s], WU[:, :, cols]).then_inc(up_loaded[s], 16)
                with sp.Fori(0, KD // 2) as i:
                    for s in range(2):
                        sp.wait_ge(y_done, i * 2 + (s + 1))
                        sp.dma_start(down_ring[:, s], WD[:, :, bass.ds(i * 256 + s * P, P)]).then_inc(down_loaded[s], 16)

            @block.tensor
            def _(pe):
                pe.sem_inc(gate_done, 2)
                pe.sem_inc(up_done, 2)
                pe.sem_inc(y_done, 2)
                with pe.Fori(0, FT // 2) as i:
                    for s in range(2):
                        f = i * 2 + s
                        for banks, ring, loaded, free, done in ((0, gate_ring, gate_loaded, silu_ready, gate_done),
                                                                (3, up_ring, up_loaded, h_ready, up_done)):
                            pe.wait_ge(loaded[s], i * 16 + 16)
                            pe.wait_ge(free, f + 1)
                            for b in range(3):
                                for k in range(KD):
                                    last = nc.tensor.matmul(psum[:, banks + b, 0:NB], ring[:, s, k, :], hfT[:, k, b * NB:(b + 1) * NB],
                                                            start=(k == 0), stop=(k == KD - 1))
                            last.then_inc(done, 1)
                pe.wait_ge(h_ready, FT + 1)
                with pe.Fori(0, KD // 2) as i:
                    for s in range(2):
                        pe.wait_ge(down_loaded[s], i * 16 + 16)
                        pe.wait_ge(y_copied, i * 2 + (s + 1))
                        for b in range(3):
                            for f in range(FT):
                                last = nc.tensor.matmul(psum[:, 3 * s + b, 0:NB], down_ring[:, s, f, :], hT[:, f, b * NB:(b + 1) * NB],
                                                        start=(f == 0), stop=(f == FT - 1))
                        last.then_inc(y_done, 1)

            @block.scalar
            def _(act):
                act.sem_inc(silu_ready, 1)
                act.sem_inc(y_copied, 2)
                with act.Fori(0, FT // 2) as i:
                    for s in range(2):
                        f = i * 2 + s
                        act.wait_ge(gate_done, f + 3)
                        act.wait_ge(h_ready, f + 1)
                        for b in range(3):
                            last = nc.scalar.activation(silu[:, b * NB:(b + 1) * NB], psum[:, b, 0:NB], ACT.Silu)
                        last.then_inc(silu_ready, 1)
                act.wait_ge(up_done, FT + 2)
                with act.Fori(0, KD // 2) as i:
                    for s in range(2):
                        act.wait_ge(y_done, i * 2 + (s + 3))
                        for b in range(3):
                            last = nc.scalar.copy(hfT[:, bass.ds(i * 2 + s, 1), b * NB:(b + 1) * NB].rearrange("p o n -> p (o n)"),
                                                  psum[:, 3 * s + b, 0:NB])
                        last.then_inc(y_copied, 1)
                act.wait_ge(y_copied, KD + 2)

            @block.vector
            def _(dve):
                dve.sem_inc(h_ready, 1)
                with dve.Fori(0, FT // 2) as i:
                    for s in range(2):
                        f = i * 2 + s
                        dve.wait_ge(up_done, f + 3)
                        dve.wait_ge(silu_ready, f + 2)
                        for b in range(3):
                            last = nc.vector.tensor_tensor(hT[:, bass.ds(f, 1), b * NB:(b + 1) * NB].rearrange("p o n -> p (o n)"),
                                                           psum[:, 3 + b, 0:NB], silu[:, b * NB:(b + 1) * NB], ALU.mult)
                        last.then_inc(h_ready, 1)


def build_f(nc, a, o, env, yT):
    xT, gains, psum, sem, ident = (env[k] for k in ("xT", "gains", "psum", "sem", "ident"))
    y_prompt, y_sample = o[0], o[1]
    ctx = ExitStack()
    with ctx:
        def sb(name, shape, dt=F32):
            return ctx.enter_context(nc.sbuf_tensor(name, shape, dt))

        sq = sb("f_sq", [P, 2, N])
        ssum = sb("f_ssum", [P, N])
        rstd = sb("f_rstd", [P, N])
        y_nat = sb("y_nat", [P, QT + 1, D])
        norm = RmsNorm(env, "f_norm", KD, 0)
        scaled, added, turned, copied, stored = (sem("f_" + n) for n in ("scaled", "added", "turned", "copied", "stored"))
        with nc.Block() as block:
            @block.sync
            def _(sp):
                for t in range(QT + 1):
                    sp.wait_ge(copied, 2 * t + 2)
                    if t < QT:
                        sp.dma_start(y_prompt[0, t * P:(t + 1) * P, :], y_nat[:, t, :]).then_inc(stored, 16)
                    else:
                        sp.dma_start(y_sample.rearrange("s t d -> (s t) d"), y_nat[0:S, t, :]).then_inc(stored, 16)
                sp.wait_ge(stored, 16 * (QT + 1))

            @block.tensor
            def _(pe):
                norm.pe(pe, ssum)
                for t in range(QT + 1):
                    n = P if t < QT else S
                    for b in range(2):
                        j = 2 * t + b
                        if j >= 4:
                            pe.wait_ge(copied, j - 3)
                        for q in range(4):
                            k = 4 * b + q
                            if t == 0:
                                pe.wait_ge(added, k + 1)
                            last = nc.tensor.transpose(psum[0:n, 4 + j % 4, q * P:(q + 1) * P], xT[:, k, t * P:t * P + n], ident[:, :])
                        last.then_inc(turned, 1)

            @block.scalar
            def _(act):
                norm.act(act, lambda k: yT[:, k, :], lambda e, k: None, sq, rstd[:, :])

            @block.vector
            def _(dve):
                norm.dve(dve, sq, ssum, rstd[:, :])
                for k in range(KD):
                    nc.vector.scalar_tensor_tensor(out=yT[:, k, :], in0=yT[:, k, :], scalar=gains[:, 3, k:k + 1], in1=rstd[:, :],
                                                   op0=ALU.mult, op1=ALU.mult).then_inc(scaled, 1)
                for k in range(KD):
                    dve.wait_ge(scaled, k + 1)
                    nc.vector.tensor_tensor(xT[:, k, :], xT[:, k, :], yT[:, k, :], ALU.add).then_inc(added, 1)
                for t in range(QT + 1):
                    n = P if t < QT else S
                    for b in range(2):
                        j = 2 * t + b
                        dve.wait_ge(turned, j + 1)
                        nc.vector.tensor_copy(y_nat[0:n, t, b * 512:(b + 1) * 512], psum[0:n, 4 + j % 4, :]).then_inc(copied, 1)


OUTS = [(1, 1024, 1024), (8, 4, 1024), (1, 1, 1024, 4, 2, 64), (1, 1, 1024, 2, 8, 64), (1, 1, 1024, 8), (1, 1, 512, 2, 2, 64),
        (1, 8, 4, 4, 2, 64), (1, 8, 4, 2, 8, 64), (1, 8, 4, 8), (1, 8, 512, 2, 2, 64)]
INS = ["x_prompt", "x_sample", "cache_nsa_kv", "cache_fox_kv", "cache_fox_logf", "state_win_kv", "page_table", "rel_bias",
       "norm_mix_pre", "norm_mix_post", "norm_ffn_pre", "norm_ffn_post", "w_in", "b_gate", "b_forget", "cmp_pe", "cmp_w1",
       "cmp_w2", "grp_norm_nsa", "grp_norm_fox", "w_o", "w_ffn_gate", "w_ffn_up", "w_ffn_down"]


def kernel(**inputs):
    import concourse.bacc as bacc
    from concourse.bass_utils import run_bass_kernel_spmd

    nc = bacc.Bacc("TRN2", target_bir_lowering=False, num_devices=1)
    arrays, a, c = {}, {}, {}
    for name in INS:
        x = np.ascontiguousarray(inputs[name])
        arrays["in_" + name] = x
        a[name] = nc.dram_tensor("in_" + name, x.shape, mybir.dt.from_np(x.dtype), kind="ExternalInput").ap()
    for name, x in constants().items():
        arrays["const_" + name] = x
        c[name] = nc.dram_tensor("const_" + name, x.shape, mybir.dt.from_np(x.dtype), kind="ExternalInput").ap()
    o = [nc.dram_tensor(f"out_{i}", s, F32, kind="ExternalOutput").ap() for i, s in enumerate(OUTS)]
    program(nc, a, o, c)
    r = run_bass_kernel_spmd(nc, [arrays], core_ids=[0])
    return tuple(r.results[0][f"out_{i}"] for i in range(len(OUTS)))


def constants():
    f = np.float32
    dist = 255 - np.arange(384)
    n = np.maximum(dist, 1).astype(f)
    large = 16 + (np.log(n / f(16)) / f(np.log(128 / 16)) * f(16)).astype(np.int32)
    bucket = np.where(dist < 16, np.maximum(dist, 0), np.minimum(large, 31))
    onehot = np.zeros((33, 384), f)
    onehot[bucket, np.arange(384)] = 1
    onehot[31] -= 1
    onehot[:32, dist < 0] = 0
    onehot[32] = dist < 0
    q, k = np.arange(P)[:, None], np.arange(P)[None]
    row = np.arange(H * TS)
    t, new = row[:, None] % TS, np.arange(TS)[None]
    head = row // TS
    blk = np.arange(NC)[:, None] * CS
    slc = np.arange(16)[None] * 64
    return {
        "ident": np.eye(P, dtype=f),
        "onehot": onehot,
        "causal": np.where(k > q, f(NEG), f(0)).astype(f),
        "band": np.where(k <= q, f(NEG), f(0)).astype(f),
        "mask_new": np.concatenate([np.where(new > t, f(NEG), f(0)), np.where(new <= t, f(NEG), f(0))], 1).astype(f),
        "overlap": ((blk < slc + 64) & (blk + CB > slc)).astype(f),
        "group_sum": ((head[:, None] // R == head[None] // R) & (row[:, None] % TS == row[None] % TS)).astype(f),
        "neg_pick": -(np.arange(H)[:, None] == head[None]).astype(f),
        "iota": np.tile(np.arange(16, dtype=f), (32, 1)),
    }
```

```python
import numpy as np
import concourse.bass as bass
from concourse import mybir
from contextlib import ExitStack

F32 = mybir.dt.float32
F32R = mybir.dt.float32r
I32 = mybir.dt.int32
ACT = mybir.ActivationFunctionType
ALU = mybir.AluOpType
AX = mybir.AxisListType

P = 128
D = 1024
KD = D // P
T = 1024
QT = T // P
NS, TS = 8, 4
S = NS * TS
N = T + S
NB = N // 3
DH = 64
H = 8
G, R = 2, 4
PAST = 1024
PAGE = 128
PAGES = PAST // PAGE
WIN = 512
DFF = 2816
FT = DFF // P
CB, CS = 32, 16
NC = PAST // CS - 1
EPS = 1e-6
POOL_PAGES = 80
NEG = -1e30
SCALE = DH ** -0.5
GF = 64
GATE0 = 32


class Steps:

    def __init__(self, sem, names, rounds=1):
        self.sem, self.names, self.per = sem, list(names), len(names)
        self.index = {n: i for i, n in enumerate(self.names)}
        assert len(self.index) == self.per, "two steps of one name"
        self.slack = self.per if rounds > 1 else 0
        self.cursor = 0

    def start(self, eng):
        if self.slack:
            eng.sem_inc(self.sem, self.slack)

    def at(self, name, i=0, back=0):
        return i * self.per + (self.index[name] + 1 + self.slack - back * self.per)

    def wait(self, eng, name, i=0, back=0):
        if back and not self.slack:
            return
        eng.wait_ge(self.sem, self.at(name, i, back))

    def done(self, instruction, name):
        assert self.names[self.cursor] == name, (self.names[self.cursor], name)
        self.cursor = (self.cursor + 1) % self.per
        instruction.then_inc(self.sem, 1)


def apart(eng):
    eng.nop(nofuse=True)


def projection_plan():
    loops = [dict(name="q_n", col=0, pairs=2, turn=False), dict(name="nsa_kv", col=512, pairs=2, turn=True),
             dict(name="win_kv", col=1024, pairs=1, turn=True), dict(name="q_f", col=1304, pairs=2, turn=False),
             dict(name="fox_kv", col=1816, pairs=4, turn=True)]
    n = t = 0
    stored = [16, 16]
    for l in loops:
        l.update(n0=n, t0=t, stored0=list(stored))
        n += 2 * l["pairs"]
        if l["turn"]:
            t += 2 * l["pairs"]
            per = [32, 48] if l["name"] == "win_kv" else [32, 32]
            l["per"] = per
            stored = [a + b * l["pairs"] for a, b in zip(stored, per)]
    return loops, n, t, stored


PLAN, NZ, NTURN, NAT_STORED = projection_plan()
TILE = {l["name"]: l["n0"] for l in PLAN}


def program(nc, a, o, c):
    (y_prompt, y_sample, nsa_kv_prompt, fox_kv_prompt, logf_prompt, win_kv_prompt,
     nsa_kv_sample, fox_kv_sample, logf_sample, win_kv_sample) = o
    root = ExitStack()
    with root:
        def sb(ctx, name, shape, dt=F32):
            return ctx.enter_context(nc.sbuf_tensor(name, shape, dt))

        def sem(name):
            return root.enter_context(nc.semaphore(name))

        psum = root.enter_context(nc.psum_tensor("psum", [P, 8, 512], F32))
        bank = [psum[:, i, :] for i in range(8)]

        zT = nc.dram_tensor("zT", (NZ, P, N), F32).ap()
        vw_nat = nc.dram_tensor("vw_nat", (T, P), F32).ap()
        negck = nc.dram_tensor("negck", (H, T), F32).ap()
        gfT = nc.dram_tensor("gfT", (GF, N), F32).ap()
        bias_tab = nc.dram_tensor("bias_tab", (H, P, 384), F32).ap()
        gates_dram = nc.dram_tensor("gates_dram", (3, NS, H * TS), F32).ap()
        kc_dram = nc.dram_tensor("kc_dram", (G * DH, NC), F32).ap()
        vc_dram = nc.dram_tensor("vc_dram", (NC, G * DH), F32).ap()
        x_dram = nc.dram_tensor("x_dram", (P, KD, N), F32).ap()
        x1_dram = nc.dram_tensor("x1_dram", (P, KD, N), F32).ap()
        oT_dram = nc.dram_tensor("oT_dram", (2 * H * DH, N), F32).ap()

        ident = sb(root, "ident", [P, P])
        ones = sb(root, "ones", [P, P])
        gains = sb(root, "gains", [P, 6, KD])
        eps = sb(root, "eps", [P, 1])
        gf_nat = sb(root, "gf_nat", [P, QT + 1, GF])

        env = dict(locals())
        build_a(nc, a, o, c, env)
        build_b(nc, a, o, c, env)
        with ExitStack() as ffn:
            with ExitStack() as later:
                ffn_out = sb(later, "ffn_out", [P, KD, N])
            hf_hi = sb(ffn, "hf_hi", [P, KD, N], F32R)
            hf_lo = sb(ffn, "hf_lo", [P, KD, N], F32R)
            with ExitStack() as mixing:
                mixT = sb(mixing, "mixT", [P, KD, N])
                build_c(nc, a, o, c, env, mixT)
                build_d(nc, a, env, mixT, hf_hi, hf_lo)
            build_e(nc, a, env, hf_hi, hf_lo, ffn_out)
            build_f(nc, a, o, env, ffn_out)


def product(nc, dst, w_hi, w_lo, x_hi, x_lo, start, stop):
    nc.tensor.matmul(dst, w_hi, x_hi, start=start, stop=False)
    nc.tensor.matmul(dst, w_hi, x_lo, start=False, stop=False)
    return nc.tensor.matmul(dst, w_lo, x_hi, start=False, stop=stop)


def norm_act(nc, act, src, n, sq, sq_free, sq_ready):
    for k in range(n):
        if k >= 2:
            act.wait_ge(sq_free, k - 1)
        nc.scalar.activation(sq[:, k % 2, :], src(k), ACT.Square).then_inc(sq_ready, 1)


def build_a(nc, a, o, c, env):
    (y_prompt, y_sample, nsa_kv_prompt, fox_kv_prompt, logf_prompt, win_kv_prompt,
     nsa_kv_sample, fox_kv_sample, logf_sample, win_kv_sample) = o
    ident, ones, gains, gf_nat, bank = (env[k] for k in ("ident", "ones", "gains", "gf_nat", "bank"))
    eps = env["eps"]
    x_dram, zT, vw_nat, negck, gfT = (env[k] for k in ("x_dram", "zT", "vw_nat", "negck", "gfT"))
    sem = env["sem"]
    ctx = ExitStack()
    with ctx:
        def sb(name, shape, dt=F32):
            return ctx.enter_context(nc.sbuf_tensor(name, shape, dt))

        xT = sb("xT", [P, KD, N])
        x_hi = sb("x_hi", [P, KD, N], F32R)
        with ExitStack() as early:
            x_nat = early.enter_context(nc.sbuf_tensor("x_nat", [P, QT, D], F32))
            xs_nat = early.enter_context(nc.sbuf_tensor("xs_nat", [S, D], F32))
        x_lo = sb("x_lo", [P, KD, N], F32R)
        sq = sb("sq", [P, 2, N])
        ssum = sb("ssum", [P, N])
        rstd = sb("rstd", [P, N])
        w_ring = sb("w_ring", [P, 2, KD, P])
        w_hi = sb("w_hi", [P, 2, KD, P], F32R)
        w_lo = sb("w_lo", [P, 2, KD, P], F32R)
        w_gf = sb("w_gf", [P, KD, GF])
        w_gf_hi = sb("w_gf_hi", [P, KD, GF], F32R)
        w_gf_lo = sb("w_gf_lo", [P, KD, GF], F32R)
        z_stage = sb("z_stage", [P, 2, N])
        nat = sb("nat", [P, 2, QT + 1, P])
        gf_bias = sb("gf_bias", [GF, 1])
        gfz = sb("gfz", [GF, N])
        lf_min = sb("lf_min", [H, N])
        lf_abs = sb("lf_abs", [H, N])
        neg_cum = sb("neg_cum", [H, T])

        x_loaded = [sem(f"x_loaded{t}") for t in range(QT // 2 + 1)]
        const_loaded = sem("const_loaded")
        gf_loaded = sem("gf_loaded")
        ones_set = sem("ones_set")
        xt_turned = sem("xt_turned")
        xt_copied = sem("xt_copied")
        sq_ready = sem("sq_ready")
        ssum_ready = sem("ssum_ready")
        ms_ready = sem("ms_ready")
        rms_ready = sem("rms_ready")
        rstd_ready = sem("rstd_ready")
        xn_ready = sem("xn_ready")
        w_loaded = [sem(f"w_loaded{s}") for s in range(2)]
        w_high = sem("w_high")
        w_split = sem("w_split")
        gf_split = sem("gf_split")
        xn_high = sem("xn_high")
        xn_split = sem("xn_split")
        z_done = sem("z_done")
        z_copied = sem("z_copied")
        zt_stored = [sem(f"zt_stored{s}") for s in range(2)]
        turned = sem("turned")
        turn_copied = sem("turn_copied")
        nat_stored = [sem(f"nat_stored{s}") for s in range(2)]
        gf_done = sem("gf_done")
        gf_act = sem("gf_act")
        gf_dve = sem("gf_dve")
        gf_turned = sem("gf_turned")
        gf_copied = sem("gf_copied")
        gf_stored = sem("gf_stored")
        win_moved = sem("win_moved")
        x_stored = sem("x_stored")

        W = a["w_in"][0].rearrange("(k p) n -> p k n", p=P)
        block = ctx.enter_context(nc.Block())

        @block.sync
        def _(sp):
            for t in range(QT):
                sp.dma_start(x_nat[:, t, :], a["x_prompt"][0, t * P:(t + 1) * P, :]).then_inc(x_loaded[t // 2], 16)
            sp.dma_start(xs_nat[:, :], a["x_sample"].rearrange("s t d -> (s t) d")).then_inc(x_loaded[QT // 2], 16)
            for s in range(2):
                sp.sem_inc(zt_stored[s], 16)
                sp.sem_inc(nat_stored[s], 16)
            sp.wait_ge(xt_copied, 18)
            sp.dma_start(x_dram[:, :, :], xT[:, :, :]).then_inc(x_stored, 16)
            sp.wait_ge(gf_act, 4)
            sp.wait_ge(gf_dve, 5)
            sp.dma_start(gfT[:, :], gfz[:, :]).then_inc(gf_stored, 16)
            sp.dma_start(negck[:, :], neg_cum[:, :]).then_inc(gf_stored, 16)
            sp.wait_ge(gf_copied, 2)
            with nc.allow_non_contiguous_dma(reason="eight numbers per token"):
                sp.dma_start(logf_prompt[0, 0].rearrange("(t p) h -> p t h", p=P), gf_nat[:, 0:QT, 0:H]).then_inc(gf_stored, 16)
                sp.dma_start(logf_sample[0].rearrange("s t h -> (s t) h"), gf_nat[0:S, QT, 0:H]).then_inc(gf_stored, 16)

            for l in PLAN:
                def pair(i):
                    for s in range(2):
                        n = i * 2 + (l["n0"] + s)
                        sp.wait_ge(z_copied, n + 3)
                        sp.dma_start(zT[bass.ds(n, 1)].rearrange("o p n -> p (o n)"), z_stage[:, s, :]).then_inc(zt_stored[s], 16)
                    if not l["turn"]:
                        return
                    for s in range(2):
                        m = i * 2 + (l["t0"] + s)
                        sp.wait_ge(turn_copied, m * 3 + 5)
                        done = nat_stored[s]
                        if l["name"] == "win_kv":
                            kv = s
                            sp.dma_start(win_kv_prompt[0, 0].rearrange("(t p) a g d -> p t a (g d)", p=P)[:, :, kv],
                                           nat[:, s, QT // 2:QT, :]).then_inc(done, 16)
                            sp.dma_start(win_kv_sample[0, :, WIN - TS:WIN, kv].rearrange("s t g d -> s t (g d)"),
                                           nat[0:S, s, QT, :]).then_inc(done, 16)
                            if s == 1:
                                sp.dma_start(vw_nat.rearrange("(t p) d -> p t d", p=P), nat[:, s, 0:QT, :]).then_inc(done, 16)
                        else:
                            op, os = (nsa_kv_prompt, nsa_kv_sample) if l["name"] == "nsa_kv" else (fox_kv_prompt, fox_kv_sample)
                            cols = bass.ds(i * 256 + s * P, P)
                            sp.dma_start(op[0, 0].rearrange("(t p) a g d -> p t (a g d)", p=P)[:, :, cols],
                                           nat[:, s, 0:QT, :]).then_inc(done, 16)
                            sp.dma_start(os[0].rearrange("s t a g d -> (s t) (a g d)")[:, cols],
                                           nat[0:S, s, QT, :]).then_inc(done, 16)
                loop(sp, l["pairs"], pair)
            for s in range(2):
                sp.wait_ge(zt_stored[s], 16 + 16 * (NZ // 2))
                sp.wait_ge(nat_stored[s], NAT_STORED[s])
            sp.wait_ge(gf_stored, 64)
            sp.wait_ge(x_stored, 16)

        @block.gpsimd
        def _(pool):
            pool.memset(ones[:, :], 1.0).then_inc(ones_set, 1)
            pool.memset(w_gf[:, :, :], 0.0).then_inc(ones_set, 1)
            pool.memset(gf_bias[:, :], 0.0).then_inc(ones_set, 1)
            pool.memset(eps[:, :], EPS).then_inc(ones_set, 1)
            pool.dma_start(ident[:, :], c["ident"]).then_inc(const_loaded, 16)
            with nc.allow_non_contiguous_dma(reason="gains are one number per row"):
                for i, g in enumerate(("norm_mix_pre", "norm_mix_post", "norm_ffn_pre", "norm_ffn_post")):
                    pool.dma_start(gains[:, i, :], a[g][0].rearrange("(k p) -> p k", p=P)).then_inc(const_loaded, 16)
                pool.dma_start(gains[:, 4, 0:4], a["grp_norm_nsa"][0].rearrange("(k p) -> p k", p=P)).then_inc(const_loaded, 16)
                pool.dma_start(gains[:, 4, 4:8], a["grp_norm_fox"][0].rearrange("(k p) -> p k", p=P)).then_inc(const_loaded, 16)
                pool.wait_ge(ones_set, 4)
                pool.dma_start(w_gf[:, :, 0:H], W[:, :, 2840:2848]).then_inc(gf_loaded, 16)
                pool.dma_start(w_gf[:, :, GATE0:GATE0 + 24], W[:, :, 1280:1304]).then_inc(gf_loaded, 16)
                pool.dma_start(gf_bias[0:H, :], a["b_forget"][0].rearrange("(h o) -> h o", o=1)).then_inc(gf_loaded, 16)
                pool.dma_start(gf_bias[GATE0:GATE0 + 24, :], a["b_gate"][0].rearrange("b (h o) -> (b h) o", o=1)).then_inc(gf_loaded, 16)
            pool.dma_start(win_kv_sample[0, :, 0:WIN - TS].rearrange("s w a g d -> s w (a g d)"),
                           a["state_win_kv"][0, :, TS:WIN].rearrange("s w a g d -> s w (a g d)")).then_inc(win_moved, 16)
            for l in PLAN:
                def pair(i):
                    for s in range(2):
                        n = i * 2 + (l["n0"] + s)
                        pool.wait_ge(w_split, n + 1)
                        pool.dma_start(w_ring[:, s], W[:, :, bass.ds(i * 256 + (l["col"] + s * P), P)]).then_inc(w_loaded[s], 16)
                loop(pool, l["pairs"], pair)

            pool.wait_ge(win_moved, 16)

        @block.tensor
        def _(pe):
            pe.sem_inc(z_done, 2)
            pe.wait_ge(const_loaded, 16 * 7)
            for t in range(QT + 1):
                rows = P if t < QT else S
                pe.wait_ge(x_loaded[t // 2], 32 if t < QT else 16)
                for b in range(2):
                    j = 2 * t + b
                    if j >= 6:
                        pe.wait_ge(xt_copied, j - 5)
                    for q in range(4):
                        k = 4 * b + q
                        src = x_nat[:, t, k * P:(k + 1) * P] if t < QT else xs_nat[:, k * P:(k + 1) * P]
                        last = nc.tensor.transpose(bank[j % 6][:, q * P:q * P + rows], src, ident[0:rows, 0:rows])
                    last.then_inc(xt_turned, 1)
            pe.wait_ge(xt_copied, 18)
            pe.wait_ge(ones_set, 4)
            pe.wait_ge(ssum_ready, KD)
            for b in range(3):
                last = nc.tensor.matmul(bank[b][:, 0:NB], ones[:, :], ssum[:, b * NB:(b + 1) * NB], start=True, stop=True)
            last.then_inc(ms_ready, 1)
            pe.wait_ge(gf_split, 2)
            pe.wait_ge(xn_split, KD)
            for b in range(3):
                for k in range(KD):
                    tok = slice(b * NB, (b + 1) * NB)
                    last = product(nc, bank[3 + b][:, 0:NB][0:GF], w_gf_hi[:, k, :], w_gf_lo[:, k, :], x_hi[:, k, tok], x_lo[:, k, tok],
                                   k == 0, k == KD - 1)
            last.then_inc(gf_done, 1)
            pe.wait_ge(gf_act, 4)
            pe.wait_ge(gf_dve, 5)
            for t in range(QT + 1):
                n = P if t < QT else S
                dst = bank[6][0:n, t * GF:(t + 1) * GF] if t < QT else bank[7][0:n, 0:GF]
                last = nc.tensor.transpose(dst, gfz[:, t * P:t * P + n], ident[0:GF, 0:GF])
            last.then_inc(gf_turned, 1)
            pe.wait_ge(gf_copied, 2)
            for l in PLAN:
                def pair(i):
                    for s in range(2):
                        n = i * 2 + (l["n0"] + s)
                        pe.wait_ge(w_split, n + 3)
                        pe.wait_ge(z_copied, n + 1)
                        for b in range(3):
                            for k in range(KD):
                                tok = slice(b * NB, (b + 1) * NB)
                                last = product(nc, bank[3 * s + b][:, 0:NB], w_hi[:, s, k, :], w_lo[:, s, k, :],
                                               x_hi[:, k, tok], x_lo[:, k, tok], k == 0, k == KD - 1)
                        last.then_inc(z_done, 1)
                    if not l["turn"]:
                        return
                    for s in range(2):
                        n = i * 2 + (l["n0"] + s)
                        m = i * 2 + (l["t0"] + s)
                        pe.wait_ge(z_copied, n + 3)
                        for part in range(3):
                            pe.wait_ge(turn_copied, m * 3 + (part + 1))
                            for q in range(4 if part < 2 else 1):
                                t = 4 * part + q
                                cols = P if part < 2 else S
                                dst = bank[6 + (part if s == 0 else 1 - part) % 2]
                                last = nc.tensor.transpose(dst[0:cols, q * P:(q + 1) * P],
                                                           z_stage[:, s, t * P:t * P + cols], ident[:, :])
                            last.then_inc(turned, 1)
                loop(pe, l["pairs"], pair)

        @block.scalar
        def _(act):
            act.wait_ge(xt_copied, 18)
            norm_act(nc, act, lambda k: xT[:, k, :], KD, sq, ssum_ready, sq_ready)
            act.wait_ge(ms_ready, 1)
            act.wait_ge(ones_set, 4)
            for b in range(3):
                last = nc.scalar.activation(rstd[:, b * NB:(b + 1) * NB], bank[b][:, 0:NB], ACT.Sqrt, bias=eps[:, 0:1], scale=1.0 / D)
            last.then_inc(rms_ready, 1)
            for k in range(KD):
                act.wait_ge(xn_ready, k + 1)
                nc.scalar.copy(x_hi[:, k, :], sq[:, k % 2, :]).then_inc(xn_high, 1)
            act.wait_ge(gf_done, 1)
            for b in range(3):
                nc.scalar.activation(gfz[:, b * NB:(b + 1) * NB], bank[3 + b][0:GF, 0:NB], ACT.Identity,
                                     bias=gf_bias[:, :]).then_inc(gf_act, 1) if b == 2 else \
                    nc.scalar.activation(gfz[:, b * NB:(b + 1) * NB], bank[3 + b][0:GF, 0:NB], ACT.Identity, bias=gf_bias[:, :])
            act.wait_ge(gf_act, 1)
            nc.scalar.activation(gfz[GATE0:GF, :], gfz[GATE0:GF, :], ACT.Sigmoid).then_inc(gf_act, 1)
            act.wait_ge(gf_dve, 2)
            nc.scalar.activation(lf_abs[:, :], lf_abs[:, :], ACT.Exp, scale=-1.0).then_inc(gf_act, 1)
            act.wait_ge(gf_act, 3)
            nc.scalar.activation(lf_abs[:, :], lf_abs[:, :], ACT.Ln, bias=1.0).then_inc(gf_act, 1)
            act.sem_inc(z_copied, 2)
            for l in PLAN:
                scale = SCALE if l["name"] in ("q_n", "q_f") else 1.0

                def pair(i):
                    for s in range(2):
                        n = i * 2 + (l["n0"] + s)
                        act.wait_ge(z_done, n + 3)
                        act.wait_ge(zt_stored[s], i * 16 + 16 * (l["n0"] // 2 + 1))
                        for b in range(3):
                            last = nc.scalar.activation(z_stage[:, s, b * NB:(b + 1) * NB], bank[3 * s + b][:, 0:NB],
                                                        ACT.Copy, scale=scale)
                        last.then_inc(z_copied, 1)
                loop(act, l["pairs"], pair)

        @block.vector
        def _(dve):
            for t in range(QT + 1):
                rows = P if t < QT else S
                for b in range(2):
                    j = 2 * t + b
                    dve.wait_ge(xt_turned, j + 1)
                    nc.vector.tensor_copy(xT[:, 4 * b:4 * b + 4, t * P:t * P + rows],
                                          bank[j % 6][:, :].rearrange("p (q n) -> p q n", q=4)[:, :, 0:rows]).then_inc(xt_copied, 1)
            for k in range(KD):
                dve.wait_ge(sq_ready, k + 1)
                if k == 0:
                    nc.vector.tensor_copy(ssum[:, :], sq[:, 0, :]).then_inc(ssum_ready, 1)
                else:
                    dve.wait_ge(ssum_ready, k)
                    nc.vector.tensor_tensor(ssum[:, :], ssum[:, :], sq[:, k % 2, :], ALU.add).then_inc(ssum_ready, 1)
            dve.wait_ge(rms_ready, 1)
            nc.vector.reciprocal(rstd[:, :], rstd[:, :]).then_inc(rstd_ready, 1)
            dve.wait_ge(rstd_ready, 1)
            dve.wait_ge(const_loaded, 16 * 7)
            def low(k):
                dve.wait_ge(xn_high, k + 1)
                nc.vector.tensor_tensor(x_lo[:, k, :], sq[:, k % 2, :], x_hi[:, k, :].bitcast(F32), ALU.subtract).then_inc(xn_split, 1)

            for k in range(KD):
                if k >= 2:
                    dve.wait_ge(xn_split, k - 1)
                nc.vector.scalar_tensor_tensor(out=sq[:, k % 2, :], in0=xT[:, k, :], scalar=gains[:, 0, k:k + 1], in1=rstd[:, :],
                                               op0=ALU.mult, op1=ALU.mult).then_inc(xn_ready, 1)
                if k >= 1:
                    low(k - 1)
            low(KD - 1)
            dve.wait_ge(gf_loaded, 64)
            nc.vector.tensor_copy(w_gf_hi[:, :, :], w_gf[:, :, :]).then_inc(gf_split, 1)
            dve.wait_ge(gf_split, 1)
            nc.vector.tensor_tensor(w_gf_lo[:, :, :], w_gf[:, :, :], w_gf_hi[:, :, :].bitcast(F32), ALU.subtract).then_inc(gf_split, 1)
            dve.sem_inc(w_split, 2)

            def split(n, s, load):
                dve.wait_ge(w_loaded[s], load)
                dve.wait_ge(z_done, n + 1)
                nc.vector.tensor_copy(w_hi[:, s], w_ring[:, s]).then_inc(w_high, 1)
                dve.wait_ge(w_high, n + 1)
                nc.vector.tensor_tensor(w_lo[:, s], w_ring[:, s], w_hi[:, s].bitcast(F32), ALU.subtract).then_inc(w_split, 1)

            split(0, 0, 16)
            split(1, 1, 16)
            dve.wait_ge(gf_act, 1)
            nc.vector.tensor_scalar(lf_min[:, :], gfz[0:H, :], 0.0, None, ALU.min).then_inc(gf_dve, 1)
            dve.wait_ge(gf_dve, 1)
            nc.vector.scalar_tensor_tensor(out=lf_abs[:, :], in0=lf_min[:, :], scalar=-2.0, in1=gfz[0:H, :],
                                           op0=ALU.mult, op1=ALU.add).then_inc(gf_dve, 1)
            dve.wait_ge(gf_act, 4)
            nc.vector.tensor_tensor(gfz[0:H, :], lf_min[:, :], lf_abs[:, :], ALU.subtract).then_inc(gf_dve, 1)
            dve.wait_ge(gf_dve, 3)
            dve.wait_ge(ones_set, 4)
            nc.vector.tensor_tensor_scan(neg_cum[:, :], ones[0:H, 0:1].to_broadcast([H, T]), gfz[0:H, 0:T], 0.0, ALU.mult, ALU.subtract).then_inc(gf_dve, 2)
            dve.wait_ge(gf_turned, 1)
            nc.vector.tensor_copy(gf_nat[:, 0:QT, :], bank[6][:, :].rearrange("p (t g) -> p t g", t=QT)).then_inc(gf_copied, 1)
            nc.vector.tensor_copy(gf_nat[0:S, QT, :], bank[7][0:S, 0:GF]).then_inc(gf_copied, 1)
            dve.sem_inc(turn_copied, 2)
            for l in PLAN:
                def pair(i, ahead=True):
                    for s in range(2):
                        if ahead:
                            n = i * 2 + (l["n0"] + s + 2)
                            split(n, s, i * 16 + 16 * (l["n0"] // 2 + 2))
                    if not l["turn"]:
                        return
                    for s in range(2):
                        m = i * 2 + (l["t0"] + s)
                        dve.wait_ge(nat_stored[s], i * l["per"][s] + l["stored0"][s])
                        for part in range(3):
                            dve.wait_ge(turned, m * 3 + (part + 1))
                            src = bank[6 + (part if s == 0 else 1 - part) % 2]
                            if part < 2:
                                nc.vector.tensor_copy(nat[:, s, 4 * part:4 * part + 4, :],
                                                      src[:, :].rearrange("p (q n) -> p q n", q=4)).then_inc(turn_copied, 1)
                            else:
                                nc.vector.tensor_copy(nat[0:S, s, QT, :], src[0:S, 0:P]).then_inc(turn_copied, 1)
                if l is PLAN[-1]:
                    loop(dve, l["pairs"] - 1, pair)
                    pair(l["pairs"] - 1, ahead=False)
                else:
                    loop(dve, l["pairs"], pair)


def loop(eng, count, body):
    if count == 1:
        body(0)
        return
    with eng.Fori(0, count) as i:
        body(i)



def compress_jobs(seqs):
    jobs = [(("ct", kv, g, half), "AV"[(2 * kv + g + half) % 2]) for kv in range(2) for g in range(G) for half in range(2)]
    jobs += [(("hid", 0), "A"), (("hid", 1), "A"), (("kc",), "V")]
    jobs += [(("vc", b), "V") for b in range(seqs)]
    return jobs


def sample_jobs(b):
    jobs = [("s_cmp", "V"), ("lf0", "V"), ("lf1", "V"), ("ks0", "A"), ("ks1", "A"), ("kw", "A"), ("s_win", "V"), ("s_win_new", "V"),
            ("s_slc0", "V"), ("s_slc1", "V"), ("s_slc_new", "V"), ("pt_imp", "A")]
    jobs += [(f"kf{n}", "AV"[n % 2]) for n in range(4)]
    jobs += [("imp", "A")]
    jobs += [(f"kf{n}", "AV"[n % 2]) for n in range(4, 8)]
    jobs += [("imp_sum", "V"), ("s_fox0", "V"), ("s_fox1", "V"), ("s_fox_new", "V"), ("pt_cw", "A"), ("pt_slc", "A"), ("o_nsa", "V"),
             ("pt_fox", "A"), ("o_fox", "V")]
    return [((name, b), engine) for name, engine in jobs]


class Banks:

    def __init__(self, jobs):
        self.order = [name for name, _ in jobs]
        self.engine = dict(jobs)
        self.bank, self.before = {}, {}
        for engine, first in (("A", 0), ("V", 4)):
            mine = [name for name, e in jobs if e == engine]
            for n, name in enumerate(mine):
                self.bank[name] = first + n % 4
            for n, name in enumerate(mine):
                same = [m for m in range(len(mine)) if m % 4 == n % 4]
                p = same.index(n)
                self.before[name] = (mine[same[p - 1]], int(p == 0))


def compress_dve(seqs):
    return [("ord", 0)] + [("ev", j) for j, e in compress_jobs(seqs) if e == "V"]


def compress_act(seqs):
    return [("ord", 1)] + [("ev", j) for j, e in compress_jobs(seqs) if e == "A"]


def sample_act(b):
    return [(n, b) if isinstance(n, str) else ("ev", (n[1], b)) for n in (
        ("ev", "ks0"), ("ev", "ks1"), ("ev", "kw"), "exp_cmp", ("ev", "pt_imp"), "exp_win", ("ev", "kf0"), ("ev", "kf2"), ("ev", "imp"),
        ("ev", "kf4"), ("ev", "kf6"), "exp_slc", "exp_fox", ("ev", "pt_cw"), ("ev", "pt_slc"), ("ev", "pt_fox"))]


def sample_dve(b):
    return [(n, b) if isinstance(n, str) else ("ev", (n[1], b)) for n in (
        ("ev", "s_cmp"), "max_cmp", ("ev", "lf0"), ("ev", "lf1"), "scan", ("ev", "s_win"), ("ev", "s_win_new"), "max_win",
        ("ev", "s_slc0"), ("ev", "s_slc1"), ("ev", "s_slc_new"),
        "rec_cmp", "norm_cmp", "gate_cmp", "rec_win", "fac_win", "gate_win", ("ev", "kf1"), ("ev", "kf3"), ("ev", "kf5"), ("ev", "kf7"),
        ("ev", "imp_sum"), "least", "which", "last", "drop", "mask", "max_slc",
        ("ev", "s_fox0"), ("ev", "s_fox1"), ("ev", "s_fox_new"), "max_fox",
        "rec_slc", "fac_slc", "gate_slc", "rec_fox", "gate_fox", ("ev", "o_nsa"), ("ev", "o_fox"))]


def order_chunks(nc, eng, copy, i, kv, seqs, PE, MINE, buf, loaded):
    rows = seqs * DH
    eng.wait_ge(*loaded)
    PE.wait(eng, ("ct", kv, 1, 1), i, back=1)
    for g in range(G):
        col = (2 * kv + g) * DH
        last = copy(buf["chunks_by_head"][0:rows, kv, g], buf["chunks"][0:rows, :, col:col + DH])
    MINE.done(last, ("ord", kv))


def pe_compress(nc, pe, i, seqs, B, PE, ENG, buf):
    rows = seqs * DH
    psum, ident = buf["psum"], buf["ident"]
    n_blk = seqs * NC

    def start(job):
        before, back = B.before[job]
        e = ENG[B.engine[job]]
        e.wait(pe, ("ev", before), i, back=back) if (back == 0 or e.slack) else None
        return psum[:, B.bank[job], :]

    for kv in range(2):
        ENG["VA"[kv]].wait(pe, ("ord", kv), i)
        for g in range(G):
            for half in range(2):
                job = ("ct", kv, g, half)
                dst = start(job)
                for q in range(4):
                    jj = 4 * half + q
                    src = buf["chunks_by_head"][0:rows, kv, g, 2 * jj:2 * jj + 2].rearrange("p j d -> p (j d)")
                    last = nc.tensor.transpose(dst[:, q * P:q * P + rows], src, ident[0:rows, 0:rows])
                PE.done(last, job)
    for kv in range(2):
        job = ("hid", kv)
        dst = start(job)
        for g in range(G):
            for half in range(2):
                j = ("ct", kv, g, half)
                ENG[B.engine[j]].wait(pe, ("ev", j), i)
        ct = buf["chunksT"][:, kv].rearrange("p j g (b c) -> p j g b c", c=DH)
        for jj in range(16):
            first = jj // 8
            for g in range(G):
                last = nc.tensor.matmul(dst[:, g * n_blk:(g + 1) * n_blk], buf["w1"][:, kv, jj, :],
                                        ct[:, jj % 8, g, 0:seqs, first:first + NC], start=(jj == 0 and g == 0), stop=(jj == 15),
                                        skip_group_check=True)
        PE.done(last, job)
    job = ("kc",)
    dst = start(job)
    ENG["A"].wait(pe, ("ev", ("hid", 0)), i)
    w2k = buf["w2k"]
    nc.tensor.matmul(dst[:, 0:n_blk], w2k[:, DH:3 * DH], buf["hidden"][:, 0, 0:n_blk], start=True, stop=False)
    PE.done(nc.tensor.matmul(dst[:, 0:n_blk], w2k[:, 0:2 * DH], buf["hidden"][:, 0, n_blk:2 * n_blk], start=False, stop=True), job)
    for b in range(seqs):
        job = ("vc", b)
        dst = start(job)
        ENG["A"].wait(pe, ("ev", ("hid", 1)), i)
        apart(pe)
        for g in range(G):
            at = g * n_blk + b * NC
            last = nc.tensor.matmul(dst[0:NC, g * DH:(g + 1) * DH], buf["hidden"][:, 1, at:at + NC], buf["w2v"][:, :], start=True, stop=True)
        PE.done(last, job)


def evict_ct(nc, eng, copy, i, seqs, B, PE, MINE, buf, job):
    _, kv, g, half = job
    rows = seqs * DH
    PE.wait(eng, job, i)
    if PE.slack:
        PE.wait(eng, ("s_fox1", 1), i, back=1)
    MINE.done(copy(buf["chunksT"][:, kv, 4 * half:4 * half + 4, g, 0:rows],
                   buf["psum"][:, B.bank[job], :].rearrange("p (q n) -> p q n", q=4)[:, :, 0:rows]), ("ev", job))


def act_compress(nc, act, i, seqs, B, PE, MINE, buf, loaded):
    order_chunks(nc, act, nc.scalar.copy, i, 1, seqs, PE, MINE, buf, loaded)
    for job, e in compress_jobs(seqs):
        if e != "A":
            continue
        if job[0] == "ct":
            evict_ct(nc, act, nc.scalar.copy, i, seqs, B, PE, MINE, buf, job)
        else:
            kv = job[1]
            PE.wait(act, job, i)
            PE.wait(act, ("kc",) if kv == 0 else ("vc", seqs - 1), i, back=1)
            n = G * seqs * NC
            MINE.done(nc.scalar.activation(buf["hidden"][:, kv, 0:n], buf["psum"][:, B.bank[job], 0:n], ACT.Gelu_apprx_tanh,
                                           bias=buf["pe_bias"][:, kv:kv + 1]), ("ev", job))


def dve_compress(nc, dve, i, seqs, B, PE, MINE, buf, loaded, kc_free, vc_free):
    order_chunks(nc, dve, nc.vector.tensor_copy, i, 0, seqs, PE, MINE, buf, loaded)
    for job, e in compress_jobs(seqs):
        if e != "V":
            continue
        if job[0] == "ct":
            evict_ct(nc, dve, nc.vector.tensor_copy, i, seqs, B, PE, MINE, buf, job)
        elif job[0] == "kc":
            PE.wait(dve, job, i)
            kc_free(dve)
            MINE.done(nc.vector.tensor_copy(buf["kc"][:, 0:seqs * NC], buf["psum"][:, B.bank[job], 0:seqs * NC]), ("ev", job))
        else:
            b = job[1]
            PE.wait(dve, job, i)
            vc_free(dve, b)
            MINE.done(nc.vector.tensor_copy(buf["vc"][0:NC, b, :], buf["psum"][0:NC, B.bank[job], 0:P]), ("ev", job))


def build_b(nc, a, o, c, env):
    (y_prompt, y_sample, nsa_kv_prompt, fox_kv_prompt, logf_prompt, win_kv_prompt,
     nsa_kv_sample, fox_kv_sample, logf_sample, win_kv_sample) = o
    ident, psum, sem = env["ident"], env["psum"], env["sem"]
    zT, gfT, oT_dram, bias_tab, kc_dram, vc_dram, gates_dram = (env[k] for k in ("zT", "gfT", "oT_dram", "bias_tab", "kc_dram", "vc_dram", "gates_dram"))
    ctx = ExitStack()
    with ctx:
        def sb(name, shape, dt=F32, where=None):
            return (where or ctx).enter_context(nc.sbuf_tensor(name, shape, dt))

        w1 = sb("w1", [P, 2, 16, P])
        w2k = sb("w2k", [P, 3 * DH])
        w2v = sb("w2v", [P, DH])
        pe_cols = sb("pe_cols", [P, 2, 16])
        pe_bias = sb("pe_bias", [P, 2])
        chunks = sb("chunks", [P, CS, 2 * P])
        chunks_by_head = sb("chunks_by_head", [P, 2, G, CS, DH])
        turned = sb("turned", [P, 4 * PAST])
        chunksT = turned[:, :].rearrange("p (v j g n) -> p v j g n", v=2, j=8, g=G)
        kT_fox = turned[:, :].rearrange("p (n k) -> p n k", n=4)
        hidden = sb("hidden", [P, 2, G * 2 * NC])
        kc = sb("kc", [P, 2 * NC])
        vc = sb("vc", [NC, 2, P])
        buf = dict(psum=psum, ident=ident, w1=w1, w2k=w2k, w2v=w2v, pe_bias=pe_bias, chunks=chunks, chunks_by_head=chunks_by_head, chunksT=chunksT,
                   hidden=hidden, kc=kc, vc=vc)

        with ExitStack() as first:
            rel = sb("rel", [33, H], where=first)
            onehot = sb("onehot", [33, 384], where=first)
            bias_vec = sb("bias_vec", [H, 384], where=first)
            w_loaded, rel_loaded, rel_set, chunk_loaded = sem("b0_w_loaded"), sem("b0_rel_loaded"), sem("b0_rel_set"), sem("b0_chunk_loaded")
            tab_done, tab_copied, tab_stored = sem("b0_tab_done"), sem("b0_tab_copied"), sem("b0_tab_stored")
            peb_done, peb_copied, w2_zero = sem("b0_peb_done"), sem("b0_peb_copied"), sem("b0_w2_zero")
            B0 = Banks(compress_jobs(1))
            PE0 = Steps(sem("b0_pe"), B0.order)
            ACT0 = Steps(sem("b0_act"), compress_act(1))
            DVE0 = Steps(sem("b0_dve"), compress_dve(1))
            ENG0 = {"A": ACT0, "V": DVE0}
            with nc.Block() as block:
                @block.sync
                def _(sp):
                    sp.dma_start(rel[0:32, :], a["rel_bias"]).then_inc(rel_loaded, 16)
                    sp.dma_start(onehot[:, :], c["onehot"]).then_inc(rel_loaded, 16)
                    sp.dma_start(w1[:, 0], a["cmp_w1"][0, 0].rearrange("(j p) n -> p j n", p=P)).then_inc(w_loaded, 16)
                    sp.dma_start(chunks[0:DH, :, :], nsa_kv_prompt[0, 0].rearrange("(c j) a g d -> c j (a g d)", j=CS)[:, :, 0:2 * P]).then_inc(chunk_loaded, 16)
                    sp.wait_ge(w2_zero, 1)
                    sp.dma_start(w2k[:, DH:2 * DH], a["cmp_w2"][0, 0]).then_inc(w_loaded, 16)
                    sp.dma_start(w2v[:, :], a["cmp_w2"][0, 1]).then_inc(w_loaded, 16)
                    with nc.allow_non_contiguous_dma(reason="gates of the sampled tokens"):
                        for br in range(3):
                            sp.dma_start(gates_dram[br].rearrange("s (h t) -> h s t", t=TS),
                                         gfT[GATE0 + br * H:GATE0 + (br + 1) * H, T:N].rearrange("h (s t) -> h s t", t=TS)).then_inc(tab_stored, 16)
                    sp.wait_ge(tab_copied, 1)
                    sp.dma_start(bias_tab, bias_vec[:, :].unsqueeze(1).to_broadcast([H, P, 384])).then_inc(tab_stored, 16)
                    DVE0.wait(sp, ("ev", ("kc",)))
                    sp.dma_start(kc_dram, kc[:, 0:NC]).then_inc(tab_stored, 16)
                    DVE0.wait(sp, ("ev", ("vc", 0)))
                    sp.dma_start(vc_dram, vc[:, 0, :]).then_inc(tab_stored, 16)
                    sp.wait_ge(tab_stored, 96)

                @block.gpsimd
                def _(pool):
                    pool.memset(w2k[:, :], 0.0).then_inc(w2_zero, 1)
                    pool.wait_ge(w2_zero, 1)
                    pool.memset(rel[32:33, :], NEG).then_inc(rel_set, 1)

                @block.tensor
                def _(pe):
                    pe.wait_ge(rel_loaded, 32)
                    pe.wait_ge(rel_set, 1)
                    nc.tensor.matmul(psum[0:H, 7, 0:384], rel[:, :], onehot[:, :], start=True, stop=True).then_inc(tab_done, 1)
                    pe.wait_ge(tab_copied, 1)
                    pe.wait_ge(w_loaded, 96)
                    for kv in range(2):
                        for jj in range(16):
                            last = nc.tensor.matmul(psum[:, 7, kv:kv + 1], w1[:, kv, jj, :], pe_cols[:, kv, jj:jj + 1], start=(jj == 0), stop=(jj == 15))
                    last.then_inc(peb_done, 1)
                    pe.wait_ge(peb_copied, 1)
                    pe_compress(nc, pe, 0, 1, B0, PE0, ENG0, buf)

                @block.scalar
                def _(act):
                    with nc.allow_non_contiguous_dma(reason="position embeddings as columns"):
                        for kv in range(2):
                            act.dma_start(pe_cols[:, kv, :], a["cmp_pe"][0, kv].rearrange("(j b) d -> (b d) j", b=2)).then_inc(w_loaded, 16)
                    act.dma_start(w1[:, 1], a["cmp_w1"][0, 1].rearrange("(j p) n -> p j n", p=P)).then_inc(w_loaded, 16)
                    act.wait_ge(peb_copied, 1)
                    act_compress(nc, act, 0, 1, B0, PE0, ACT0, buf, (chunk_loaded, 16))

                @block.vector
                def _(dve):
                    dve.wait_ge(tab_done, 1)
                    nc.vector.tensor_copy(bias_vec[:, :], psum[0:H, 7, 0:384]).then_inc(tab_copied, 1)
                    dve.wait_ge(peb_done, 1)
                    nc.vector.tensor_copy(pe_bias[:, :], psum[:, 7, 0:2]).then_inc(peb_copied, 1)
                    dve_compress(nc, dve, 0, 1, B0, PE0, DVE0, buf, (chunk_loaded, 16), lambda e: None, lambda e, b: None)

        L = PAST + TS
        pages = sb("pages", [1, NS * PAGES], I32)
        nsa_page = sb("nsa_page", [P, 2, PAGES, 2 * P])
        fox_k = sb("fox_k", [P, PAGES, 512])
        fox_v = sb("fox_v", [P, PAGES, 512])
        win_rows = sb("win_rows", [P, 2, WIN // P, 2 * P])
        lf_rows = sb("lf_rows", [P, 2, PAGES, H])
        kT_slc = sb("kT_slc", [P, PAST])
        kT_win = sb("kT_win", [P, WIN])
        lfT = sb("lfT", [H, 2, L])
        ck = sb("ck", [H, L])
        q_nsa = sb("sq_nsa", [P, 2, 32])
        q_fox = sb("sq_fox", [P, 2, 160])
        k_new = sb("k_new", [P, 2, 6, TS])
        v_new = sb("v_new", [TS, 2, 2 * P + 512])
        gates = sb("gates", [32, 2, 3])
        s_cmp, s_win, s_slc, s_fox = sb("s_cmp", [32, NC]), sb("s_win", [32, WIN + TS]), sb("s_slc", [32, L]), sb("s_fox", [32, L])
        p_imp = sb("p_imp", [32, NC])
        stat = sb("stat", [32, 16])
        choice = sb("choice", [32, 4, 16])
        iota = sb("iota", [32, 16])
        bias_s = sb("bias_s", [32, P + TS])
        bias_c = sb("bias_c", [32, NC])
        mask_new = sb("mask_new", [32, 2 * TS])
        overlap = sb("overlap", [NC, 16])
        group_sum = sb("group_sum", [32, 32])
        neg_pick = sb("neg_pick", [H, 32])
        ptT = sb("ptT", [P, 4, 320])
        imp_rows = sb("imp_rows", [32, 16])
        o_nsa = sb("so_nsa", [P, 2, 32])
        o_fox = sb("so_fox", [P, 2, 160])

        jobs = compress_jobs(2) + sample_jobs(0) + sample_jobs(1)
        B = Banks(jobs)
        RN = NS // 2
        PE = Steps(sem("b_pe"), B.order, RN)
        ACTS = Steps(sem("b_act"), compress_act(2) + sample_act(0) + sample_act(1), RN)
        DVE = Steps(sem("b_dve"), compress_dve(2) + sample_dve(0) + sample_dve(1), RN)
        ENG = {"A": ACTS, "V": DVE}
        setup_loaded, setup_set, bias_c_set = sem("b_setup_loaded"), sem("b_setup_set"), sem("b_bias_c_set")
        pages_loaded = sem("b_pages_loaded")
        ch_loaded = sem("b_ch_loaded")
        fk_loaded = sem("b_fk_loaded")
        fv_loaded = sem("b_fv_loaded")
        ns_loaded = [sem(f"b_ns_loaded{b}") for b in range(2)]
        small_loaded = [sem(f"b_small_loaded{b}") for b in range(2)]
        so_stored = [sem(f"b_so_stored{b}") for b in range(2)]
        so_free = [sem(f"b_so_free{b}") for b in range(2)]
        zrow = zT.rearrange("n p t -> (n p) t")

        with nc.Block() as block:
            @block.sync
            def _(sp):
                sp.dma_start(pages[:, :], a["page_table"].rearrange("s (p o) -> o (s p)", o=1)).then_inc(pages_loaded, 16)
                flat = bias_tab.rearrange("h q x -> h (q x)")[:, 127:127 + P * 383].rearrange("h (q x) -> h q x", x=383)
                for h in range(H):
                    sp.dma_start(bias_s[h * TS:(h + 1) * TS, :], flat[h, 0:TS, 0:P + TS]).then_inc(setup_loaded, 16)
                for dst, name in ((mask_new, "mask_new"), (overlap, "overlap"), (group_sum, "group_sum"), (neg_pick, "neg_pick"), (iota, "iota")):
                    sp.dma_start(dst[:, :], c[name]).then_inc(setup_loaded, 16)
                sp.wait_ge(pages_loaded, 16)
                sp.wait_ge(setup_set, 2)

                def load_chunks(i):
                    for b in range(2):
                        for p in range(PAGES):
                            page = sp.value_load(pages[0:1, bass.ds(i * (2 * PAGES) + (b * PAGES + p), 1)], min_val=0, max_val=POOL_PAGES - 1)
                            src = a["cache_nsa_kv"][0, bass.ds(page, 1)].rearrange("o (c j) a g d -> (o c) j (a g d)", j=CS)[:, :, 0:2 * P]
                            sp.dma_start(chunks[b * DH + p * 8:b * DH + (p + 1) * 8, :, :], src).then_inc(ch_loaded, 16)

                def one_round(i):
                    DVE.wait(sp, ("ord", 0), i, back=1)
                    ACTS.wait(sp, ("ord", 1), i, back=1)
                    load_chunks(i)
                    for b in range(2):
                        s = i * 2 + b
                        other = 1 - b
                        col = s * TS + T
                        back = int(b == 0)
                        PE.wait(sp, ("o_fox", b), i, back=1)
                        with nc.allow_non_contiguous_dma(reason="four new tokens"):
                            small = small_loaded[b]
                            for e in range(2):
                                sp.dma_start(q_fox[e * DH:(e + 1) * DH, b].rearrange("p (n x) -> p n x", x=40)[:, :, 4 * e:4 * e + 4],
                                             zT[TILE["q_f"]:TILE["q_f"] + 4, e * DH:(e + 1) * DH, bass.ds(col, TS)].rearrange("n p t -> p n t")).then_inc(small, 16)
                                sp.dma_start(q_nsa[e * DH:(e + 1) * DH, b, 16 * e:16 * e + 16].rearrange("p (r t) -> p r t", t=TS),
                                             zrow[TILE["q_n"] * P + e * 4 * DH:TILE["q_n"] * P + (e + 1) * 4 * DH, bass.ds(col, TS)].rearrange("(r d) t -> d r t", d=DH)).then_inc(small, 16)
                            sp.dma_start(k_new[:, b, 0, :], zT[TILE["nsa_kv"] + 2, :, bass.ds(col, TS)]).then_inc(small, 16)
                            sp.dma_start(k_new[:, b, 1, :], zT[TILE["win_kv"], :, bass.ds(col, TS)]).then_inc(small, 16)
                            sp.dma_start(k_new[:, b, 2:6, :], zT[TILE["fox_kv"]:TILE["fox_kv"] + 4, :, bass.ds(col, TS)].rearrange("n p t -> p n t")).then_inc(small, 16)
                            sp.dma_start(lfT[:, b, PAST:L], gfT[0:H, bass.ds(col, TS)]).then_inc(small, 16)
                            sp.dma_start(gates[:, b, :], gates_dram[:, bass.ds(s, 1), :].rearrange("b o r -> (o r) b")).then_inc(small, 16)
                        sp.dma_start(v_new[:, b, 0:P], nsa_kv_sample[0, bass.ds(s, 1), :, 3].rearrange("o t g d -> (o t) (g d)")).then_inc(small, 16)
                        sp.dma_start(v_new[:, b, P:2 * P], win_kv_sample[0, bass.ds(s, 1), WIN - TS:WIN, 1].rearrange("o t g d -> (o t) (g d)")).then_inc(small, 16)
                        sp.dma_start(v_new[:, b, 2 * P:2 * P + 512], fox_kv_sample[0, bass.ds(s, 1), :, 1].rearrange("o t h d -> (o t) (h d)")).then_inc(small, 16)
                        sp.dma_start(win_rows[:, b], a["state_win_kv"][0, bass.ds(s, 1)].rearrange("o (t p) a g d -> p (o t) (a g d)", p=P)).then_inc(small, 16)
                        for p in range(PAGES):
                            page = sp.value_load(pages[0:1, bass.ds(i * (2 * PAGES) + (b * PAGES + p), 1)], min_val=0, max_val=POOL_PAGES - 1)
                            sp.dma_start(nsa_page[:, b, p, :], a["cache_nsa_kv"][0, bass.ds(page, 1)].rearrange("o p a g d -> (o p) (a g d)")[:, 2 * P:4 * P]).then_inc(ns_loaded[b], 16)
                            sp.dma_start(lf_rows[:, b, p, :], a["cache_fox_logf"][0, bass.ds(page, 1)].rearrange("o p h -> (o p) h")).then_inc(ns_loaded[b], 16)
                            if p == 0:
                                PE.wait(sp, ("kf7", other), i, back=back)
                            src = a["cache_fox_kv"][0, bass.ds(page, 1)].rearrange("o p a h d -> (o p) (a h d)")
                            sp.dma_start(fox_k[:, p, :], src[:, 0:512]).then_inc(fk_loaded, 16)
                        for p in range(PAGES):
                            page = sp.value_load(pages[0:1, bass.ds(i * (2 * PAGES) + (b * PAGES + p), 1)], min_val=0, max_val=POOL_PAGES - 1)
                            if p == 0:
                                PE.wait(sp, ("o_fox", other), i, back=back)
                            src = a["cache_fox_kv"][0, bass.ds(page, 1)].rearrange("o p a h d -> (o p) (a h d)")
                            sp.dma_start(fox_v[:, p, :], src[:, 512:1024]).then_inc(fv_loaded, 16)
                with sp.Fori(0, RN) as i:
                    one_round(i)

            @block.gpsimd
            def _(pool):
                pool.memset(q_nsa[:, :, :], 0.0).then_inc(setup_set, 1)
                pool.memset(q_fox[:, :, :], 0.0).then_inc(setup_set, 1)
                for s in so_free:
                    pool.sem_inc(s, 1)

                def one_round(i):
                    for b in range(2):
                        cols = bass.ds(i * (2 * TS) + (b * TS + T), TS)
                        with nc.allow_non_contiguous_dma(reason="four tokens of each feature"):
                            DVE.wait(pool, ("ev", ("o_nsa", b)), i)
                            for g in range(G):
                                pool.dma_start(oT_dram[g * 4 * DH:(g + 1) * 4 * DH, cols].rearrange("(r d) t -> d r t", d=DH),
                                               o_nsa[g * DH:(g + 1) * DH, b, 16 * g:16 * g + 16].rearrange("p (r t) -> p r t", t=TS)).then_inc(so_stored[b], 16)
                            DVE.wait(pool, ("ev", ("o_fox", b)), i)
                            for e in range(2):
                                pool.dma_start(oT_dram[H * DH:2 * H * DH, cols].rearrange("(n e d) t -> e d n t", e=2, d=DH)[e],
                                               o_fox[e * DH:(e + 1) * DH, b, 0:160].rearrange("p (n x) -> p n x", x=40)[:, :, 4 * e:4 * e + 4]).then_inc(so_stored[b], 16)
                        pool.wait_ge(so_stored[b], i * 64 + 64)
                        pool.sem_inc(so_free[b], 1)
                with pool.Fori(0, RN) as i:
                    one_round(i)

            @block.tensor
            def _(pe):
                PE.start(pe)
                pe.wait_ge(setup_loaded, 16 * 13)

                def start(job, i):
                    before, back = B.before[job]
                    ENG[B.engine[job]].wait(pe, ("ev", before), i, back=back)
                    return psum[:, B.bank[job], :]

                def one_round(i):
                    pe_compress(nc, pe, i, 2, B, PE, ENG, buf)
                    for b in range(2):
                        def wait_ev(name):
                            ENG[B.engine[name, b]].wait(pe, ("ev", (name, b)), i)

                        def turn_pages(name, src, n):
                            dst = start((name, b), i)
                            for q in range(n):
                                last = nc.tensor.transpose(dst[:, q * P:(q + 1) * P], src(q), ident[:, :])
                            PE.done(last, (name, b))

                        def turn_fox(n):
                            half, p = n // 4, n % 4
                            if n == 0:
                                pe.wait_ge(fk_loaded, i * 256 + 128 * (b + 1))
                            turn_pages(f"kf{n}", lambda q: fox_k[:, 4 * half + q, p * P:(p + 1) * P], 4)

                        pe.wait_ge(small_loaded[b], i * 208 + 208)
                        dst = start(("s_cmp", b), i)
                        if b == 0:
                            DVE.wait(pe, ("ev", ("kc",)), i)
                        PE.done(nc.tensor.matmul(dst[0:32, 0:NC], q_nsa[:, b, :], kc[:, b * NC:(b + 1) * NC], start=True, stop=True), ("s_cmp", b))
                        pe.wait_ge(ns_loaded[b], i * 256 + 256)
                        for half in range(2):
                            dst = start((f"lf{half}", b), i)
                            for q in range(4):
                                last = nc.tensor.transpose(dst[0:H, q * P:(q + 1) * P], lf_rows[:, b, 4 * half + q, :], ident[:, :])
                            PE.done(last, (f"lf{half}", b))
                        for half in range(2):
                            turn_pages(f"ks{half}", lambda q: nsa_page[:, b, 4 * half + q, 0:P], 4)
                        turn_pages("kw", lambda q: win_rows[:, b, q, 0:P], 4)

                        def score(name, terms):
                            dst = start((name, b), i)
                            for n, (lhs, rhs) in enumerate(terms):
                                last = nc.tensor.matmul(dst[0:32, 0:rhs.shape[-1]], lhs, rhs, start=(n == 0), stop=(n == len(terms) - 1))
                            PE.done(last, (name, b))

                        wait_ev("kw")
                        score("s_win", [(q_nsa[:, b, :], kT_win[:, :])])
                        score("s_win_new", [(q_nsa[:, b, :], k_new[:, b, 1, :])])
                        score("s_slc0", [(q_nsa[:, b, :], kT_slc[:, 0:512])])
                        score("s_slc1", [(q_nsa[:, b, :], kT_slc[:, 512:1024])])
                        score("s_slc_new", [(q_nsa[:, b, :], k_new[:, b, 0, :])])
                        dst = start(("pt_imp", b), i)
                        DVE.wait(pe, ("norm_cmp", b), i)
                        apart(pe)
                        PE.done(nc.tensor.transpose(dst[0:NC, 0:32], p_imp[:, :], ident[0:32, 0:32]), ("pt_imp", b))
                        for n in range(4):
                            turn_fox(n)
                        dst = start(("imp", b), i)
                        wait_ev("pt_imp")
                        apart(pe)
                        PE.done(nc.tensor.matmul(dst[0:32, 0:16], ptT[0:NC, 0, 0:32], overlap[:, :], start=True, stop=True), ("imp", b))
                        for n in range(4, 8):
                            turn_fox(n)
                        dst = start(("imp_sum", b), i)
                        wait_ev("imp")
                        apart(pe)
                        PE.done(nc.tensor.matmul(dst[0:32, 0:16], group_sum[:, :], imp_rows[:, :], start=True, stop=True), ("imp_sum", b))
                        DVE.wait(pe, ("scan", b), i)
                        for half in range(2):
                            wait_ev(f"kf{4 * half + 2}")
                            wait_ev(f"kf{4 * half + 3}")
                            cols = slice(half * 512, half * 512 + 512)
                            score(f"s_fox{half}", [(q_fox[:, b, 32 * p:32 * p + 32], kT_fox[:, p, cols]) for p in range(4)] + [(neg_pick[:, :], ck[:, cols])])
                        score("s_fox_new", [(q_fox[:, b, 32 * p:32 * p + 32], k_new[:, b, 2 + p, :]) for p in range(4)] + [(neg_pick[:, :], ck[:, PAST:L])])

                        def turn_probs(name, pieces):
                            dst = start((name, b), i)
                            apart(pe)
                            for n, (src, w) in enumerate(pieces):
                                last = nc.tensor.transpose(dst[0:w, n * 32:n * 32 + 32], src, ident[0:32, 0:32])
                            PE.done(last, (name, b))

                        DVE.wait(pe, ("gate_win", b), i)
                        turn_probs("pt_cw", [(s_cmp[:, :], NC)] + [(s_win[:, n * P:(n + 1) * P], P) for n in range(4)] + [(s_win[:, WIN:WIN + TS], TS)])
                        DVE.wait(pe, ("gate_slc", b), i)
                        turn_probs("pt_slc", [(s_slc[:, n * P:(n + 1) * P], P) for n in range(8)] + [(s_slc[:, PAST:L], TS)])
                        dst = start(("o_nsa", b), i)
                        wait_ev("pt_slc")
                        if b == 0:
                            DVE.wait(pe, ("ev", ("vc", 1)), i)
                        apart(pe)
                        terms = [(vc[:, b, :], ptT[0:NC, 1, 0:32])]
                        terms += [(win_rows[:, b, n, P:2 * P], ptT[:, 1, 32 * (n + 1):32 * (n + 2)]) for n in range(4)]
                        terms += [(v_new[:, b, P:2 * P], ptT[0:TS, 1, 160:192])]
                        terms += [(nsa_page[:, b, n, P:2 * P], ptT[:, 2, 32 * n:32 * (n + 1)]) for n in range(8)]
                        terms += [(v_new[:, b, 0:P], ptT[0:TS, 2, 256:288])]
                        for n, (lhs, rhs) in enumerate(terms):
                            last = nc.tensor.matmul(dst[:, 0:32], lhs, rhs, start=(n == 0), stop=(n == len(terms) - 1))
                        PE.done(last, ("o_nsa", b))
                        DVE.wait(pe, ("gate_fox", b), i)
                        turn_probs("pt_fox", [(s_fox[:, n * P:(n + 1) * P], P) for n in range(8)] + [(s_fox[:, PAST:L], TS)])
                        dst = start(("o_fox", b), i)
                        wait_ev("pt_fox")
                        pe.wait_ge(fv_loaded, i * 256 + 128 * (b + 1))
                        for p in range(4):
                            for n in range(9):
                                lhs = fox_v[:, n, p * P:(p + 1) * P] if n < 8 else v_new[:, b, 2 * P + p * P:2 * P + (p + 1) * P]
                                rhs = ptT[:, 3, 32 * n:32 * n + 32] if n < 8 else ptT[0:TS, 3, 256:288]
                                last = nc.tensor.matmul(dst[:, 32 * p:32 * p + 32], lhs, rhs, start=(n == 0), stop=(n == 8))
                        PE.done(last, ("o_fox", b))
                with pe.Fori(0, RN) as i:
                    one_round(i)

            @block.scalar
            def _(act):
                ACTS.start(act)

                def one_round(i):
                    act_compress(nc, act, i, 2, B, PE, ACTS, buf, (ch_loaded, i * 256 + 256))
                    for b in range(2):
                        back = int(b == 0)
                        other = 1 - b

                        def copy(name, dst, n=512, rows=P, free=None):
                            PE.wait(act, (name, b), i)
                            if free:
                                PE.wait(act, (free, other), i, back=back)
                            ACTS.done(nc.scalar.copy(dst, psum[0:rows, B.bank[name, b], 0:n]), ("ev", (name, b)))

                        def exponent(kind, s, at, out=None):
                            DVE.wait(act, (f"max_{kind}", b), i)
                            ACTS.done(nc.scalar.activation(s[:, :] if out is None else out, s[:, :], ACT.Exp, bias=stat[:, at:at + 1], scale=1.0,
                                                           accum_out=stat[:, at + 4:at + 5]), (f"exp_{kind}", b))

                        copy("ks0", kT_slc[:, 0:512], free="s_slc1")
                        copy("ks1", kT_slc[:, 512:1024], free="s_slc1")
                        copy("kw", kT_win[:, :], free="s_win")
                        exponent("cmp", s_cmp, 0)
                        copy("pt_imp", ptT[0:NC, 0, 0:32], n=32, rows=NC, free="imp")
                        exponent("win", s_win, 1)
                        for n in (0, 2):
                            copy(f"kf{n}", kT_fox[:, n % 4, 0:512], free="s_fox1")
                        copy("imp", imp_rows[:, :], n=16, rows=32, free="imp_sum")
                        for n in (4, 6):
                            copy(f"kf{n}", kT_fox[:, n % 4, 512:1024], free="s_fox1")
                        exponent("slc", s_slc, 2)
                        exponent("fox", s_fox, 3)
                        PE.wait(act, ("pt_cw", b), i)
                        PE.wait(act, ("o_nsa", other), i, back=back)
                        nc.scalar.copy(ptT[0:NC, 1, 0:32], psum[0:NC, B.bank["pt_cw", b], 0:32])
                        nc.scalar.copy(ptT[:, 1, 32:160], psum[:, B.bank["pt_cw", b], 32:160])
                        ACTS.done(nc.scalar.copy(ptT[0:TS, 1, 160:192], psum[0:TS, B.bank["pt_cw", b], 160:192]), ("ev", ("pt_cw", b)))
                        for name, k, user in (("pt_slc", 2, "o_nsa"), ("pt_fox", 3, "o_fox")):
                            PE.wait(act, (name, b), i)
                            PE.wait(act, (user, other), i, back=back)
                            nc.scalar.copy(ptT[:, k, 0:256], psum[:, B.bank[name, b], 0:256])
                            ACTS.done(nc.scalar.copy(ptT[0:TS, k, 256:288], psum[0:TS, B.bank[name, b], 256:288]), ("ev", (name, b)))
                with act.Fori(0, RN) as i:
                    one_round(i)

            @block.vector
            def _(dve):
                DVE.start(dve)
                dve.wait_ge(setup_loaded, 16 * 13)
                dve.wait_ge(setup_set, 2)
                nc.vector.memset(bias_c[:, 0:55], 0.0).then_inc(bias_c_set, 1)
                nc.vector.tensor_copy(bias_c[:, 55:63], bias_s[:, 15:P:16]).then_inc(bias_c_set, 1)
                dve.wait_ge(bias_c_set, 2)

                def one_round(i):
                    dve_compress(nc, dve, i, 2, B, PE, DVE, buf, (ch_loaded, i * 256 + 256),
                                 lambda e: PE.wait(e, ("s_cmp", 1), i, back=1), lambda e, b: PE.wait(e, ("o_nsa", 1), i, back=1))
                    for b in range(2):
                        back = int(b == 0)
                        other = 1 - b

                        def bk(name):
                            return psum[:, B.bank[name, b], :]

                        def step(ins, name):
                            DVE.done(ins, (name, b))

                        def after(name):
                            DVE.wait(dve, (name, b), i)

                        def ev(name):
                            return ("ev", (name, b))

                        def top(kind, s, at, last):
                            DVE.wait(dve, last, i)
                            step(nc.vector.tensor_reduce(stat[:, at:at + 1], s[:, :], AX.X, ALU.max, negate=True), f"max_{kind}")

                        PE.wait(dve, ("s_cmp", b), i)
                        PE.wait(dve, ("pt_cw", other), i, back=back)
                        DVE.done(nc.vector.tensor_tensor(s_cmp[:, :], bk("s_cmp")[0:32, 0:NC], bias_c[:, :], ALU.add), ev("s_cmp"))
                        top("cmp", s_cmp, 0, ev("s_cmp"))
                        dve.wait_ge(small_loaded[b], i * 208 + 208)
                        for half in range(2):
                            PE.wait(dve, (f"lf{half}", b), i)
                            DVE.done(nc.vector.tensor_copy(lfT[:, b, half * 512:half * 512 + 512], bk(f"lf{half}")[0:H, :]), ev(f"lf{half}"))
                        DVE.wait(dve, ev("lf1"), i)
                        PE.wait(dve, ("s_fox_new", other), i, back=back)
                        step(nc.vector.tensor_tensor_scan(ck[:, :], env["ones"][0:H, 0:1].to_broadcast([H, L]), lfT[:, b, :], 0.0, ALU.mult, ALU.add), "scan")
                        PE.wait(dve, ("s_win", b), i)
                        w = bk("s_win")
                        nc.vector.tensor_tensor(s_win[:, 0:TS], w[0:32, 0:TS], mask_new[:, TS:2 * TS], ALU.add)
                        nc.vector.tensor_copy(s_win[:, TS:WIN - P], w[0:32, TS:WIN - P])
                        DVE.done(nc.vector.tensor_tensor(s_win[:, WIN - P:WIN], w[0:32, WIN - P:WIN], bias_s[:, 0:P], ALU.add), ev("s_win"))
                        PE.wait(dve, ("s_win_new", b), i)
                        DVE.done(nc.vector.tensor_tensor(s_win[:, WIN:WIN + TS], bk("s_win_new")[0:32, 0:TS], bias_s[:, P:P + TS], ALU.add), ev("s_win_new"))
                        top("win", s_win, 1, ev("s_win_new"))
                        PE.wait(dve, ("s_slc0", b), i)
                        PE.wait(dve, ("pt_slc", other), i, back=back)
                        DVE.done(nc.vector.tensor_copy(s_slc[:, 0:512], bk("s_slc0")[0:32, :]), ev("s_slc0"))
                        PE.wait(dve, ("s_slc1", b), i)
                        w = bk("s_slc1")
                        nc.vector.tensor_copy(s_slc[:, 512:PAST - P], w[0:32, 0:512 - P])
                        DVE.done(nc.vector.tensor_tensor(s_slc[:, PAST - P:PAST], w[0:32, 512 - P:512], bias_s[:, 0:P], ALU.add), ev("s_slc1"))
                        PE.wait(dve, ("s_slc_new", b), i)
                        DVE.done(nc.vector.tensor_tensor(s_slc[:, PAST:L], bk("s_slc_new")[0:32, 0:TS], bias_s[:, P:P + TS], ALU.add), ev("s_slc_new"))
                        ACTS.wait(dve, ("exp_cmp", b), i)
                        step(nc.vector.reciprocal(stat[:, 8:9], stat[:, 4:5]), "rec_cmp")
                        after("rec_cmp")
                        step(nc.vector.tensor_scalar(p_imp[:, :], s_cmp[:, :], stat[:, 8:9], None, ALU.mult), "norm_cmp")
                        after("norm_cmp")
                        step(nc.vector.tensor_scalar(s_cmp[:, :], p_imp[:, :], gates[:, b, 0:1], None, ALU.mult), "gate_cmp")

                        def weigh(kind, s, at, br, fac, gate):
                            ACTS.wait(dve, (f"exp_{kind}", b), i)
                            step(nc.vector.reciprocal(stat[:, at + 8:at + 9], stat[:, at + 4:at + 5]), f"rec_{kind}")
                            after(f"rec_{kind}")
                            if fac:
                                step(nc.vector.tensor_tensor(stat[:, at + 8:at + 9], stat[:, at + 8:at + 9], gates[:, b, br:br + 1], ALU.mult), fac)
                                after(fac)
                            step(nc.vector.tensor_scalar(s[:, :], s[:, :], stat[:, at + 8:at + 9], None, ALU.mult), gate)

                        weigh("win", s_win, 1, 2, "fac_win", "gate_win")

                        def keys(n):
                            half, p = n // 4, n % 4
                            PE.wait(dve, (f"kf{n}", b), i)
                            PE.wait(dve, ("s_fox1", other), i, back=back)
                            DVE.done(nc.vector.tensor_copy(kT_fox[:, p, half * 512:half * 512 + 512], bk(f"kf{n}")), ev(f"kf{n}"))
                        for n in (1, 3, 5, 7):
                            keys(n)
                        PE.wait(dve, ("imp_sum", b), i)
                        cand = choice[:, 0, 0:14]
                        DVE.done(nc.vector.tensor_copy(cand, bk("imp_sum")[0:32, 1:15]), ev("imp_sum"))
                        DVE.wait(dve, ev("imp_sum"), i)
                        step(nc.vector.tensor_reduce(stat[:, 12:13], cand, AX.X, ALU.min), "least")
                        after("least")
                        step(nc.vector.scalar_tensor_tensor(out=choice[:, 1, 0:14], in0=cand, scalar=stat[:, 12:13], in1=iota[:, 1:15],
                                                            op0=ALU.is_equal, op1=ALU.mult), "which")
                        after("which")
                        step(nc.vector.tensor_reduce(stat[:, 13:14], choice[:, 1, 0:14], AX.X, ALU.max), "last")
                        after("last")
                        step(nc.vector.tensor_scalar(choice[:, 2, 0:14], iota[:, 1:15], stat[:, 13:14], NEG, ALU.is_equal, ALU.mult), "drop")
                        after("drop")
                        part = s_slc[:, 64:960].rearrange("p (j n) -> p j n", n=64)
                        step(nc.vector.tensor_tensor(part, part, choice[:, 2, 0:14].unsqueeze(2).to_broadcast([32, 14, 64]), ALU.add), "mask")
                        top("slc", s_slc, 2, ("mask", b))
                        PE.wait(dve, ("s_fox0", b), i)
                        PE.wait(dve, ("pt_fox", other), i, back=back)
                        DVE.done(nc.vector.tensor_copy(s_fox[:, 0:512], bk("s_fox0")[0:32, :]), ev("s_fox0"))
                        PE.wait(dve, ("s_fox1", b), i)
                        DVE.done(nc.vector.tensor_copy(s_fox[:, 512:1024], bk("s_fox1")[0:32, :]), ev("s_fox1"))
                        PE.wait(dve, ("s_fox_new", b), i)
                        DVE.done(nc.vector.tensor_tensor(s_fox[:, PAST:L], bk("s_fox_new")[0:32, 0:TS], mask_new[:, 0:TS], ALU.add), ev("s_fox_new"))
                        top("fox", s_fox, 3, ev("s_fox_new"))
                        weigh("slc", s_slc, 2, 1, "fac_slc", "gate_slc")
                        weigh("fox", s_fox, 3, None, None, "gate_fox")
                        dve.wait_ge(so_free[b], i + 1)
                        PE.wait(dve, ("o_nsa", b), i)
                        DVE.done(nc.vector.tensor_copy(o_nsa[:, b, :], bk("o_nsa")[:, 0:32]), ev("o_nsa"))
                        PE.wait(dve, ("o_fox", b), i)
                        DVE.done(nc.vector.tensor_copy(o_fox[:, b, 0:P], bk("o_fox")[:, 0:P]), ev("o_fox"))
                with dve.Fori(0, RN) as i:
                    one_round(i)


def attention_units():
    units = []
    for i in range(QT):
        units += [("cmp", i, 0, 0), ("slc", i, 0, i), ("win", i, max(0, i - WIN // P), i)]
    units += [("fox", i, 0, i) for i in range(QT)]
    return units


HR = 4
UNITS = attention_units() * HR
NU = len(UNITS)
NH = NU // HR


def head_of(h, u):
    return h * HR + u // NH


LAG = 2


def unit_groups(u):
    kind, i, lo, hi = UNITS[u]
    tiles = list(range(lo, hi + 1))
    return [tiles[n:n + 4] for n in range(0, len(tiles), 4)]


GROUPS = [(u, n) for u in range(NU) for n in range(len(unit_groups(u)))]
GROUP_NO = {g: n for n, g in enumerate(GROUPS)}
NG = len(GROUPS)
assert NG % 4 == 0 and NU % 4 == 0


def last_of_output(u):
    return UNITS[u][0] in ("win", "fox")


def output_no(u):
    return u // NH * 2 * QT + UNITS[u][1] + (QT if UNITS[u][0] == "fox" else 0)


def pe_order():
    names = []
    for step in range(-2, NU + LAG + 1):
        if 0 <= step + 2 < NU:
            names.append(("S", step + 2))
        if 0 <= step - LAG < NU:
            names += [("T", step - LAG, n) for n in range(len(unit_groups(step - LAG)))]
        if 0 <= step - LAG - 1 < NU:
            names += [("PV", step - LAG - 1, n) for n in range(len(unit_groups(step - LAG - 1)))]
    return names


def act_order():
    names = []
    for step in range(NU + 1 + LAG):
        if step < NU:
            names.append(("exp", step))
        if 0 <= step - 1 - LAG:
            names += [("pt", step - 1 - LAG, n) for n in range(len(unit_groups(step - 1 - LAG)))]
    return names


def dve_order():
    names = []
    for step in range(NU + 3 + LAG):
        if step < NU:
            kind, i, lo, hi = UNITS[step]
            names.append(("bias", step))
            if kind == "win" and i - lo == WIN // P:
                names.append(("band", step))
            names.append(("max", step))
            if kind == "cmp":
                names.append(("guard", step))
        if 0 <= step - 1 < NU:
            if UNITS[step - 1][0] == "cmp":
                names.append(("dguard", step - 1))
            names.append(("recip", step - 1))
            if UNITS[step - 1][0] != "fox":
                names.append(("gate", step - 1))
        if 0 <= step - 3 - LAG and last_of_output(step - 3 - LAG):
            names.append(("out", output_no(step - 3 - LAG)))
    return names


def gate_step(u):
    return ("gate", u) if UNITS[u][0] != "fox" else ("recip", u)


def max_step(u):
    return ("guard", u) if UNITS[u][0] == "cmp" else ("max", u)


def build_c(nc, a, o, c, env, mixT):
    (y_prompt, y_sample, nsa_kv_prompt, fox_kv_prompt, logf_prompt, win_kv_prompt,
     nsa_kv_sample, fox_kv_sample, logf_sample, win_kv_sample) = o
    ident, gf_nat, psum = (env[k] for k in ("ident", "gf_nat", "psum"))
    zT, vw_nat, negck, oT_dram, bias_tab, kc_dram, vc_dram = (env[k] for k in ("zT", "vw_nat", "negck", "oT_dram", "bias_tab", "kc_dram", "vc_dram"))
    sem = env["sem"]
    rows = zT.rearrange("n p t -> (n p) t")
    ctx = ExitStack()
    with ctx:
        def sb(name, shape, dt=F32):
            return ctx.enter_context(nc.sbuf_tensor(name, shape, dt))

        bias = sb("bias", [P, H, 2 * P])
        bias_cmp = sb("bias_cmp", [P, H, 119])
        causal = sb("causal", [P, P])
        band = sb("band", [P, P])
        q_nsa = sb("q_nsa", [DH, T])
        k_slc = sb("k_slc", [DH, T])
        k_win = sb("k_win", [DH, T])
        v_slc = sb("v_slc", [P, QT, DH])
        v_win = sb("v_win", [P, QT, DH])
        k_cmp = sb("k_cmp", [DH, NC])
        v_cmp = sb("v_cmp", [NC, DH])
        q_fox = sb("q_fox", [DH + 1, T])
        k_fox = sb("k_fox", [DH + 1, T])
        v_fox = sb("v_fox", [P, QT, DH])
        probs = sb("probs", [P, 4, T])
        probsT = sb("probsT", [P, 4, 512])
        neg_max = sb("neg_max", [P, 4])
        denom = sb("denom", [P, 4])
        factor = sb("factor", [P, 4])
        o_nsa = sb("o_nsa", [DH, T])
        o_fox = sb("o_fox", [DH, T])
        scores = [psum[:, 2 * b:2 * b + 2, :].rearrange("p b n -> p (b n)") for b in range(2)]
        turns = [psum[:, 4 + b, :] for b in range(2)]
        outs = [psum[:, 6 + b, :] for b in range(2)]

        PE = Steps(sem("c_pe"), pe_order(), H // HR)
        ACTS = Steps(sem("c_act"), act_order(), H // HR)
        DVE = Steps(sem("c_dve"), dve_order(), H // HR)
        POOL = Steps(sem("c_pool"), [("scale", u) for u in range(NU)], H // HR)
        tables_loaded = sem("c_tables_loaded")
        bias_cmp_set = sem("bias_cmp_set")
        ones_row_set = sem("ones_row_set")
        nsa_loaded = sem("nsa_loaded")
        fox_loaded = sem("fox_loaded")
        sampled_loaded = sem("c_sampled_loaded")
        o_stored = [sem("o_nsa_stored"), sem("o_fox_stored")]
        block = ctx.enter_context(nc.Block())

        LAST_NSA = NH - QT - 1

        @block.sync
        def _(sp):
            for s in o_stored:
                sp.sem_inc(s, 16)
            flat = bias_tab.rearrange("h q x -> h (q x)")[:, 127:127 + P * 383].rearrange("h (q x) -> q h x", x=383)
            sp.dma_start(bias[:, :, :], flat[:, :, 0:2 * P]).then_inc(tables_loaded, 16)
            sp.dma_start(causal[:, :], c["causal"]).then_inc(tables_loaded, 16)
            sp.dma_start(band[:, :], c["band"]).then_inc(tables_loaded, 16)

            def load_nsa(h):
                g = h // R
                for dst, src in (
                        (q_nsa, rows[bass.ds(h * DH + TILE["q_n"] * P, DH), 0:T]),
                        (k_slc, rows[bass.ds(g * DH + (TILE["nsa_kv"] + 2) * P, DH), 0:T]),
                        (k_win, rows[bass.ds(g * DH + TILE["win_kv"] * P, DH), 0:T]),
                        (k_cmp, kc_dram[bass.ds(g * DH, DH), :])):
                    sp.dma_start(dst[:, :], src).then_inc(nsa_loaded, 16)
                sp.dma_start(v_slc[:, :, :], nsa_kv_prompt[0, 0].rearrange("(t p) a g d -> p t (a g d)", p=P)[:, :, bass.ds(g * DH + 6 * DH, DH)]).then_inc(nsa_loaded, 16)
                sp.dma_start(v_win[:, :, :], vw_nat.rearrange("(t p) d -> p t d", p=P)[:, :, bass.ds(g * DH, DH)]).then_inc(nsa_loaded, 16)
                sp.dma_start(v_cmp[:, :], vc_dram[:, bass.ds(g * DH, DH)]).then_inc(nsa_loaded, 16)

            def load_fox(h):
                sp.dma_start(q_fox[0:DH, :], rows[bass.ds(h * DH + TILE["q_f"] * P, DH), 0:T]).then_inc(fox_loaded, 16)
                sp.dma_start(k_fox[0:DH, :], rows[bass.ds(h * DH + TILE["fox_kv"] * P, DH), 0:T]).then_inc(fox_loaded, 16)
                sp.dma_start(k_fox[DH:DH + 1, :], negck[bass.ds(h, 1), :]).then_inc(fox_loaded, 16)
                sp.dma_start(v_fox[:, :, :], fox_kv_prompt[0, 0].rearrange("(t p) a h d -> p t (a h d)", p=P)[:, :, bass.ds(h * DH + H * DH, DH)]).then_inc(fox_loaded, 16)

            sp.dma_start(mixT[:, :, T:N], oT_dram.rearrange("(k p) n -> p k n", p=P)[:, :, T:N]).then_inc(sampled_loaded, 16)
            load_nsa(0)

            def mix_rows(h, e, first):
                half = slice(e % 2 * DH, (e % 2 + 1) * DH)
                return mixT[half, bass.ds(h * (HR // 2) + (first + e // 2), 1), 0:T].rearrange("p o n -> p (o n)")

            def one_round(h, last):
                for e in range(HR):
                    head = h * HR + e
                    PE.wait(sp, ("PV", (e * NH - 1) % NU, 1), h, back=int(e == 0))
                    load_fox(head)
                    DVE.wait(sp, ("out", (2 * e + 1) * QT - 1), h)
                    sp.dma_start(mix_rows(h, e, 0), o_nsa[:, :]).then_inc(o_stored[0], 16)
                    if not (last and e == HR - 1):
                        PE.wait(sp, ("PV", e * NH + LAST_NSA, 1), h)
                        load_nsa(head + 1)
                    DVE.wait(sp, ("out", (2 * e + 2) * QT - 1), h)
                    sp.dma_start(mix_rows(h, e, H // 2), o_fox[:, :]).then_inc(o_stored[1], 16)

            with sp.Fori(0, H // HR - 1) as h:
                one_round(h, False)
            one_round(H // HR - 1, True)
            sp.wait_ge(sampled_loaded, 16)
            for s in o_stored:
                sp.wait_ge(s, 16 + 16 * H)

        @block.tensor
        def _(pe):
            PE.start(pe)
            pe.wait_ge(ones_row_set, 1)

            def one_round(h):
                def scores_of(u):
                    kind, i, lo, hi = UNITS[u]
                    if u % NH == 0:
                        pe.wait_ge(nsa_loaded, head_of(h, u) * 112 + 112)
                    if kind == "fox" and i == 0:
                        pe.wait_ge(fox_loaded, head_of(h, u) * 64 + 64)
                    ACTS.wait(pe, ("exp", (u - 2) % NU), h, back=int(u < 2))
                    q = (q_fox if kind == "fox" else q_nsa)[:, i * P:(i + 1) * P]
                    k = {"cmp": k_cmp, "slc": k_slc, "win": k_win, "fox": k_fox}[kind]
                    first, n = lo * P, (hi - lo + 1) * P if kind != "cmp" else NC
                    for at in range(0, n, 512):
                        w = min(512, n - at)
                        last = nc.tensor.matmul(scores[u % 2][:, at:at + w], q, k[:, first + at:first + at + w], start=True, stop=True)
                    PE.done(last, ("S", u))

                def turn(u):
                    POOL.wait(pe, ("scale", u), h)
                    for n, tiles in enumerate(unit_groups(u)):
                        g = GROUP_NO[u, n]
                        before = GROUPS[(g - 2) % NG]
                        ACTS.wait(pe, ("pt", *before), h, back=int(g < 2))
                        if UNITS[u][0] == "cmp":
                            apart(pe)
                        for j, t in enumerate(tiles):
                            w = NC if UNITS[u][0] == "cmp" else P
                            at = (t - UNITS[u][2]) * P
                            last = nc.tensor.transpose(turns[g % 2][0:w, j * P:(j + 1) * P], probs[:, u % 4, at:at + w], ident[:, :])
                        PE.done(last, ("T", u, n))

                def values(u):
                    kind, i, lo, hi = UNITS[u]
                    out = output_no(u)
                    if kind in ("cmp", "fox"):
                        DVE.wait(pe, ("out", (out - 2) % (HR * 2 * QT)), h, back=int(out < 2))
                    v = {"cmp": v_cmp, "slc": v_slc, "win": v_win, "fox": v_fox}[kind]
                    for n, tiles in enumerate(unit_groups(u)):
                        g = GROUP_NO[u, n]
                        ACTS.wait(pe, ("pt", u, n), h)
                        if kind == "cmp":
                            apart(pe)
                        for j, t in enumerate(tiles):
                            if kind == "cmp":
                                lhs, rhs = v[:, :], probsT[0:NC, g % 4, 0:P]
                            else:
                                lhs, rhs = v[:, t, :], probsT[:, g % 4, j * P:(j + 1) * P]
                            last = nc.tensor.matmul(outs[out % 2][0:DH, 0:P], lhs, rhs, start=(kind in ("cmp", "fox") and t == lo),
                                                    stop=(last_of_output(u) and t == hi))
                        PE.done(last, ("PV", u, n))

                for step in range(-2, NU + LAG + 1):
                    if 0 <= step + 2 < NU:
                        scores_of(step + 2)
                    if 0 <= step - LAG < NU:
                        turn(step - LAG)
                    if 0 <= step - LAG - 1 < NU:
                        values(step - LAG - 1)
            with pe.Fori(0, H // HR) as h:
                one_round(h)

        @block.scalar
        def _(act):
            ACTS.start(act)

            def one_round(h):
                for step in range(NU + 1 + LAG):
                    if step < NU:
                        u = step
                        kind, i, lo, hi = UNITS[u]
                        n = (hi - lo + 1) * P if kind != "cmp" else NC
                        DVE.wait(act, max_step(u), h)
                        old = (u - 4) % NU
                        PE.wait(act, ("T", old, len(unit_groups(old)) - 1), h, back=int(u < 4))
                        ACTS.done(nc.scalar.activation(probs[:, u % 4, 0:n], scores[u % 2][:, 0:n], ACT.Exp, bias=neg_max[:, u % 4:u % 4 + 1],
                                                       scale=1.0, accum_out=denom[:, u % 4:u % 4 + 1]), ("exp", u))
                    if step >= 1 + LAG:
                        u = step - 1 - LAG
                        for n, tiles in enumerate(unit_groups(u)):
                            g = GROUP_NO[u, n]
                            PE.wait(act, ("T", u, n), h)
                            PE.wait(act, ("PV", *GROUPS[(g - 4) % NG]), h, back=int(g < 4))
                            w = NC if UNITS[u][0] == "cmp" else P
                            ACTS.done(nc.scalar.copy(probsT[0:w, g % 4, 0:len(tiles) * P], turns[g % 2][0:w, 0:len(tiles) * P]), ("pt", u, n))
            with act.Fori(0, H // HR) as h:
                one_round(h)

        @block.gpsimd
        def _(pool):
            pool.memset(q_fox[DH:DH + 1, :], 1.0).then_inc(ones_row_set, 1)
            POOL.start(pool)

            def one_round(h):
                for u in range(NU):
                    kind, i, lo, hi = UNITS[u]
                    n = (hi - lo + 1) * P if kind != "cmp" else NC
                    DVE.wait(pool, gate_step(u), h)
                    apart(pool)
                    POOL.done(nc.gpsimd.tensor_scalar(probs[:, u % 4, 0:n], probs[:, u % 4, 0:n], factor[:, u % 4:u % 4 + 1], None, ALU.mult),
                              ("scale", u))
            with pool.Fori(0, H // HR) as h:
                one_round(h)

        @block.vector
        def _(dve):
            DVE.start(dve)
            dve.wait_ge(tables_loaded, 48)
            nc.vector.memset(bias_cmp[:, :, 0:47], 0.0).then_inc(bias_cmp_set, 1)
            nc.vector.memset(bias_cmp[:, :, 63:119], NEG).then_inc(bias_cmp_set, 1)
            nc.vector.tensor_copy(bias_cmp[:, :, 47:63], bias[:, :, 15::16]).then_inc(bias_cmp_set, 1)
            dve.wait_ge(bias_cmp_set, 3)

            def one_round(h):
                def shift(u):
                    kind, i, lo, hi = UNITS[u]
                    s = scores[u % 2]
                    PE.wait(dve, ("S", u), h)
                    if kind == "cmp":
                        at, n, add = 0, NC, bias_cmp[:, bass.ds(head_of(h, u), 1), 56 - 8 * i:56 - 8 * i + NC]
                    elif kind == "fox":
                        at, n, add = i * P, P, causal[:, :]
                    elif i == 0:
                        at, n, add = 0, P, bias[:, bass.ds(head_of(h, u), 1), P:2 * P]
                    else:
                        at, n, add = (i - 1 - lo) * P, 2 * P, bias[:, bass.ds(head_of(h, u), 1), :]
                    if kind != "fox":
                        add = add.rearrange("p o n -> p (o n)")
                    DVE.done(nc.vector.tensor_tensor(s[:, at:at + n], s[:, at:at + n], add, ALU.add), ("bias", u))
                    if kind == "win" and i - lo == WIN // P:
                        DVE.done(nc.vector.tensor_tensor(s[:, 0:P], s[:, 0:P], band[:, :], ALU.add), ("band", u))
                        DVE.wait(dve, ("band", u), h)
                    DVE.wait(dve, ("bias", u), h)
                    n = (hi - lo + 1) * P if kind != "cmp" else NC
                    m = neg_max[:, u % 4:u % 4 + 1]
                    DVE.done(nc.vector.tensor_reduce(m, s[:, 0:n], AX.X, ALU.max, negate=True), ("max", u))
                    if kind == "cmp":
                        DVE.wait(dve, ("max", u), h)
                        DVE.done(nc.vector.tensor_scalar(m, m, -0.1 * NEG, None, ALU.min), ("guard", u))

                def weigh(u):
                    kind, i, lo, hi = UNITS[u]
                    ACTS.wait(dve, ("exp", u), h)
                    POOL.wait(dve, ("scale", (u - 4) % NU), h, back=int(u < 4))
                    d, f = denom[:, u % 4:u % 4 + 1], factor[:, u % 4:u % 4 + 1]
                    if kind == "cmp":
                        DVE.done(nc.vector.tensor_scalar(d, d, 1e-30, None, ALU.max), ("dguard", u))
                        DVE.wait(dve, ("dguard", u), h)
                    DVE.done(nc.vector.reciprocal(f, d), ("recip", u))
                    if kind != "fox":
                        br = ("cmp", "slc", "win").index(kind)
                        DVE.wait(dve, ("recip", u), h)
                        DVE.done(nc.vector.tensor_tensor(f, f, gf_nat[:, i, bass.ds(head_of(h, u) + (GATE0 + br * H), 1)], ALU.mult), ("gate", u))

                for step in range(NU + 3 + LAG):
                    if step < NU:
                        shift(step)
                    if 0 <= step - 1 < NU:
                        weigh(step - 1)
                    if 0 <= step - 3 - LAG and last_of_output(step - 3 - LAG):
                        u = step - 3 - LAG
                        out = output_no(u)
                        i = UNITS[u][1]
                        PE.wait(dve, ("PV", u, len(unit_groups(u)) - 1), h)
                        if i == 0:
                            dve.wait_ge(o_stored[out // QT % 2], head_of(h, u) * 16 + 16)
                        dst = (o_nsa if UNITS[u][0] == "win" else o_fox)[:, i * P:(i + 1) * P]
                        DVE.done(nc.vector.tensor_copy(dst, outs[out % 2][0:DH, 0:P]), ("out", out))
            with dve.Fori(0, H // HR) as h:
                one_round(h)


class RmsNorm:

    def __init__(self, env, prefix, n, banks, sums=True):
        s = env["sem"]
        self.nc, self.env, self.n, self.banks = env["nc"], env, n, banks
        if sums:
            self.squared, self.summed = s(prefix + "_squared"), s(prefix + "_summed")
        self.total = s(prefix + "_total")
        self.rooted, self.inverted = s(prefix + "_rooted"), s(prefix + "_inverted")

    def act(self, act, src, ready, sq, rstd, free=None):
        nc = self.nc
        for k in range(self.n):
            ready(act, k)
            if k >= 2:
                act.wait_ge(self.summed, k - 1)
            nc.scalar.activation(sq[:, k % 2, :], src(k), ACT.Square).then_inc(self.squared, 1)
        self.root_act(act, rstd, free)

    def root_act(self, act, rstd, free=None):
        nc = self.nc
        act.wait_ge(self.total, 1)
        if free:
            free(act)
        for b in range(3):
            last = nc.scalar.activation(rstd[:, b * NB:(b + 1) * NB], self.env["psum"][:, self.banks + b, 0:NB], ACT.Sqrt,
                                        bias=self.env["eps"][:, 0:1], scale=1.0 / (self.n * P))
        last.then_inc(self.rooted, 1)

    def dve(self, dve, sq, ssum, rstd):
        nc = self.nc
        for k in range(self.n):
            dve.wait_ge(self.squared, k + 1)
            if k == 0:
                nc.vector.tensor_copy(ssum[:, :], sq[:, 0, :]).then_inc(self.summed, 1)
            else:
                dve.wait_ge(self.summed, k)
                nc.vector.tensor_tensor(ssum[:, :], ssum[:, :], sq[:, k % 2, :], ALU.add).then_inc(self.summed, 1)
        dve.wait_ge(self.rooted, 1)
        nc.vector.reciprocal(rstd[:, :], rstd[:, :]).then_inc(self.inverted, 1)
        dve.wait_ge(self.inverted, 1)

    def pe(self, pe, ssum):
        self.total_pe(pe, ssum, self.summed, self.n)

    def total_pe(self, pe, ssum, summed, count):
        nc = self.nc
        pe.wait_ge(summed, count)
        for b in range(3):
            last = nc.tensor.matmul(self.env["psum"][:, self.banks + b, 0:NB], self.env["ones"][:, :], ssum[:, b * NB:(b + 1) * NB],
                                    start=True, stop=True)
        last.then_inc(self.total, 1)


def build_d(nc, a, env, xT, m_hi, m_lo):
    x_dram, x1_dram, gains, psum, sem = (env[k] for k in ("x_dram", "x1_dram", "gains", "psum", "sem"))
    ctx = ExitStack()
    with ctx:
        def sb(name, shape, dt=F32):
            return ctx.enter_context(nc.sbuf_tensor(name, shape, dt))

        yT = sb("d_yT", [P, KD, N])
        sq = sb("d_sq", [P, 2, N])
        ssum = sb("d_ssum", [P, N])
        ssum2 = sb("d_ssum2", [P, N])
        rstd = sb("d_rstd", [P, 2, N])
        w_ring = sb("d_w_ring", [P, 2, KD, P])
        w_hi = sb("d_w_hi", [P, 2, KD, P], F32R)
        w_lo = sb("d_w_lo", [P, 2, KD, P], F32R)
        x_loaded = [sem(f"d_x_loaded{i}") for i in range(2)]
        w_loaded = [sem(f"d_w_loaded{s}") for s in range(2)]
        mix_normed, mix_high, mix_split = sem("d_mix_normed"), sem("d_mix_high"), sem("d_mix_split")
        w_high, w_split = sem("d_w_high"), sem("d_w_split")
        y_done, y_copied, y_squared, y_summed = (sem("d_y_" + n) for n in ("done", "copied", "squared", "summed"))
        x_scaled, x_added, x_stored = sem("d_x_scaled"), sem("d_x_added"), sem("d_x_stored")
        hf_normed, hf_high, hf_split = sem("d_hf_normed"), sem("d_hf_high"), sem("d_hf_split")
        sum_cleared = sem("d_sum_cleared")
        norm_n, norm_f = RmsNorm(env, "d_norm_n", 4, 0), RmsNorm(env, "d_norm_f", 4, 3)
        norm_y, norm_x = RmsNorm(env, "d_norm_y", KD, 0, sums=False), RmsNorm(env, "d_norm_x", KD, 3)
        W = a["w_o"][0].rearrange("(k p) n -> p k n", p=P)
        with nc.Block() as block:
            @block.sync
            def _(sp):
                for s in range(2):
                    sp.dma_start(w_ring[:, s], W[:, :, s * P:(s + 1) * P]).then_inc(w_loaded[s], 16)
                for i in range(2):
                    sp.wait_ge(mix_normed, 4 * i + 4)
                    sp.dma_start(xT[:, 4 * i:4 * i + 4, :], x_dram[:, 4 * i:4 * i + 4, :]).then_inc(x_loaded[i], 16)
                with sp.Fori(0, KD // 2 - 1) as i:
                    for s in range(2):
                        sp.wait_ge(w_split, i * 2 + (s + 1))
                        sp.dma_start(w_ring[:, s], W[:, :, bass.ds(i * 256 + (2 + s) * P, P)]).then_inc(w_loaded[s], 16)
                sp.wait_ge(x_added, KD)
                sp.dma_start(x1_dram[:, :, :], xT[:, :, :]).then_inc(x_stored, 16)
                sp.wait_ge(x_stored, 16)

            @block.tensor
            def _(pe):
                pe.sem_inc(y_done, 2)
                norm_n.pe(pe, ssum)
                norm_f.pe(pe, ssum2)
                pe.wait_ge(norm_f.rooted, 1)
                pe.wait_ge(w_split, 1)
                for k in range(KD):
                    pe.wait_ge(mix_split, k + 1)
                    for b in range(3):
                        tok = slice(b * NB, (b + 1) * NB)
                        last = product(nc, psum[:, b, 0:NB], w_hi[:, 0, k, :], w_lo[:, 0, k, :],
                                       m_hi[:, k, tok], m_lo[:, k, tok], k == 0, k == KD - 1)
                last.then_inc(y_done, 1)

                def tiles(i, slots):
                    for s in slots:
                        pe.wait_ge(w_split, i * 2 + (s + 1))
                        pe.wait_ge(y_copied, i * 2 + (s + 1))
                        pe.wait_ge(y_squared, i * 2 + (s + 1))
                        for b in range(3):
                            for k in range(KD):
                                tok = slice(b * NB, (b + 1) * NB)
                                last = product(nc, psum[:, 3 * s + b, 0:NB], w_hi[:, s, k, :], w_lo[:, s, k, :],
                                               m_hi[:, k, tok], m_lo[:, k, tok], k == 0, k == KD - 1)
                        last.then_inc(y_done, 1)
                tiles(0, (1,))
                with pe.Fori(0, KD // 2 - 1) as i:
                    tiles(i + 1, (0, 1))
                pe.wait_ge(y_copied, KD + 2)
                pe.wait_ge(y_squared, KD + 2)
                norm_y.total_pe(pe, ssum, y_summed, KD + 2)
                norm_x.pe(pe, ssum2)

            @block.scalar
            def _(act):
                norm_n.act(act, lambda k: xT[:, k, :], lambda e, k: None, sq, rstd[:, 0, :])
                norm_f.act(act, lambda k: xT[:, 4 + k, :],
                           lambda e, k: k < 2 and e.wait_ge(norm_n.summed, k + 3), sq, rstd[:, 1, :])
                for k in range(KD):
                    act.wait_ge(mix_normed, k + 1)
                    nc.scalar.copy(m_hi[:, k, :], sq[:, k % 2, :]).then_inc(mix_high, 1)
                act.wait_ge(mix_split, KD)
                act.sem_inc(y_copied, 2)
                act.sem_inc(y_squared, 2)
                with act.Fori(0, KD // 2) as i:
                    for s in range(2):
                        act.wait_ge(y_done, i * 2 + (s + 3))
                        for b in range(3):
                            last = nc.scalar.copy(yT[:, bass.ds(i * 2 + s, 1), b * NB:(b + 1) * NB].rearrange("p o n -> p (o n)"),
                                                  psum[:, 3 * s + b, 0:NB])
                        last.then_inc(y_copied, 1)
                        act.wait_ge(y_summed, i * 2 + (s + 1))
                        for b in range(3):
                            last = nc.scalar.activation(sq[:, s, b * NB:(b + 1) * NB], psum[:, 3 * s + b, 0:NB], ACT.Square)
                        last.then_inc(y_squared, 1)
                norm_y.root_act(act, rstd[:, 0, :], lambda e: e.wait_ge(mix_normed, KD))
                norm_x.act(act, lambda k: xT[:, k, :],
                           lambda e, k: (e.wait_ge(x_added, k + 1), k == 0 and e.wait_ge(y_summed, KD + 2)), sq, rstd[:, 1, :])
                for k in range(KD):
                    act.wait_ge(hf_normed, k + 1)
                    nc.scalar.copy(m_hi[:, k, :], sq[:, k % 2, :]).then_inc(hf_high, 1)

            @block.vector
            def _(dve):
                def parts(k, normed, high, split, gain, scale):
                    if k >= 2:
                        dve.wait_ge(split, k - 1)
                    if k < KD:
                        nc.vector.scalar_tensor_tensor(out=sq[:, k % 2, :], in0=xT[:, k, :], scalar=gains[:, gain, k:k + 1], in1=scale,
                                                       op0=ALU.mult, op1=ALU.mult).then_inc(normed, 1)
                    if k >= 1:
                        j = k - 1
                        dve.wait_ge(high, j + 1)
                        nc.vector.tensor_tensor(m_lo[:, j, :], sq[:, j % 2, :], m_hi[:, j, :].bitcast(F32), ALU.subtract).then_inc(split, 1)

                def split_w(n, s, load):
                    dve.wait_ge(w_loaded[s], load)
                    dve.wait_ge(y_done, n + 1)
                    nc.vector.tensor_copy(w_hi[:, s], w_ring[:, s]).then_inc(w_high, 1)
                    dve.wait_ge(w_high, n + 1)
                    nc.vector.tensor_tensor(w_lo[:, s], w_ring[:, s], w_hi[:, s].bitcast(F32), ALU.subtract).then_inc(w_split, 1)

                norm_n.dve(dve, sq, ssum, rstd[:, 0, :])
                norm_f.dve(dve, sq, ssum2, rstd[:, 1, :])
                split_w(0, 0, 16)
                for k in range(KD + 1):
                    parts(k, mix_normed, mix_high, mix_split, 4, rstd[:, min(k, KD - 1) // 4, :])
                split_w(1, 1, 16)

                def add_square(n, s):
                    dve.wait_ge(y_squared, n + 3)
                    dve.wait_ge(y_summed, n + 2)
                    nc.vector.tensor_tensor(ssum[:, :], ssum[:, :], sq[:, s, :], ALU.add).then_inc(y_summed, 1)

                dve.wait_ge(norm_n.total, 1)
                dve.sem_inc(y_summed, 2)
                nc.vector.memset(ssum[:, :], 0.0).then_inc(sum_cleared, 1)
                dve.wait_ge(sum_cleared, 1)
                with dve.Fori(0, KD // 2 - 1) as i:
                    for s in range(2):
                        split_w(i * 2 + (s + 2), s, i * 16 + 32)
                        add_square(i * 2 + s, s)
                for s in range(2):
                    add_square(KD - 2 + s, s)
                dve.wait_ge(norm_y.rooted, 1)
                nc.vector.reciprocal(rstd[:, 0, :], rstd[:, 0, :]).then_inc(norm_y.inverted, 1)
                dve.wait_ge(norm_y.inverted, 1)
                for k in range(KD + 1):
                    if k < KD:
                        nc.vector.scalar_tensor_tensor(out=yT[:, k, :], in0=yT[:, k, :], scalar=gains[:, 1, k:k + 1], in1=rstd[:, 0, :],
                                                       op0=ALU.mult, op1=ALU.mult).then_inc(x_scaled, 1)
                    if k >= 1:
                        j = k - 1
                        dve.wait_ge(x_scaled, j + 1)
                        dve.wait_ge(x_loaded[j // 4], 16)
                        nc.vector.tensor_tensor(xT[:, j, :], xT[:, j, :], yT[:, j, :], ALU.add).then_inc(x_added, 1)
                norm_x.dve(dve, sq, ssum2, rstd[:, 1, :])
                for k in range(KD + 1):
                    parts(k, hf_normed, hf_high, hf_split, 2, rstd[:, 1, :])
                dve.wait_ge(hf_split, KD)


def build_f(nc, a, o, env, yT):
    x1_dram, gains, psum, sem, ident = (env[k] for k in ("x1_dram", "gains", "psum", "sem", "ident"))
    y_prompt, y_sample = o[0], o[1]
    ctx = ExitStack()
    with ctx:
        def sb(name, shape, dt=F32):
            return ctx.enter_context(nc.sbuf_tensor(name, shape, dt))

        xT = sb("f_xT", [P, KD, N])
        sq = sb("f_sq", [P, 2, N])
        ssum = sb("f_ssum", [P, N])
        rstd = sb("f_rstd", [P, N])
        y_nat = sb("y_nat", [P, QT + 1, D])
        x_loaded = sem("f_x_loaded")
        norm = RmsNorm(env, "f_norm", KD, 0)
        scaled, added, turned, copied, stored = (sem("f_" + n) for n in ("scaled", "added", "turned", "copied", "stored"))
        with nc.Block() as block:
            @block.sync
            def _(sp):
                sp.dma_start(xT[:, :, :], x1_dram[:, :, :]).then_inc(x_loaded, 16)
                for t in range(QT + 1):
                    sp.wait_ge(copied, 2 * t + 2)
                    if t < QT:
                        sp.dma_start(y_prompt[0, t * P:(t + 1) * P, :], y_nat[:, t, :]).then_inc(stored, 16)
                    else:
                        sp.dma_start(y_sample.rearrange("s t d -> (s t) d"), y_nat[0:S, t, :]).then_inc(stored, 16)
                sp.wait_ge(stored, 16 * (QT + 1))

            @block.tensor
            def _(pe):
                norm.pe(pe, ssum)
                for t in range(QT + 1):
                    n = P if t < QT else S
                    for b in range(2):
                        j = 2 * t + b
                        if j >= 4:
                            pe.wait_ge(copied, j - 3)
                        for q in range(4):
                            k = 4 * b + q
                            if t == 0:
                                pe.wait_ge(added, k + 1)
                            last = nc.tensor.transpose(psum[0:n, 4 + j % 4, q * P:(q + 1) * P], xT[:, k, t * P:t * P + n], ident[:, :])
                        last.then_inc(turned, 1)

            @block.scalar
            def _(act):
                norm.act(act, lambda k: yT[:, k, :], lambda e, k: None, sq, rstd[:, :])

            @block.vector
            def _(dve):
                norm.dve(dve, sq, ssum, rstd[:, :])
                dve.wait_ge(x_loaded, 16)
                for k in range(KD):
                    nc.vector.scalar_tensor_tensor(out=yT[:, k, :], in0=yT[:, k, :], scalar=gains[:, 3, k:k + 1], in1=rstd[:, :],
                                                   op0=ALU.mult, op1=ALU.mult).then_inc(scaled, 1)
                for k in range(KD):
                    dve.wait_ge(scaled, k + 1)
                    nc.vector.tensor_tensor(xT[:, k, :], xT[:, k, :], yT[:, k, :], ALU.add).then_inc(added, 1)
                for t in range(QT + 1):
                    n = P if t < QT else S
                    for b in range(2):
                        j = 2 * t + b
                        dve.wait_ge(turned, j + 1)
                        nc.vector.tensor_copy(y_nat[0:n, t, b * 512:(b + 1) * 512], psum[0:n, 4 + j % 4, :]).then_inc(copied, 1)


def build_e(nc, a, env, hf_hi, hf_lo, yT):
    psum, sem = env["psum"], env["sem"]
    ctx = ExitStack()
    with ctx:
        hT = ctx.enter_context(nc.sbuf_tensor("hT", [P, FT, N], F32))
        with ExitStack() as one:
            def sb(name, shape, dt=F32):
                return one.enter_context(nc.sbuf_tensor(name, shape, dt))
            silu = sb("silu", [P, N])
            ring = sb("gu_ring", [P, 2, KD, P])
            w_hi = sb("gu_hi", [P, 2, KD, P], F32R)
            w_lo = sb("gu_lo", [P, 2, KD, P], F32R)
            loaded = [sem("e_gate_loaded"), sem("e_up_loaded")]
            high = [sem("e_gate_high"), sem("e_up_high")]
            split = [sem("e_gate_split"), sem("e_up_split")]
            done = [sem("e_gate_done"), sem("e_up_done")]
            silu_ready, h_ready = sem("e_silu_ready"), sem("e_h_ready")
            W = [a[n][0].rearrange("(k p) n -> p k n", p=P) for n in ("w_ffn_gate", "w_ffn_up")]
            with nc.Block() as block:
                @block.sync
                def _(sp):
                    with sp.Fori(0, FT) as f:
                        for s in range(2):
                            sp.wait_ge(split[s], f + 1)
                            sp.dma_start(ring[:, s], W[s][:, :, bass.ds(f * P, P)]).then_inc(loaded[s], 16)

                @block.tensor
                def _(pe):
                    for s in range(2):
                        pe.sem_inc(done[s], 1)
                    with pe.Fori(0, FT) as f:
                        for s in range(2):
                            pe.wait_ge(split[s], f + 2)
                            pe.wait_ge((silu_ready, h_ready)[s], f + 1)
                            for b in range(3):
                                for k in range(KD):
                                    tok = slice(b * NB, (b + 1) * NB)
                                    last = product(nc, psum[:, 3 * s + b, 0:NB], w_hi[:, s, k, :], w_lo[:, s, k, :],
                                                   hf_hi[:, k, tok], hf_lo[:, k, tok], k == 0, k == KD - 1)
                            last.then_inc(done[s], 1)

                @block.scalar
                def _(act):
                    act.sem_inc(silu_ready, 1)
                    with act.Fori(0, FT) as f:
                        act.wait_ge(done[0], f + 2)
                        act.wait_ge(h_ready, f + 1)
                        for b in range(3):
                            last = nc.scalar.activation(silu[:, b * NB:(b + 1) * NB], psum[:, b, 0:NB], ACT.Silu)
                        last.then_inc(silu_ready, 1)

                @block.vector
                def _(dve):
                    dve.sem_inc(h_ready, 1)
                    for s in range(2):
                        dve.sem_inc(split[s], 1)

                    def split_tile(f, s):
                        dve.wait_ge(loaded[s], f * 16 + 16)
                        dve.wait_ge(done[s], f + 1)
                        nc.vector.tensor_copy(w_hi[:, s], ring[:, s]).then_inc(high[s], 1)
                        dve.wait_ge(high[s], f + 1)
                        nc.vector.tensor_tensor(w_lo[:, s], ring[:, s], w_hi[:, s].bitcast(F32), ALU.subtract).then_inc(split[s], 1)

                    def gated(f):
                        dve.wait_ge(done[1], f + 2)
                        dve.wait_ge(silu_ready, f + 2)
                        for b in range(3):
                            dst = hT[:, f, :] if isinstance(f, int) else hT[:, bass.ds(f, 1), :].rearrange("p o n -> p (o n)")
                            last = nc.vector.tensor_tensor(dst[:, b * NB:(b + 1) * NB], psum[:, 3 + b, 0:NB], silu[:, b * NB:(b + 1) * NB], ALU.mult)
                        last.then_inc(h_ready, 1)

                    split_tile(0, 0)
                    split_tile(0, 1)
                    with dve.Fori(0, FT - 1) as f:
                        split_tile(f + 1, 0)
                        gated(f)
                        split_tile(f + 1, 1)
                    gated(FT - 1)
                    dve.wait_ge(h_ready, FT + 1)
        with ExitStack() as two:
            def sb(name, shape, dt=F32):
                return two.enter_context(nc.sbuf_tensor(name, shape, dt))
            FG = 2
            ring = sb("down_ring", [P, 2, FG, 2 * P])
            w_hi = sb("down_hi", [P, 2, FG, 2 * P], F32R)
            w_lo = sb("down_lo", [P, 2, FG, 2 * P], F32R)
            h_hi = sb("h_hi", [P, 2, N], F32R)
            h_lo = sb("h_lo", [P, 2, N], F32R)
            loaded = [sem(f"e_down_loaded{s}") for s in range(2)]
            w_high, w_split, h_high, h_split, used = (sem("e_" + n) for n in ("w_high", "w_split", "h_high", "h_split", "used"))
            y_copied = [sem("e_y_copied_act"), sem("e_y_copied_dve")]
            W = a["w_ffn_down"][0].rearrange("(k p) n -> p k n", p=P)
            STEPS = FT // FG
            with nc.Block() as block:
                def groups(i):
                    for half in range(2):
                        for step in range(STEPS):
                            j = half * STEPS + step
                            yield half, step, j % 2, i * (2 * STEPS) + j

                @block.sync
                def _(sp):
                    with sp.Fori(0, 2) as i:
                        for half, step, s, g in groups(i):
                            sp.wait_ge(w_split, g + 1)
                            sp.dma_start(ring[:, s], W[:, FG * step:FG * step + FG, bass.ds(i * 512 + half * 256, 256)]).then_inc(loaded[s], 16)

                @block.tensor
                def _(pe):
                    pe.sem_inc(used, 2 * FG)
                    with pe.Fori(0, 2) as i:
                        for half, step, s, g in groups(i):
                            pe.wait_ge(w_split, g + 3)
                            if step == 0:
                                for e in range(2):
                                    pe.wait_ge(y_copied[e], i * 2 + half + 1)
                            for q in range(FG):
                                f = FG * step + q
                                pe.wait_ge(h_split, g * FG + (q + 1))
                                for c in range(2):
                                    for b in range(3):
                                        tok = slice(b * NB, (b + 1) * NB)
                                        col = slice(c * P, (c + 1) * P)
                                        last = product(nc, psum[:, 3 * c + b, 0:NB], w_hi[:, s, q, col], w_lo[:, s, q, col],
                                                       h_hi[:, q, tok], h_lo[:, q, tok], f == 0, f == FT - 1)
                                last.then_inc(used, 1)

                @block.scalar
                def _(act):
                    act.sem_inc(y_copied[0], 1)
                    with act.Fori(0, 2) as i:
                        for half, step, s, g in groups(i):
                            for q in range(FG):
                                act.wait_ge(used, g * FG + (q + 1 + FG))
                                nc.scalar.copy(h_hi[:, q, :], hT[:, FG * step + q, :]).then_inc(h_high, 1)
                            if step == STEPS - 1:
                                act.wait_ge(used, g * FG + 3 * FG)
                                for b in range(3):
                                    last = nc.scalar.copy(yT[:, bass.ds(i * 4 + half * 2, 1), b * NB:(b + 1) * NB].rearrange("p o n -> p (o n)"),
                                                          psum[:, b, 0:NB])
                                last.then_inc(y_copied[0], 1)

                @block.vector
                def _(dve):
                    dve.sem_inc(y_copied[1], 1)
                    dve.sem_inc(w_split, 2)
                    with dve.Fori(0, 2) as i:
                        for half, step, s, g in groups(i):
                            j = half * STEPS + step
                            dve.wait_ge(loaded[s], i * (16 * STEPS) + 16 * (j // 2 + 1))
                            dve.wait_ge(used, g * FG + 2)
                            nc.vector.tensor_copy(w_hi[:, s], ring[:, s]).then_inc(w_high, 1)
                            dve.wait_ge(w_high, g + 1)
                            nc.vector.tensor_tensor(w_lo[:, s], ring[:, s], w_hi[:, s].bitcast(F32), ALU.subtract).then_inc(w_split, 1)
                            for q in range(FG):
                                dve.wait_ge(h_high, g * FG + (q + 1))
                                nc.vector.tensor_tensor(h_lo[:, q, :], hT[:, FG * step + q, :], h_hi[:, q, :].bitcast(F32), ALU.subtract).then_inc(h_split, 1)
                            if step == STEPS - 1:
                                dve.wait_ge(used, g * FG + 3 * FG)
                                for b in range(3):
                                    last = nc.vector.tensor_copy(yT[:, bass.ds(i * 4 + half * 2 + 1, 1), b * NB:(b + 1) * NB].rearrange("p o n -> p (o n)"),
                                                                 psum[:, 3 + b, 0:NB])
                                last.then_inc(y_copied[1], 1)
                    dve.wait_ge(y_copied[1], 5)



OUTS = [(1, 1024, 1024), (8, 4, 1024), (1, 1, 1024, 4, 2, 64), (1, 1, 1024, 2, 8, 64), (1, 1, 1024, 8), (1, 1, 512, 2, 2, 64),
        (1, 8, 4, 4, 2, 64), (1, 8, 4, 2, 8, 64), (1, 8, 4, 8), (1, 8, 512, 2, 2, 64)]
INS = ["x_prompt", "x_sample", "cache_nsa_kv", "cache_fox_kv", "cache_fox_logf", "state_win_kv", "page_table", "rel_bias",
       "norm_mix_pre", "norm_mix_post", "norm_ffn_pre", "norm_ffn_post", "w_in", "b_gate", "b_forget", "cmp_pe", "cmp_w1",
       "cmp_w2", "grp_norm_nsa", "grp_norm_fox", "w_o", "w_ffn_gate", "w_ffn_up", "w_ffn_down"]


def kernel(**inputs):
    import concourse.bacc as bacc
    from concourse.bass_utils import run_bass_kernel_spmd

    nc = bacc.Bacc("TRN2", target_bir_lowering=False, num_devices=1)
    arrays, a, c = {}, {}, {}
    for name in INS:
        x = np.ascontiguousarray(inputs[name])
        arrays["in_" + name] = x
        a[name] = nc.dram_tensor("in_" + name, x.shape, mybir.dt.from_np(x.dtype), kind="ExternalInput").ap()
    for name, x in constants().items():
        arrays["const_" + name] = x
        c[name] = nc.dram_tensor("const_" + name, x.shape, mybir.dt.from_np(x.dtype), kind="ExternalInput").ap()
    o = [nc.dram_tensor(f"out_{i}", s, F32, kind="ExternalOutput").ap() for i, s in enumerate(OUTS)]
    program(nc, a, o, c)
    r = run_bass_kernel_spmd(nc, [arrays], core_ids=[0])
    return tuple(r.results[0][f"out_{i}"] for i in range(len(OUTS)))


def constants():
    f = np.float32
    dist = 255 - np.arange(384)
    n = np.maximum(dist, 1).astype(f)
    large = 16 + (np.log(n / f(16)) / f(np.log(128 / 16)) * f(16)).astype(np.int32)
    bucket = np.where(dist < 16, np.maximum(dist, 0), np.minimum(large, 31))
    onehot = np.zeros((33, 384), f)
    onehot[bucket, np.arange(384)] = 1
    onehot[31] -= 1
    onehot[:32, dist < 0] = 0
    onehot[32] = dist < 0
    q, k = np.arange(P)[:, None], np.arange(P)[None]
    row = np.arange(H * TS)
    t, new = row[:, None] % TS, np.arange(TS)[None]
    head = row // TS
    blk = np.arange(NC)[:, None] * CS
    slc = np.arange(16)[None] * 64
    return {
        "ident": np.eye(P, dtype=f),
        "onehot": onehot,
        "causal": np.where(k > q, f(NEG), f(0)).astype(f),
        "band": np.where(k <= q, f(NEG), f(0)).astype(f),
        "mask_new": np.concatenate([np.where(new > t, f(NEG), f(0)), np.where(new <= t, f(NEG), f(0))], 1).astype(f),
        "overlap": ((blk < slc + 64) & (blk + CB > slc)).astype(f),
        "group_sum": ((head[:, None] // R == head[None] // R) & (row[:, None] % TS == row[None] % TS)).astype(f),
        "neg_pick": -(np.arange(H)[:, None] == head[None]).astype(f),
        "iota": np.tile(np.arange(16, dtype=f), (32, 1)),
    }
```
